# Optimizing a Trainium2 kernel written in Bass

```python
import math
import jax, jax.numpy as jnp
from jax import lax
import numpy as np

D_MODEL = 1024
BATCH = 1
SEQ = 1024
DEPTH = 1

MLA_HEADS = 8
QK_NOPE = 64
QK_ROPE = 32
V_HEAD = 64
Q_LORA = 256
KV_LORA = 128
ROPE_THETA = 10000.0
Q_BLOCK = 128
MLA_WIDTH = MLA_HEADS * V_HEAD
RWKV_HEADS = 8
RWKV_HEAD = 64
RWKV_WIDTH = RWKV_HEADS * RWKV_HEAD
DECAY_LORA = 64
A_LORA = 64
GATE_LORA = 128
GN_EPS = 64e-5
N_BRANCHES = 2
MIX_WIDTH = MLA_WIDTH + RWKV_WIDTH
FFN_HIDDEN = 2816
CONV_WIDTH = 3
NORM_EPS = 1e-6
MLA_COLS = Q_LORA + KV_LORA + QK_ROPE
RWKV_COLS = 3 * RWKV_WIDTH + A_LORA + 2 * DECAY_LORA + 2 * GATE_LORA
GATE_COLS = N_BRANCHES * D_MODEL
IN_COLS = MLA_COLS + RWKV_COLS + GATE_COLS


def _split(t, sizes):
    out, start = [], 0
    for s in sizes:
        out.append(t[..., start:start + s])
        start += s
    return out

def rms_norm(t, g, eps=NORM_EPS):
    tf = t.astype(jnp.float32)
    y = tf * lax.rsqrt(jnp.mean(tf * tf, axis=-1, keepdims=True) + eps)
    return (y * g.astype(jnp.float32)).astype(t.dtype)

def rope(t, cos, sin):
    half = t.shape[-1] // 2
    t1, t2 = t[..., :half], t[..., half:]
    return jnp.concatenate([t1 * cos - t2 * sin, t2 * cos + t1 * sin], axis=-1)

def centered_shift(u, mu_prev, mu_next):
    zero = jnp.zeros_like(u[:, :1])
    prev = jnp.concatenate([zero, u[:, :-1]], axis=1)
    nxt = jnp.concatenate([u[:, 1:], zero], axis=1)
    return u + mu_prev * (prev - u) + mu_next * (nxt - u)

def dwconv_centered(u, w, b):
    up = jnp.pad(u, ((0, 0), (1, 1), (0, 0)))
    return up[:, :-2] * w[0] + up[:, 1:-1] * w[1] + up[:, 2:] * w[2] + b

def blocked_mla_attention(q_nope, q_rope, k_nope, k_rope, v):
    B, S, H, _ = q_nope.shape
    nb = S // Q_BLOCK
    scale = 1.0 / math.sqrt(QK_NOPE + QK_ROPE)
    qn = jnp.moveaxis(q_nope.reshape(B, nb, Q_BLOCK, H, QK_NOPE), 1, 0)
    qr = jnp.moveaxis(q_rope.reshape(B, nb, Q_BLOCK, H, QK_ROPE), 1, 0)

    def one_block(args):
        qn_b, qr_b = args
        s = (jnp.einsum('bqhd,bkhd->bhqk', qn_b, k_nope)
             + jnp.einsum('bqhd,bkd->bhqk', qr_b, k_rope))
        p = jax.nn.softmax(s.astype(jnp.float32) * scale, axis=-1)
        return jnp.einsum('bhqk,bkhd->bqhd', p.astype(v.dtype), v)

    o = lax.map(one_block, (qn, qr))
    return jnp.moveaxis(o, 0, 1).reshape(B, S, H * V_HEAD)

def mla_branch(cols, cos, sin, q_a_norm_g, kv_a_norm_g, w_uq, w_ukv, qn_g, qr_g, kn_g, kr_g):
    B, S, _ = cols.shape
    c_q, c_kv, k_rope = _split(cols, [Q_LORA, KV_LORA, QK_ROPE])
    c_q = rms_norm(c_q, q_a_norm_g)
    c_kv = rms_norm(c_kv, kv_a_norm_g)
    q = (c_q @ w_uq).reshape(B, S, MLA_HEADS, QK_NOPE + QK_ROPE)
    kv = (c_kv @ w_ukv).reshape(B, S, MLA_HEADS, QK_NOPE + V_HEAD)
    q_nope, q_rope = q[..., :QK_NOPE], q[..., QK_NOPE:]
    k_nope, v = kv[..., :QK_NOPE], kv[..., QK_NOPE:]
    q_nope = rms_norm(q_nope, qn_g)
    k_nope = rms_norm(k_nope, kn_g)
    q_rope = rope(rms_norm(q_rope, qr_g), cos[:, :, None, :], sin[:, :, None, :])
    k_rope = rope(rms_norm(k_rope, kr_g), cos, sin)
    return blocked_mla_attention(q_nope, q_rope, k_nope, k_rope, v)

def wkv7_scan(r, w, k, v, a, b, reverse):
    B, S, H, N = r.shape
    xs = tuple(jnp.moveaxis(t.astype(jnp.float32), 1, 0) for t in (r, w, k, v, a, b))

    def step(state, inp):
        r_t, w_t, k_t, v_t, a_t, b_t = inp
        sa = jnp.einsum('bhvk,bhk->bhv', state, a_t)
        state = (state * w_t[:, :, None, :] + sa[..., None] * b_t[:, :, None, :]
                 + v_t[..., None] * k_t[:, :, None, :])
        return state, jnp.einsum('bhvk,bhk->bhv', state, r_t)

    s0 = jnp.zeros((B, H, N, N), jnp.float32)
    _, out = lax.scan(step, s0, xs, reverse=reverse)
    return jnp.moveaxis(out, 0, 1)

def head_group_norm(o, g, b):
    mu = jnp.mean(o, axis=-1, keepdims=True)
    var = jnp.mean(jnp.square(o - mu), axis=-1, keepdims=True)
    y = (o - mu) * lax.rsqrt(var + GN_EPS)
    return (y * g.astype(jnp.float32).reshape(RWKV_HEADS, RWKV_HEAD)
            + b.astype(jnp.float32).reshape(RWKV_HEADS, RWKV_HEAD))

def rwkv7_branch(cols, shift_mu, w0, w2, a0, a2, g2, k_k, k_a, r_k, ln_g, ln_b):
    B, S, _ = cols.shape
    u = centered_shift(cols, shift_mu[0], shift_mu[1])
    r, k, v, a_lo, dlo_f, dlo_b, glo_f, glo_b = _split(
        u, [RWKV_WIDTH, RWKV_WIDTH, RWKV_WIDTH, A_LORA, DECAY_LORA, DECAY_LORA, GATE_LORA, GATE_LORA])
    heads = lambda t: t.reshape(B, S, RWKV_HEADS, RWKV_HEAD)
    a = jax.nn.sigmoid(a0 + a_lo @ a2)
    kkf = heads(k * k_k).astype(jnp.float32)
    kk = kkf / jnp.maximum(jnp.sqrt(jnp.sum(kkf * kkf, axis=-1, keepdims=True)), 1e-12)
    k = k * (1.0 + (a - 1.0) * k_a)
    rh, kh, vh, ah = heads(r), heads(k), heads(v), heads(a)
    bonus = (jnp.sum(rh * kh * r_k, axis=-1, keepdims=True) * vh).astype(jnp.float32)
    b_vec = kk * ah.astype(jnp.float32)

    def direction(dlo, glo, w0_d, w2_d, g2_d, reverse):
        w = -jax.nn.softplus(-(w0_d + jnp.tanh(dlo) @ w2_d)) - 0.5
        decay = jnp.exp(-jnp.exp(w.astype(jnp.float32)))
        o = wkv7_scan(rh, heads(decay), kh, vh, -kk, b_vec, reverse)
        o = (head_group_norm(o, ln_g, ln_b) + bonus).reshape(B, S, RWKV_WIDTH)
        g = jax.nn.sigmoid(glo) @ g2_d
        return o.astype(cols.dtype) * g

    fwd = direction(dlo_f, glo_f, w0[0], w2[0], g2[0], False)
    bwd = direction(dlo_b, glo_b, w0[1], w2[1], g2[1], True)
    return fwd + bwd

def first_inputs(seed: int = 0) -> dict:
    key = jax.random.key(seed)
    ks = iter(jax.random.split(key, 40))
    nrm = lambda shape, s: jax.random.normal(next(ks), shape, jnp.float32) * s
    gain = lambda shape: 1.0 + nrm(shape, 0.05)
    L, D = DEPTH, D_MODEL
    x = jax.random.normal(next(ks), (BATCH, SEQ, D), jnp.float32)
    offs = jax.random.randint(next(ks), (BATCH, 1), 0, 2048, dtype=jnp.int32)
    positions = offs + jnp.arange(SEQ, dtype=jnp.int32)[None, :]
    return {
        "x": x,
        "positions": positions,
        "norm_mix_g": gain((L, D)),
        "w_in": nrm((L, D, IN_COLS), D ** -0.5),
        "b_gate": nrm((L, N_BRANCHES, D), 0.1),
        "q_a_norm_g": gain((L, Q_LORA)),
        "kv_a_norm_g": gain((L, KV_LORA)),
        "w_uq": nrm((L, Q_LORA, MLA_HEADS * (QK_NOPE + QK_ROPE)), Q_LORA ** -0.5),
        "w_ukv": nrm((L, KV_LORA, MLA_HEADS * (QK_NOPE + V_HEAD)), KV_LORA ** -0.5),
        "qn_norm_g": gain((L, QK_NOPE)),
        "qr_norm_g": gain((L, QK_ROPE)),
        "kn_norm_g": gain((L, QK_NOPE)),
        "kr_norm_g": gain((L, QK_ROPE)),
        "shift_mu": jax.random.uniform(next(ks), (L, 2, RWKV_COLS), jnp.float32, 0.0, 0.5),
        "w0": jax.random.uniform(next(ks), (L, 2, RWKV_WIDTH), jnp.float32, -6.0, -1.0),
        "w2": nrm((L, 2, DECAY_LORA, RWKV_WIDTH), 0.1 * DECAY_LORA ** -0.5),
        "a0": nrm((L, RWKV_WIDTH), 0.1),
        "a2": nrm((L, A_LORA, RWKV_WIDTH), 0.5 * A_LORA ** -0.5),
        "g2": nrm((L, 2, GATE_LORA, RWKV_WIDTH), GATE_LORA ** -0.5),
        "k_k": 0.85 + nrm((L, RWKV_WIDTH), 0.05),
        "k_a": gain((L, RWKV_WIDTH)),
        "r_k": nrm((L, RWKV_HEADS, RWKV_HEAD), 0.1),
        "ln_x_g": gain((L, RWKV_WIDTH)),
        "ln_x_b": nrm((L, RWKV_WIDTH), 0.02),
        "w_o": nrm((L, MIX_WIDTH, D), MLA_WIDTH ** -0.5),
        "w_merge": nrm((L, D, D), D ** -0.5),
        "norm_ffn_g": gain((L, D)),
        "w_ffn_gate": nrm((L, D, FFN_HIDDEN), D ** -0.5),
        "w_ffn_up": nrm((L, D, FFN_HIDDEN), D ** -0.5),
        "ffn_conv_w": nrm((L, CONV_WIDTH, FFN_HIDDEN), CONV_WIDTH ** -0.5),
        "ffn_conv_b": nrm((L, FFN_HIDDEN), 0.02),
        "w_ffn_down": nrm((L, FFN_HIDDEN, D), FFN_HIDDEN ** -0.5),
    }

def first_block(x, positions, norm_mix_g, w_in, b_gate, q_a_norm_g, kv_a_norm_g, w_uq, w_ukv,
              qn_norm_g, qr_norm_g, kn_norm_g, kr_norm_g, shift_mu, w0, w2, a0, a2, g2,
              k_k, k_a, r_k, ln_x_g, ln_x_b, w_o, w_merge, norm_ffn_g, w_ffn_gate, w_ffn_up,
              ffn_conv_w, ffn_conv_b, w_ffn_down):
    B, S, D = x.shape
    inv_freq = ROPE_THETA ** (-jnp.arange(0, QK_ROPE, 2, dtype=jnp.float32) / QK_ROPE)
    ang = positions.astype(jnp.float32)[..., None] * inv_freq
    cos, sin = jnp.cos(ang).astype(x.dtype), jnp.sin(ang).astype(x.dtype)

    for l in range(DEPTH):
        h = rms_norm(x, norm_mix_g[l])
        proj = h @ w_in[l]
        mla_cols, rw_cols, gate_cols = _split(proj, [MLA_COLS, RWKV_COLS, GATE_COLS])
        o_a = mla_branch(mla_cols, cos, sin, q_a_norm_g[l], kv_a_norm_g[l], w_uq[l], w_ukv[l],
                         qn_norm_g[l], qr_norm_g[l], kn_norm_g[l], kr_norm_g[l])
        o_b = rwkv7_branch(rw_cols, shift_mu[l], w0[l], w2[l], a0[l], a2[l], g2[l],
                           k_k[l], k_a[l], r_k[l], ln_x_g[l], ln_x_b[l])
        w_o_l = w_o[l]
        y_a = o_a @ w_o_l[:MLA_WIDTH]
        y_b = o_b @ w_o_l[MLA_WIDTH:]
        gates = jax.nn.sigmoid(gate_cols.reshape(B, S, N_BRANCHES, D) + b_gate[l])
        x = x + (gates[:, :, 0] * y_a + gates[:, :, 1] * y_b) @ w_merge[l]
        h = rms_norm(x, norm_ffn_g[l])
        gp = dwconv_centered(h @ w_ffn_gate[l], ffn_conv_w[l], ffn_conv_b[l])
        x = x + (jax.nn.silu(gp) * (h @ w_ffn_up[l])) @ w_ffn_down[l]
    return x


GLA_HEADS = 4
GLA_DK = 64
GLA_DV = 128
GLA_QK_WIDTH = GLA_HEADS * GLA_DK
GLA_WIDTH = GLA_HEADS * GLA_DV
GATE_RANK = 16
GATE_NORMALIZER = 16.0
CHUNK = 64
CONV_WIDTH_2 = D_MODEL // 2
CONV_GROUPS = 8
CONV_K = 3
MIX_WIDTH_2 = GLA_WIDTH + CONV_WIDTH_2
D_FF = int(math.ceil(8 * D_MODEL / 3 / 256) * 256)

COL_Q = GLA_QK_WIDTH
COL_K = GLA_QK_WIDTH
COL_V = GLA_WIDTH
COL_G = GLA_WIDTH
COL_A = GATE_RANK
COL_CB = CONV_WIDTH_2
COL_CC = CONV_WIDTH_2
COL_CH = CONV_WIDTH_2
IN_COLS_2 = COL_Q + COL_K + COL_V + COL_G + COL_A + COL_CB + COL_CC + COL_CH


def rmsnorm(x, g):
    xf = x.astype(jnp.float32)
    y = xf * lax.rsqrt(jnp.mean(xf * xf, axis=-1, keepdims=True) + NORM_EPS)
    return (y * g.astype(jnp.float32)).astype(x.dtype)

def gla_chunked(q, k, v, log_a):
    bsz, seq, heads, dk = q.shape
    dv = v.shape[-1]
    n_chunks = seq // CHUNK

    def to_chunks(t):
        return t.astype(jnp.float32).reshape(bsz, n_chunks, CHUNK, heads, t.shape[-1]).transpose(1, 0, 3, 2, 4)

    q, k, v, log_a = to_chunks(q), to_chunks(k), to_chunks(v), to_chunks(log_a)
    b = jnp.cumsum(log_a, axis=-2)
    b_last = b[..., -1:, :]
    q_i = q * jnp.exp(b)
    k_i = k * jnp.exp(-b)
    k_s = k * jnp.exp(b_last - b)

    causal = jnp.tril(jnp.ones((CHUNK, CHUNK), dtype=bool))
    scores = jnp.einsum('nbhck,nbhsk->nbhcs', q_i, k_i)
    scores = jnp.where(causal, scores, 0.0)
    o_intra = jnp.einsum('nbhcs,nbhsv->nbhcv', scores, v)

    chunk_kv = jnp.einsum('nbhsk,nbhsv->nbhkv', k_s, v)
    chunk_decay = jnp.exp(b_last[..., 0, :])

    def step(state, inp):
        dec, kv_c = inp
        return dec[..., None] * state + kv_c, state

    state0 = jnp.zeros((bsz, heads, dk, dv), jnp.float32)
    _, state_prev = lax.scan(step, state0, (chunk_decay, chunk_kv))
    o_inter = jnp.einsum('nbhck,nbhkv->nbhcv', q_i, state_prev)

    o = o_intra + o_inter
    return o.transpose(1, 0, 3, 2, 4).reshape(bsz, seq, heads, dv)

def causal_depthwise_conv(u, w):
    seq = u.shape[1]
    u_pad = jnp.pad(u, ((0, 0), (CONV_K - 1, 0), (0, 0)))
    y = w[0] * u_pad[:, 0:seq]
    for j in range(1, CONV_K):
        y = y + w[j] * u_pad[:, j:j + seq]
    return y

def second_inputs(seed: int = 0) -> dict:
    key = jax.random.key(seed)
    ks = jax.random.split(key, 16)
    f32 = jnp.float32
    n = lambda k, shape, scale: (jax.random.normal(k, shape, f32) * scale)
    return {
        "x": n(ks[0], (BATCH, SEQ, D_MODEL), 1.0),
        "norm1_g": 1.0 + n(ks[1], (DEPTH, D_MODEL), 0.02),
        "w_in": n(ks[2], (DEPTH, D_MODEL, IN_COLS_2), D_MODEL ** -0.5),
        "w_gate_up": n(ks[3], (DEPTH, GATE_RANK, GLA_QK_WIDTH), GATE_RANK ** -0.5),
        "b_gate": n(ks[4], (DEPTH, GLA_QK_WIDTH), 0.01),
        "gla_norm_g": 1.0 + n(ks[5], (DEPTH, GLA_DV), 0.02),
        "conv_w": n(ks[6], (DEPTH, CONV_K, CONV_WIDTH_2), CONV_K ** -0.5),
        "w_out": n(ks[7], (DEPTH, MIX_WIDTH_2, D_MODEL), MIX_WIDTH_2 ** -0.5),
        "norm2_g": 1.0 + n(ks[8], (DEPTH, D_MODEL), 0.02),
        "w_ffn_gate": n(ks[9], (DEPTH, D_MODEL, D_FF), D_MODEL ** -0.5),
        "w_ffn_up": n(ks[10], (DEPTH, D_MODEL, D_FF), D_MODEL ** -0.5),
        "w_ffn_down": n(ks[11], (DEPTH, D_FF, D_MODEL), D_FF ** -0.5),
        "norm_f_g": 1.0 + n(ks[12], (D_MODEL,), 0.02),
    }

def second_block(x, norm1_g, w_in, w_gate_up, b_gate, gla_norm_g, conv_w, w_out,
              norm2_g, w_ffn_gate, w_ffn_up, w_ffn_down, norm_f_g):
    bsz, seq, _ = x.shape
    splits = np.cumsum([COL_Q, COL_K, COL_V, COL_G, COL_A, COL_CB, COL_CC])
    for l in range(DEPTH):
        h = rmsnorm(x, norm1_g[l])
        proj = h @ w_in[l]
        p_q, p_k, p_v, p_g, p_a, c_b, c_c, c_h = jnp.split(proj, splits, axis=-1)

        q = p_q.reshape(bsz, seq, GLA_HEADS, GLA_DK) * (GLA_DK ** -0.5)
        k = p_k.reshape(bsz, seq, GLA_HEADS, GLA_DK)
        v = p_v.reshape(bsz, seq, GLA_HEADS, GLA_DV)
        gate_logits = (p_a @ w_gate_up[l] + b_gate[l]).astype(jnp.float32)
        log_a = (jax.nn.log_sigmoid(gate_logits) / GATE_NORMALIZER).reshape(bsz, seq, GLA_HEADS, GLA_DK)
        o = gla_chunked(q, k, v, log_a)
        o = rmsnorm(o, gla_norm_g[l]).astype(x.dtype)
        o = o * jax.nn.silu(p_g.reshape(bsz, seq, GLA_HEADS, GLA_DV))
        o_gla = o.reshape(bsz, seq, GLA_WIDTH)

        u = c_c * c_h
        o_conv = c_b * causal_depthwise_conv(u, conv_w[l])

        mixed = jnp.concatenate([o_gla, o_conv], axis=-1) @ w_out[l]
        x = x + mixed

        h2 = rmsnorm(x, norm2_g[l])
        ffn = (jax.nn.silu(h2 @ w_ffn_gate[l]) * (h2 @ w_ffn_up[l])) @ w_ffn_down[l]
        x = x + ffn
    return rmsnorm(x, norm_f_g)


def setup_inputs(seed=0):
    out = dict(first_inputs(seed))
    for name, value in second_inputs(seed + 1).items():
        if name != "x":
            out[name + "_2"] = value
    return out


def reference(
    x, positions, norm_mix_g, w_in, b_gate, q_a_norm_g, kv_a_norm_g, w_uq, w_ukv, qn_norm_g,
    qr_norm_g, kn_norm_g, kr_norm_g, shift_mu, w0, w2, a0, a2, g2, k_k, k_a, r_k, ln_x_g,
    ln_x_b, w_o, w_merge, norm_ffn_g, w_ffn_gate, w_ffn_up, ffn_conv_w, ffn_conv_b, w_ffn_down,
    norm1_g_2, w_in_2, w_gate_up_2, b_gate_2, gla_norm_g_2, conv_w_2, w_out_2, norm2_g_2,
    w_ffn_gate_2, w_ffn_up_2, w_ffn_down_2, norm_f_g_2,
):
    x = first_block(
        x, positions, norm_mix_g, w_in, b_gate, q_a_norm_g, kv_a_norm_g, w_uq, w_ukv, qn_norm_g,
        qr_norm_g, kn_norm_g, kr_norm_g, shift_mu, w0, w2, a0, a2, g2, k_k, k_a, r_k, ln_x_g,
        ln_x_b, w_o, w_merge, norm_ffn_g, w_ffn_gate, w_ffn_up, ffn_conv_w, ffn_conv_b,
        w_ffn_down,
    )
    return second_block(
        x, norm1_g_2, w_in_2, w_gate_up_2, b_gate_2, gla_norm_g_2, conv_w_2, w_out_2, norm2_g_2,
        w_ffn_gate_2, w_ffn_up_2, w_ffn_down_2, norm_f_g_2,
    )


_drawn_inputs = setup_inputs


def setup_inputs(seed=0):
    import zlib

    import numpy as np

    out = dict(_drawn_inputs(seed))
    spreads = {}
    factors = {'q_a_norm_g': 8.0,
     'kv_a_norm_g': 8.0,
     'qn_norm_g': 8.0,
     'qr_norm_g': 8.0,
     'kn_norm_g': 8.0,
     'kr_norm_g': 8.0,
     'w2': 57.617,
     'ln_x_b': 14.53,
     'ffn_conv_b': 4.086,
     'b_gate_2': 8.0,
     'gla_norm_g_2': 24.45,
     'norm2_g_2': 5.06,
     'norm_f_g_2': 8.028,
     'a0': 6.959,
     'k_k': 5.621,
     'k_a': 5.123,
     'ln_x_g': 5.934,
     'norm_ffn_g': 2.739}
    for name, (base, spread) in spreads.items():
        noise = np.random.default_rng([zlib.crc32(name.encode()), seed]).standard_normal(out[name].shape)
        drawn = base * np.exp(spread * noise) if base else spread * noise
        out[name] = __import__('jax').numpy.asarray(drawn.astype(out[name].dtype))
    for name, factor in factors.items():
        out[name] = (out[name] * factor).astype(out[name].dtype)
    return out
```

```python
from contextlib import ExitStack
import math

import numpy as np

import concourse.bass as bass
from concourse import mybir

F32 = mybir.dt.float32
I32 = mybir.dt.int32
ACT = mybir.ActivationFunctionType
ALU = mybir.AluOpType
AX = mybir.AxisListType

P = 128
S = 1024
D = 1024
NT = S // P
FF = 2816
NF = FF // P
EPS = 1e-6
GN_EPS = 64e-5
EH = math.exp(-0.5)
SCALE = 1.0 / math.sqrt(96.0)

CONST = ["ident", "SU", "SL", "IU", "IL", "DU", "DL", "OU", "OL", "BD", "TCF", "TCB", "TRI", "REST"]
COLS = [("col", 2), ("invf", 16)]
PCOLS = [("g_mix", 8), ("g_qa", 2), ("g_kva", 1), ("mup", 16), ("mun", 16), ("bg", 16), ("g_ffn", 8),
         ("cw0", NF), ("cw1", NF), ("cw2", NF), ("cb", NF), ("g_n1", 8), ("g_n2", 8),
         ("gw0", 4), ("gw1", 4), ("gw2", 4)]


def const_table():
    i = np.arange(P)
    p, f = i[:, None], i[None, :]
    blk = (p // 16) == (f // 16)
    half = (p // 64) == (f // 64)
    mid_f = (p <= 63).astype(np.float32)
    mid_b = (p >= 64).astype(np.float32)
    m = {
        "ident": p == f, "SU": p < f, "SL": p > f, "IU": p <= f, "IL": p >= f,
        "DU": (p < f) & blk, "DL": (p > f) & blk, "OU": (p < f) & ~blk, "OL": (p > f) & ~blk,
        "BD": half,
        "TCF": (p <= f).astype(np.float32) - mid_f, "TCB": (p >= f).astype(np.float32) - mid_b,
        "TRI": (p <= f) & half, "REST": (p > f) & half,
    }
    parts = [np.broadcast_to(m[n], (P, P)).astype(np.float32) for n in CONST]
    parts.append(np.stack([(i <= 63), (i > 63)], 1).astype(np.float32))
    inv = 10000.0 ** (-np.arange(0, 32, 2, dtype=np.float64) / 32)
    parts.append(np.broadcast_to(inv.astype(np.float32), (P, 16)))
    return np.ascontiguousarray(np.concatenate(parts, 1))


class Eng:

    def __init__(self, sem):
        self.sem, self.n, self.q, self.seen = sem, 0, [], {}

    def wait(self, *toks):
        for t in toks:
            if t is None:
                continue
            if isinstance(t, list):
                self.wait(*t)
            elif self.seen.get(id(t[0]), 0) < t[1]:
                self.seen[id(t[0])] = t[1]
                self.q.append(lambda e, t=t: e.wait_ge(t[0], t[1]))

    def do(self, fn, *toks):
        self.wait(*toks)
        self.n += 1
        self.q.append(lambda e: fn(e).then_inc(self.sem, 1))
        return (self.sem, self.n)

    def quiet(self, fn, *toks):
        self.wait(*toks)
        self.q.append(lambda e: fn(e))

    def run(self, e):
        for f in self.q:
            f(e)


class Slot:

    def __init__(self, sem, ap=None):
        self.sem, self.n, self.ap, self.free = sem, 0, ap, None

    def dma(self, eng, out, in_, *toks):
        eng.wait(*toks)
        self.n += 16
        eng.q.append(lambda e: e.dma_start(out, in_).then_inc(self.sem, 16))
        return (self.sem, self.n)


def interleave(*gens):
    gens = list(gens)
    while gens:
        for g in list(gens):
            try:
                next(g)
            except StopIteration:
                gens.remove(g)


class K:
    pass


def program(nc, a, out):
    ctx = ExitStack()
    with ctx:
        nsem = [0]

        def sem(name):
            return ctx.enter_context(nc.semaphore(name))

        def sb(name, n):
            return ctx.enter_context(nc.sbuf_tensor(name, [P, n], F32))

        PE, VE, AE, GE, SP = [Eng(sem(f"s_{n}")) for n in ("pe", "ve", "ae", "ge", "sp")]

        def slot(ap=None):
            nsem[0] += 1
            return Slot(sem(f"d{nsem[0]}"), ap)

        X = sb("X", 8192)
        W = sb("W", 4096)
        W1 = sb("W1", 2052)
        NCST = len(CONST) * P + 18
        CS = sb("CS", NCST)
        NPC = sum(n for _, n in PCOLS)
        PC = sb("PC", NPC)
        SM = sb("SM", 1024)

        def region(st, name, n, dt=F32):
            return st.enter_context(nc.sbuf_tensor(name, [P, n], dt))

        room = ExitStack()
        HT = region(room, "HT_1", 8192)
        AR = region(room, "AR_1", 22528)
        EX = region(room, "EX_1", 4096)
        ps = ctx.enter_context(nc.psum_tensor("ps", [P, 8, 512], F32))

        cst = {n: CS[:, i * P:(i + 1) * P] for i, n in enumerate(CONST)}
        cst["col"] = CS[:, len(CONST) * P:len(CONST) * P + 2]
        cst["invf"] = CS[:, len(CONST) * P + 2:len(CONST) * P + 18]
        pc = {}
        at = 0
        for n, w in PCOLS:
            pc[n] = PC[:, at:at + w]
            at += w

        def v3(ap, k):
            return ap.rearrange("p (a b) -> p a b", a=k)

        def bc(ap, k):
            return ap.unsqueeze(1).broadcast_to([P, k, ap.shape[1]])

        def bl(ap, k):
            return ap.unsqueeze(2).broadcast_to([P, ap.shape[1], k])

        sc = slot()
        t_cst = sc.dma(SP, CS[:, :], a["cst"])
        t_cst = sc.dma(SP, PC[:, :], a["pcols"])
        ident = cst["ident"]

        bank_free = [None] * 8
        bank_at = [0]

        def acquire(n=1):
            if n == 2 and bank_at[0] % 2:
                bank_at[0] += 1
            b = bank_at[0] % 8
            bank_at[0] += n
            toks = [bank_free[b + i] for i in range(n)]
            return b, toks

        def release(b, tok, n=1):
            for i in range(n):
                bank_free[b + i] = tok

        ring = [slot(W[:, i * 1024:(i + 1) * 1024]) for i in range(4)]
        ring_at = [0]

        def load_w(src, n=1024):
            r = ring[ring_at[0] % 4]
            ring_at[0] += 1
            t = r.dma(SP, r.ap[:, 0:n], src, r.free)
            r.free = None
            return r, t

        def mm(o, l, r, start, stop, *toks, mark=False, lax=False):
            f = lambda e: e.matmul(o, l, r, start=start, stop=stop, **({"skip_group_check": True} if lax else {}))
            if mark:
                return PE.do(f, *toks)
            PE.quiet(f, *toks)

        def tr(o, i, *toks, mark=False):
            f = lambda e: e.transpose(o, i, ident)
            if mark:
                return PE.do(f, *toks)
            PE.quiet(f, *toks)

        def act(o, i, f, *toks, **kw):
            return AE.do(lambda e: e.activation(o, i, f, **kw), *toks)

        def tt(o, x, y, op, *toks, eng=None):
            return (eng or VE).do(lambda e: e.tensor_tensor(o, x, y, op), *toks)

        def ts(o, x, s1, s2, o1, o2, *toks, eng=None):
            if s2 is None:
                return (eng or VE).do(lambda e: e.tensor_scalar(o, x, s1, None, o1), *toks)
            return (eng or VE).do(lambda e: e.tensor_scalar(o, x, s1, s2, o1, o2), *toks)

        def stt(o, x, s, y, o1, o2, *toks):
            return VE.do(lambda e: e.scalar_tensor_tensor(out=o, in0=x, scalar=s, in1=y, op0=o1, op1=o2), *toks)

        def red(o, x, *toks, op=ALU.add):
            return VE.do(lambda e: e.tensor_reduce(o, x, AX.X, op), *toks)

        def recip(o, x, *toks):
            return VE.do(lambda e: e.reciprocal(o, x), *toks)

        def cp(eng, o, x, *toks):
            if eng is AE:
                return act(o, x, ACT.Copy, *toks)
            return eng.do(lambda e: e.tensor_copy(o, x), *toks)

        def memset(eng, o, v, *toks):
            return eng.do(lambda e: e.memset(o, v), *toks)

        def last(eng):
            return (eng.sem, eng.n) if eng.n else None

        def all_done():
            return [last(e) for e in (PE, VE, AE, GE)]

        def sm(at, n):
            return SM[:, at:at + n]

        def rstd(o, n, eps, *toks):
            t = ts(o, o, 1.0 / n, eps, ALU.mult, ALU.add, *toks)
            t = act(o, o, ACT.Sqrt, t)
            return recip(o, o, t)

        def norm_tile(t, gain, xs, ss, tok, xs_free, HT, lo):
            xt = X[:, t * D:(t + 1) * D]
            tq = act(xs, xt, ACT.Square, tok, xs_free, accum_out=ss)
            tq = rstd(ss, D, EPS, tq)
            tq = ts(xs, xt, ss, None, ALU.mult, None, tq)
            toks = []
            for h in range(2):
                b, fr = acquire()
                for j in range(4):
                    k = 4 * h + j
                    tp = tr(ps[:, b, j * P:(j + 1) * P], xs[:, k * P:(k + 1) * P], tq, fr, t_cst, mark=(j == 3))
                o = v3(HT, 8)[:, 4 * h:4 * h + 4, t * P:(t + 1) * P]
                gb = bl(gain[:, 4 * h:4 * h + 4], P)
                if lo is None:
                    te = tt(o, v3(ps[:, b, :], 4), gb, ALU.mult, tp)
                    release(b, te)
                    continue
                nt = v3(W1[:, 1024:1536], 4)
                te = tt(nt, v3(ps[:, b, :], 4), gb, ALU.mult, tp, nfree[0])
                release(b, te)
                th = act(o, nt, ACT.Copy, te)
                te = tt(v3(lo, 8)[:, 4 * h:4 * h + 4, t * P:(t + 1) * P], nt, o.bitcast(F32), ALU.subtract, th)
                nfree[0] = te
            return te, tp

        nfree = [None]

        def norm_all(gain, tok_of, tmp, free_ht, HT, lo=None):
            VE.wait(free_ht)
            AE.wait(free_ht)
            fr = [None] * len(tmp)
            for t in range(NT):
                s = t % len(tmp)
                te, fr[s] = norm_tile(t, gain, tmp[s], sm(t, 1), tok_of[t], fr[s], HT, lo)
            return te

        HT3 = v3(HT[:, :], 8)

        def feat(src, ncol, tok_h, HT3):
            r, tw = load_w(src)
            w3 = v3(r.ap, 8)
            res = []
            for h in range(2):
                b, fr = acquire()
                for k in range(8):
                    tk = mm(ps[0:ncol, b, :], w3[:, k, 0:ncol], HT3[:, k, h * 512:(h + 1) * 512],
                            k == 0, k == 7, tw, tok_h, fr, mark=(k == 7))
                res.append((b, tk))
            r.free = tk
            return res

        def tokmajor(src_of, A3, nk, ncols, tok_a, evac):
            for nh in range(ncols):
                for tg in range(2):
                    banks = [acquire() for _ in range(4)]
                    marks = [None] * 4
                    for s in range(nk // 2):
                        r, tw = load_w(src_of(nh, s))
                        w3 = v3(r.ap, 2)
                        for kk in range(2):
                            k = 2 * s + kk
                            for j in range(4):
                                t = tg * 4 + j
                                b, fr = banks[j]
                                lastk = k == nk - 1
                                tk = mm(ps[:, b, :], A3[:, k, t * P:(t + 1) * P], w3[:, kk, :], k == 0, lastk,
                                        tw, tok_a, fr, mark=(lastk or (kk == 1 and j == 3)))
                                if lastk:
                                    marks[j] = tk
                        r.free = tk
                    for j in range(4):
                        release(banks[j][0], evac(tg * 4 + j, nh, ps[:, banks[j][0], :], marks[j]))

        xsl = [slot() for _ in range(NT)]
        t_x = [xsl[t].dma(SP, X[:, t * D:(t + 1) * D], a["x"][t * P:(t + 1) * P, :]) for t in range(NT)]

        A = 0
        MC = AR[:, 0:3328]
        CQT = AR[:, 3328:5376]
        CKT = AR[:, 5376:6400]
        WUQ = AR[:, 6400:7936]
        WUKV = AR[:, 7936:8960]
        Q = AR[:, 8960:15104]
        WM = AR[:, 15104:18432]
        tmpn = [AR[:, 18432:19456], AR[:, 19456:20480]]
        s_m = slot()
        t_wm = s_m.dma(SP, v3(WM, 8), a["w_mla"])
        t_wm = s_m.dma(SP, v3(WUQ, 2), a["w_uq"].rearrange("(k p) n -> p k n", p=P))
        t_wm = s_m.dma(SP, WUKV, a["w_ukv"])
        GB = AR[:, 20480:20480 + 192]
        t_wm = s_m.dma(SP, GB[:, 0:64], a["qn_norm_g"].partition_broadcast(P).rearrange("p a n -> p (a n)"))
        t_wm = s_m.dma(SP, GB[:, 64:96], a["qr_norm_g"].partition_broadcast(P).rearrange("p a n -> p (a n)"))
        t_wm = s_m.dma(SP, GB[:, 96:160], a["kn_norm_g"].partition_broadcast(P).rearrange("p a n -> p (a n)"))
        t_wm = s_m.dma(SP, GB[:, 160:192], a["kr_norm_g"].partition_broadcast(P).rearrange("p a n -> p (a n)"))
        POS = AR[:, 20672:20680].bitcast(I32)
        t_wm = s_m.dma(SP, POS, a["pos"])

        AE.wait(t_cst)
        VE.wait(t_cst)
        t_h = norm_all(pc["g_mix"], t_x, tmpn, None, HT[:, :])

        MC3 = v3(MC, 8)
        WM3 = v3(WM, 8)
        for t in range(NT):
            b, fr = acquire()
            for k in range(8):
                tk = mm(ps[:, b, 0:416], HT3[:, k, t * P:(t + 1) * P], WM3[:, k, :], k == 0, k == 7, t_h, t_wm, fr,
                        mark=(k == 7))
            te = cp(AE, MC3[:, t, :], ps[:, b, 0:416], tk)
            release(b, te)
        t_mc = te
        SQ = WM
        SQ3 = v3(SQ, 8)
        tq = tt(SQ, MC, MC, ALU.mult, t_mc, tk)
        ss = v3(sm(16, 24), 3)
        tq1 = red(ss[:, 0, :], SQ3[:, :, 0:256], tq)
        tq2 = red(ss[:, 1, :], SQ3[:, :, 256:384], tq)
        tq3 = red(ss[:, 2, :], SQ3[:, :, 384:416], tq)
        ts(ss[:, 0, :], ss[:, 0, :], 1.0 / 256, EPS, ALU.mult, ALU.add, tq1)
        ts(ss[:, 1, :], ss[:, 1, :], 1.0 / 128, EPS, ALU.mult, ALU.add, tq2)
        tq = ts(ss[:, 2, :], ss[:, 2, :], 1.0 / 32, EPS, ALU.mult, ALU.add, tq3)
        tq = act(sm(16, 24), sm(16, 24), ACT.Sqrt, tq)
        tq = recip(sm(16, 24), sm(16, 24), tq)
        tn = None
        for i, (lo, hi) in enumerate(((0, 256), (256, 384), (384, 416))):
            tn = tt(MC3[:, :, lo:hi], MC3[:, :, lo:hi], bl(ss[:, i, :], hi - lo), ALU.mult, tq)
        CQ3 = v3(CQT, 2)
        for t in range(NT):
            b, fr = acquire()
            for j in range(3):
                tk = tr(ps[:, b, j * P:(j + 1) * P], MC3[:, t, j * P:(j + 1) * P], tn, fr, mark=(j == 2))
            te = tt(CQ3[:, :, t * P:(t + 1) * P], v3(ps[:, b, 0:256], 2), bl(pc["g_qa"], P), ALU.mult, tk)
            te = ts(CKT[:, t * P:(t + 1) * P], ps[:, b, 256:384], pc["g_kva"], None, ALU.mult, None)
            release(b, te)
        t_cT = te

        POSF = sm(40, 8)
        ANG, COS, SIN, TMP = [AR[:, 20700 + 128 * i:20828 + 128 * i] for i in range(4)]
        tr0 = cp(VE, POSF, POS, t_wm)
        tr0 = tt(v3(ANG, 8), bl(POSF, 16), bc(cst["invf"], 8), ALU.mult, tr0)
        MAGIC = 12582912.0
        tr0 = ts(TMP, ANG, 1.0 / (2 * math.pi), MAGIC, ALU.mult, ALU.add, tr0)
        tr0 = ts(TMP, TMP, -MAGIC, None, ALU.add, None, tr0)
        C1 = 6.28125
        C2 = float(np.float32(int((2 * math.pi - C1) * 2 ** 20) / 2 ** 20))
        C3 = 2 * math.pi - C1 - C2
        for c in (C1, C2, C3):
            tr0 = stt(ANG, TMP, -c, ANG, ALU.mult, ALU.add, tr0)
        LIM = 3.1415925
        tr0 = ts(ANG, ANG, LIM, -LIM, ALU.min, ALU.max, tr0)
        tr1 = stt(TMP, ANG, -1.0, ANG, ALU.mult, ALU.max, tr0)
        tr1 = ts(TMP, TMP, -1.0, math.pi / 2, ALU.mult, ALU.add, tr1)
        act(SIN, ANG, ACT.Sin, tr0)
        t_rope = act(COS, TMP, ACT.Sin, tr1)

        Q4 = Q.rearrange("p (t h d) -> p t h d", t=8, h=8)
        Q3 = v3(Q, 8)
        KV3 = v3(X[:, :], 8)
        KV4 = X[:, :].rearrange("p (t h d) -> p t h d", t=8, h=8)
        WUQ3 = v3(WUQ, 2)
        for t in range(NT):
            for hh in range(2):
                b, fr = acquire()
                for k in range(2):
                    tk = mm(ps[:, b, 0:384], CQ3[:, k, t * P:(t + 1) * P], WUQ3[:, k, hh * 384:(hh + 1) * 384],
                            k == 0, k == 1, t_cT, fr, mark=(k == 1))
                te = cp(AE, Q3[:, t, hh * 384:(hh + 1) * 384], ps[:, b, 0:384], tk)
                release(b, te)
                b, fr = acquire()
                tk = mm(ps[:, b, :], CKT[:, t * P:(t + 1) * P], WUKV[:, hh * 512:(hh + 1) * 512], True, True, fr,
                        t_cT, mark=True)
                tv = cp(VE, KV3[:, t, hh * 512:(hh + 1) * 512], ps[:, b, :], tk, last(GE))
                release(b, tv)
        t_q, t_kv = te, tv
        SQ = AR[:, 0:4096]
        SQn = SQ.rearrange("p (t h d) -> p t h d", t=8, h=8)
        ssq = [v3(sm(64 + 64 * i, 64), 8) for i in range(3)]
        KR = AR[:, 21300:21556]
        KR3 = v3(KR, 8)
        tkr = tt(KR3, MC3[:, :, 384:416], bc(GB[:, 160:192], 8), ALU.mult, tn, t_wm)
        PE_t = last(PE)
        g3 = lambda ap, o: ap.rearrange("p t h d -> p (t h) d")
        tq = tt(g3(SQn, 0), g3(Q4[:, :, :, 0:64], 0), g3(Q4[:, :, :, 0:64], 0), ALU.mult, t_q, t_kv, tkr, PE_t)
        tq = red(sm(64, 64), g3(SQn, 0), tq)
        SQr = SQ[:, 0:2048].rearrange("p (g d) -> p g d", d=32)
        tq = tt(SQr, g3(Q4[:, :, :, 64:96], 0), g3(Q4[:, :, :, 64:96], 0), ALU.mult, tq)
        tq = red(sm(128, 64), SQr, tq)
        tq = tt(g3(SQn, 0), g3(KV4[:, :, :, 0:64], 0), g3(KV4[:, :, :, 0:64], 0), ALU.mult, tq)
        tq = red(sm(192, 64), g3(SQn, 0), tq)
        ts(sm(64, 64), sm(64, 64), 1.0 / 64, EPS, ALU.mult, ALU.add, tq)
        ts(sm(128, 64), sm(128, 64), 1.0 / 32, EPS, ALU.mult, ALU.add, tq)
        tq = ts(sm(192, 64), sm(192, 64), 1.0 / 64, EPS, ALU.mult, ALU.add, tq)
        tq = act(sm(64, 192), sm(64, 192), ACT.Sqrt, tq)
        tq = recip(sm(64, 192), sm(64, 192), tq)
        qn, qr, kn = g3(Q4[:, :, :, 0:64], 0), g3(Q4[:, :, :, 64:96], 0), g3(KV4[:, :, :, 0:64], 0)
        t1 = tt(qn, qn, bl(sm(64, 64), 64), ALU.mult, tq)
        t2 = tt(qr, qr, bl(sm(128, 64), 32), ALU.mult, tq)
        t3 = tt(kn, kn, bl(sm(192, 64), 64), ALU.mult, tq)
        t1 = tt(qn, qn, bc(GB[:, 0:64], 64), ALU.mult, t1)
        t2 = tt(qr, qr, bc(GB[:, 64:96], 64), ALU.mult, t2)
        t3 = tt(kn, kn, bc(GB[:, 96:160], 64), ALU.mult, t3)
        RA, RB, RC, RD = [AR[:, 1024 * i:1024 * (i + 1)] for i in range(4)]

        def rotate(a4, b4, shp, tok):
            c4, s4 = COS, SIN
            if shp == "q":
                c4 = v3(COS, 8).unsqueeze(2).broadcast_to([P, 8, 8, 16])
                s4 = v3(SIN, 8).unsqueeze(2).broadcast_to([P, 8, 8, 16])
                w = [r.rearrange("p (t h d) -> p t h d", t=8, h=8) for r in (RA, RB, RC, RD)]
            else:
                c4, s4 = v3(COS, 8), v3(SIN, 8)
                w = [v3(r[:, 0:128], 8) for r in (RA, RB, RC, RD)]
            m0 = tt(w[0], a4, c4, ALU.mult, tok, t_rope)
            m1 = tt(w[1], b4, s4, ALU.mult, tok)
            m2 = tt(w[2], b4, c4, ALU.mult, tok)
            m3 = tt(w[3], a4, s4, ALU.mult, tok)
            tt(a4, w[0], w[1], ALU.subtract, m3)
            return tt(b4, w[2], w[3], ALU.add, m3)

        tkr = rotate(KR3[:, :, 0:16], KR3[:, :, 16:32], "k", t3)
        t_qf = rotate(Q4[:, :, :, 64:80], Q4[:, :, :, 80:96], "q", tkr)

        QT = [AR[0:96, 15104 + 1024 * i:16128 + 1024 * i] for i in range(2)]
        KT = [AR[0:96, 17152 + 1024 * i:18176 + 1024 * i] for i in range(2)]
        K96 = AR[:, 19200:19968]
        PB = [AR[:, 1024 * i:1024 * (i + 1)] for i in range(2)]
        PT = [AR[:, 2048 + 1024 * i:3072 + 1024 * i] for i in range(2)]
        OP = [AR[:, 4096 + 1024 * i:5120 + 1024 * i] for i in range(2)]
        OT = [AR[:, 6144 + 1024 * i:7168 + 1024 * i] for i in range(2)]
        K3 = v3(K96, 8)
        oa_d, ob_d = a["oa_d"], a["ob_d"]
        s_oa = [slot(), slot()]
        start_att = [t_qf, last(PE)]
        qt_tok, qt_free, k_free = {}, [None, None], [None]

        def qk_T(h):
            s = h % 2
            tc = cp(GE, K3[:, :, 0:64], KV4[:, :, h, 0:64], start_att, k_free[0])
            tc = cp(GE, K3[:, :, 64:96], KR3, start_att)
            toks = []
            for (dst, src) in ((QT[s], lambda t: Q4[:, t, h, :]), (KT[s], lambda t: K3[:, t, :])):
                for g in range(2):
                    b, fr = acquire()
                    for j in range(4):
                        tk = tr(ps[0:96, b, j * P:(j + 1) * P], src(4 * g + j), tc, start_att, fr, mark=(j == 3))
                    te = cp(AE if g else VE, dst[:, g * 512:(g + 1) * 512], ps[0:96, b, :], tk, qt_free[s])
                    release(b, te)
                    toks.append(te)
            k_free[0] = tk
            qt_tok[h] = toks

        att = {}
        pb_free = [None, None]
        pt_free = [None, None]
        op_free = [None, None]
        ot_free = [None, None]

        def a_scores(i):
            h, q = divmod(i, 8)
            if q == 0:
                qk_T(h)
            b, fr = acquire(2)
            for j in range(2):
                tk = mm(ps[:, b + j, :], QT[h % 2][:, q * P:(q + 1) * P], KT[h % 2][:, j * 512:(j + 1) * 512],
                        True, True, qt_tok[h], fr, mark=(j == 1))
            if q == 7:
                qt_free[h % 2] = tk
            m = sm(256 + i % 4, 1)
            nb = sm(264 + i % 4, 1)
            rs = sm(272 + i % 4, 1)
            src = ps[:, b:b + 2, :].rearrange("p a b -> p (a b)")
            tm = red(m, src, tk, op=ALU.max)
            tm = ts(nb, m, -SCALE, None, ALU.mult, None, tm)
            te = act(PB[i % 2], src, ACT.Exp, tm, pb_free[i % 2], bias=nb, scale=SCALE, accum_out=rs)
            release(b, te, 2)
            att[i] = te

        def a_transp(i):
            b, fr = acquire(2)
            for j in range(8):
                tk = tr(ps[:, b + j // 4, (j % 4) * P:(j % 4 + 1) * P], PB[i % 2][:, j * P:(j + 1) * P],
                        att[i], fr, mark=(j in (3, 7)))
                if j == 3:
                    tk0 = tk
            pb_free[i % 2] = tk
            t0 = cp(VE, PT[i % 2][:, 0:512], ps[:, b, :], tk0, pt_free[i % 2])
            t1 = cp(AE, PT[i % 2][:, 512:1024], ps[:, b + 1, :], tk, pt_free[i % 2])
            release(b, t0)
            release(b + 1, t1)
            att[i] = [att[i], t0, t1]

        def a_pv(i):
            h, q = divmod(i, 8)
            b, fr = acquire()
            for j in range(8):
                tk = mm(ps[:, b, 0:64], PT[i % 2][:, j * P:(j + 1) * P], KV4[:, j, h, 64:128], j == 0, j == 7,
                        att[i], fr, mark=(j == 7))
            pt_free[i % 2] = tk
            rs = sm(272 + i % 4, 1)
            tq = recip(rs, rs, att[i])
            s = (h // 2) % 2
            dst = v3(OP[s], 8)[:, q, (h % 2) * 64:(h % 2) * 64 + 64]
            te = ts(dst, ps[:, b, 0:64], rs, None, ALU.mult, None, tq, tk, op_free[s])
            release(b, te)
            if i % 16 == 15:
                pr = h // 2
                for g in range(2):
                    b, fr = acquire()
                    for j in range(4):
                        tk = tr(ps[:, b, j * P:(j + 1) * P], OP[s][:, (4 * g + j) * P:(4 * g + j + 1) * P], te, fr,
                                mark=(j == 3))
                    tw = cp(VE, OT[s][:, g * 512:(g + 1) * 512], ps[:, b, :], tk, ot_free[s])
                    release(b, tw)
                op_free[s] = tk
                ot_free[s] = s_oa[s].dma(GE, oa_d[pr * P:(pr + 1) * P, :], OT[s], tw)

        for i in range(64 + 2):
            if i < 64:
                a_scores(i)
            if 1 <= i <= 64:
                a_transp(i - 1)
            if i >= 2:
                a_pv(i - 2)
        t_oa = list(ot_free)

        done = all_done() + [t_oa]
        for e in (PE, VE, AE, GE):
            e.wait(done)
        U = AR[:, 0:12288]
        U3 = v3(U, 8)
        UL = [AR[:, 12288 + 1024 * i:13312 + 1024 * i] for i in range(4)]
        BCT = AR[:, 16384:19456]
        KKB, KAB, RKB, A0B, W0F, W0B = [BCT[:, 512 * i:512 * (i + 1)] for i in range(6)]
        LW = AR[:, 19456:20480]
        A2W, W2B = LW[:, 0:512], LW[:, 512:1024]
        s_b = slot()
        rows = [(KKB, a["k_k"][0:1, :]), (KAB, a["k_a"][0:1, :]), (RKB, a["r_k"][0:1, :]), (A0B, a["a0"][0:1, :]),
                (W0F, a["w0"][0:1, :]), (W0B, a["w0"][1:2, :])]
        for dst, src in rows:
            t_b = s_b.dma(SP, dst, src.partition_broadcast(P).rearrange("p a n -> p (a n)"), done)
        t_b = s_b.dma(SP, A2W[0:64, :], a["a2"])
        t_b = s_b.dma(SP, A2W[64:128, :], a["w2"][0:64, :])
        t_b = s_b.dma(SP, W2B[0:64, :], a["w2"][64:128, :])
        RAW = [X[:, 1100 * i:1100 * i + 1026] for i in range(2)]
        U1 = [X[:, 2200 + 1024 * i:3224 + 1024 * i] for i in range(2)]
        U2 = [X[:, 4300 + 1024 * i:5324 + 1024 * i] for i in range(2)]
        C0 = sm(280, 16)
        tc0 = tt(C0, pc["mup"], pc["mun"], ALU.add)
        tc0 = ts(C0, C0, -1.0, 1.0, ALU.mult, ALU.add, tc0)
        for i in range(2):
            memset(VE, RAW[i][:, 0:1], 0.0)
            tz = memset(VE, RAW[i][:, 1025:1026], 0.0)
        raw_free, u2_free = [None, None], [None, None]
        pend = []

        def fin_shift(ft, n, dst, tok):
            s = ft % 2
            for g in range(2):
                b, fr = acquire()
                for j in range(4):
                    tk = tr(ps[:, b, j * P:(j + 1) * P], U2[s][:, (4 * g + j) * P:(4 * g + j + 1) * P], tok, fr,
                            mark=(j == 3))
                te = cp(AE, U3[:, 4 * g:4 * g + 4, ft * P:(ft + 1) * P], v3(ps[:, b, :], 4), tk)
                release(b, te)
            u2_free[s] = tk

        for ft in range(16):
            n = 64 if ft == 13 else 128
            s = ft % 2
            res = feat(a["w_rw"][ft], n, t_h, HT3)
            for h, (b, tk) in enumerate(res):
                te = cp(AE, RAW[s][0:n, 1 + 512 * h:513 + 512 * h], ps[0:n, b, :], tk, raw_free[s])
                release(b, te)
            t1 = act(U1[s][0:n, :], RAW[s][0:n, 1:1025], ACT.Copy, te, tc0, raw_free[s], scale=C0[0:n, ft:ft + 1])
            t2 = stt(U1[s][0:n, :], RAW[s][0:n, 0:1024], pc["mup"][0:n, ft:ft + 1], U1[s][0:n, :], ALU.mult, ALU.add,
                     t1, tz)
            dst = U2[s] if ft < 12 else UL[ft - 12]
            t3 = stt(dst[0:n, :], RAW[s][0:n, 2:1026], pc["mun"][0:n, ft:ft + 1], U1[s][0:n, :], ALU.mult, ALU.add,
                     t2, u2_free[s] if ft < 12 else None)
            raw_free[s] = t3
            if pend:
                fin_shift(*pend.pop())
            if ft < 12:
                pend.append((ft, n, dst, t3))
            elif ft == 12:
                tl = act(dst[64:128, :], dst[64:128, :], ACT.Tanh, t3)
            elif ft == 13:
                tl = act(dst[0:64, :], dst[0:64, :], ACT.Tanh, t3)
            else:
                tl = act(dst, dst, ACT.Sigmoid, t3)
        t_ul = [tl, t3]
        t_u = te
        t_u = last(AE)

        names = ["r", "k2", "v", "kkn", "b", "sgf", "sgb"]
        rw_d = a["rw_d"]
        RN = sm(300, 64)
        RN3 = v3(RN, 8)
        BS = sm(364, 64)
        BS3 = v3(BS, 8)
        CT = sm(428, 128)
        CT3 = v3(CT, 8)
        KT0, KT1 = X[:, 0:512], X[:, 512:1024]
        VE.wait(t_u, t3, last(PE))
        VE.wait(t_b)
        for t in range(NT):
            tq = tt(KT0, U3[:, t, 512:1024], KKB, ALU.mult, last(VE))
            tq = tt(KT0, KT0, KT0, ALU.mult, tq)
            tq = red(RN3[:, t, :], v3(KT0, 8), tq)
        tq = act(RN, RN, ACT.Sqrt, tq)
        tq = ts(RN, RN, 1e-12, None, ALU.max, None, tq)
        tq = recip(RN, RN, tq)
        t_rn = ts(RN, RN, -1.0, None, ALU.mult, None, tq)
        wb = [[X[:, 1024 + 3584 * i + 512 * j:1536 + 3584 * i + 512 * j] for j in range(7)] for i in range(2)]
        s_st = [slot(), slot()]
        st_free = [None, None]
        st_all = {}
        for t in range(NT):
            s = t % 2
            aa, k2, kkn, bb, sgf, sgb, tm = wb[s]
            sl = slice(t * P, (t + 1) * P)
            fre = st_free[s]
            sig = []
            for (row, lh, wt, bias, dst) in ((0, UL[0][0:64, sl], A2W[0:64, :], A0B, aa),
                                             (64, UL[0][64:128, sl], A2W[64:128, :], W0F, sgf),
                                             (0, UL[1][0:64, sl], W2B[0:64, :], W0B, sgb)):
                b, fr = acquire()
                tk = mm(ps[:, b, :], lh, wt, True, True, t_ul, t_b, fr, mark=True)
                te = tt(dst, ps[:, b, :], bias, ALU.add, tk, fre)
                release(b, te)
                sig.append(act(dst, dst, ACT.Sigmoid, te))
            t_a, t_f, t_g = sig
            r_, k_, v_ = U3[:, t, 0:512], U3[:, t, 512:1024], U3[:, t, 1024:1536]
            t1 = tt(kkn, k_, KKB, ALU.mult, fre)
            t1 = tt(v3(kkn, 8), v3(kkn, 8), bl(RN3[:, t, :], 64), ALU.mult, t1, t_rn)
            t1 = stt(bb, kkn, -1.0, aa, ALU.mult, ALU.mult, t1, t_a)
            t2 = stt(tm, aa, -1.0, KAB, ALU.add, ALU.mult, t_a)
            t2 = stt(k2, tm, 1.0, k_, ALU.add, ALU.mult, t2)
            t3 = tt(tm, r_, RKB, ALU.mult, t2)
            t3 = tt(tm, tm, k2, ALU.mult, t3)
            t3 = red(BS3[:, t, :], v3(tm, 8), t3)
            b, fr = acquire()
            for d, (sg, tsg) in enumerate(((sgf, t_f), (sgb, t_g))):
                for p in range(4):
                    tk = mm(ps[:, b, d * 8 + 2 * p:d * 8 + 2 * p + 2], sg[:, p * P:(p + 1) * P], cst["col"], True, True,
                            tsg, fr, mark=(d == 1 and p == 3))
            te = cp(VE, CT3[:, t, :], ps[:, b, 0:16], tk)
            release(b, te)
            ss_ = s_st[s]
            for j, (src, tok) in enumerate(((r_, t_u), (k2, t2), (v_, t_u), (kkn, t1), (bb, t1), (sgf, t_f), (sgb, t_g))):
                tw = ss_.dma(GE, rw_d[t, j], src, tok, fre)
            st_free[s] = [tw, t3, tk]
            st_all[t] = tw
        GG = sm(556, 64)
        G4 = GG.rearrange("p (d i q) -> p d i q", d=2, i=8)
        for d in range(2):
            for i in range(8):
                t = i if d == 0 else 7 - i
                o, r1 = G4[:, d, i, :], CT3[:, t, d * 8:d * 8 + 8].rearrange("p (q c) -> p q c", c=2)
                rest = r1[:, :, 1 - d]
                if i < 7:
                    nx = CT3[:, t + 1 - 2 * d, d * 8:d * 8 + 8].rearrange("p (q c) -> p q c", c=2)[:, :, d]
                    tg = tt(o, rest, nx, ALU.add, te)
                else:
                    tg = cp(VE, o, rest, te)
        t_g = act(GG, GG, ACT.Exp, tg, scale=-EH)

        done = all_done() + list(st_all.values())
        for e in (PE, VE, AE, GE):
            e.wait(done)
        GS = [UL[2], UL[3]]
        spaces = [[AR[:, 0:14336], EX[:, 0:4096]], [X[:, 0:8192], AR[:, 16384:22528], W[:, 0:4096]]]

        def allocator(regions):
            left = [[r, 0] for r in regions]

            def take(n):
                for x in left:
                    if x[0].shape[1] - x[1] >= n:
                        o = x[0][:, x[1]:x[1] + n]
                        x[1] += n
                        return o
                raise RuntimeError("no room")
            return take

        o_d = a["o_d"]
        o_marks = [{}, {}]

        def stream(d):
            take = allocator(spaces[d])
            LD = take(3072)
            r_, k2, v_, kkn, bb, sg = [LD[:, 512 * j:512 * (j + 1)] for j in range(6)]
            M4 = take(2048).rearrange("p (h c n) -> p h c n", h=4, c=4)
            ART = take(1024).rearrange("p (q c n) -> p q c n", q=4, c=2)
            BT, KT = v3(take(1024), 8), v3(take(1024), 8)
            E = [take(512) for _ in range(3)]
            Rt, Kt, Bt = E[0], E[1], take(512)
            Z0 = [take(512).rearrange("p (c h n) -> p c h n", c=2, h=4) for _ in range(2)]
            An, Dn, DT = [v3(take(512), 4) for _ in range(3)]
            D2, D2T, D4, D4T, D8 = [v3(take(512), 4) for _ in range(5)]
            Fn, FT, F2, F2T, F4T = D2, D2T, D4, D4T, D8
            XA, XB = [v3(take(512), 4) for _ in range(2)]
            zv = lambda z: z.rearrange("p h n -> p (h n)").rearrange("p (c h n) -> p c h n", c=2, h=4)
            ZA, ZB = zv(Dn), zv(DT)
            QT_, PT_ = v3(take(256), 2), v3(take(256), 2)
            SS = v3(take(512), 4)
            OB = take(512)
            s_ld, s_o = slot(), slot()
            TC = cst["TCF"] if d == 0 else cst["TCB"]
            sT, iT, sN = ("SU", "IU", "SL") if d == 0 else ("SL", "IL", "SU")
            dN, dT, oN, oT = ("DL", "DU", "OL", "OU") if d == 0 else ("DU", "DL", "OU", "OL")
            t_s = [memset(GE, SS, 0.0)] * 4
            ld_free, o_free = None, None
            b4 = lambda n: bc(cst[n], 4)
            for z in (BT, KT):
                memset(GE, z, 0.0)
            t_zero = last(GE)

            def batch(lhs, rhs, *toks):
                b, fr = acquire()
                for h in range(4):
                    tk = mm(ps[:, b, h * P:(h + 1) * P], lhs[:, h, :], rhs[:, h, :], True, True, fr, *toks,
                            mark=(h == 3))
                return b, v3(ps[:, b, :], 4), tk

            def apply(lhs, z, *toks):
                b, fr = acquire()
                pv = ps[:, b, :].rearrange("p (c h n) -> p c h n", c=2, h=4)
                for h in range(4):
                    tk = mm(pv[:, :, h, :], lhs[:, h, :], z[:, :, h, :], True, True, fr, *toks, mark=(h == 3))
                return b, pv, tk

            for i in range(8):
                t = i if d == 0 else 7 - i
                for j, (dst, jj) in enumerate(((sg, 5 + d), (r_, 0), (k2, 1), (v_, 2), (kkn, 3), (bb, 4))):
                    t_ld = s_ld.dma(SP, dst, rw_d[t, jj], done, ld_free)
                b, fr = acquire()
                tk = mm(ps[:, b, :], TC, sg, True, True, t_ld, fr, mark=True)
                te = tt(E[2], ps[:, b, :], sg, ALU.subtract, tk)
                t0 = act(E[0], ps[:, b, :], ACT.Exp, te, scale=-EH)
                t1 = act(E[1], ps[:, b, :], ACT.Exp, te, scale=EH)
                t2 = act(E[2], E[2], ACT.Exp, te, scale=-EH)
                release(b, t1)
                yield
                for u in range(2):
                    c = slice(256 * u, 256 * u + 256)
                    t_A = tt(Z0[u][:, 0, :, :], v3(kkn[:, c], 4), v3(E[2][:, c], 4), ALU.mult, t2, t_ld)
                t_B = tt(Bt, bb, E[1], ALU.mult, t1, t_ld, eng=GE)
                pt = [t_A, tt(Rt, r_, E[0], ALU.mult, t0, t_ld), t_B,
                      tt(Kt, k2, E[1], ALU.mult, t_B, eng=GE)]
                tT = []
                az = lambda p: Z0[p // 2][:, 0, 2 * (p % 2):2 * (p % 2) + 2, :].rearrange("p h n -> p (h n)")
                for n, (src, dst) in enumerate(((None, ART[:, :, 0, :]), (Rt, ART[:, :, 1, :]), (Bt, BT), (Kt, KT))):
                    b, fr = acquire()
                    for p in range(4):
                        tk = tr(ps[:, b, p * P:(p + 1) * P], src[:, p * P:(p + 1) * P] if n else az(p), pt[n], fr,
                                mark=(p == 3))
                    if n < 2:
                        te = cp(AE if n else VE, dst, v3(ps[:, b, :], 4), tk)
                    else:
                        eng = AE if n == 3 else VE
                        cp(eng, dst[0:64, 0::2, :], v3(ps[0:64, b, :], 4), tk, t_zero)
                        te = cp(eng, dst[64:128, 1::2, :], v3(ps[64:128, b, :], 4))
                    release(b, te)
                    tT.append(te)
                yield
                for u in range(2):
                    tM = []
                    for h in range(4):
                        p = 2 * u + h // 2
                        b, fr = acquire()
                        rr = ART[:, p, :, :].rearrange("k c n -> k (c n)")
                        mm(ps[:, b, 0:256], BT[:, 4 * u + h, :], rr, True, True, tT, fr)
                        tk = mm(ps[:, b, 256:512], KT[:, 4 * u + h, :], rr, True, True, mark=True)
                        pv = ps[:, b, :].rearrange("p (a c n) -> p a c n", a=2, c=2)
                        mv = M4[:, h, :, :].rearrange("p (a c) n -> p a c n", a=2)
                        ta = tt(mv[:, :, 0, :], pv[:, :, 0, :], bc(cst[sT], 2), ALU.mult, tk)
                        ta = tt(mv[:, :, 1, :], pv[:, :, 1, :], bc(cst[iT], 2), ALU.mult)
                        release(b, ta)
                        tM.append(ta)
                    b, fr = acquire()
                    for q in range(2):
                        h = 4 * u + 2 * q
                        tk = mm(ps[:, b, 256 * q:256 * q + 256], ART[:, 2 * u + q, 0, :],
                                BT[:, h:h + 2, :].rearrange("p h n -> p (h n)"), True, True, fr, mark=(q == 1))
                    tA = tt(An, v3(ps[:, b, :], 4), b4(sN), ALU.mult, tk)
                    release(b, tA)
                    yield
                    b, fr = acquire()
                    for h in range(4):
                        c = (4 * u + h) * 64
                        tk = mm(ps[:, b, h * 64:(h + 1) * 64], M4[:, h, 2, :], v_[:, c:c + 64], True, True, tM, fr,
                                mark=(h == 3))
                    tAV = cp(AE, Z0[u][:, 1, :, :], v3(ps[:, b, 0:256], 4), tk)
                    release(b, tAV)
                    tDT = tt(DT, M4[:, :, 0, :], b4(dT), ALU.mult, tM)
                    tDn = tt(Dn, An, b4(dN), ALU.mult, tA)
                    tX = tt(XA, DT, b4("ident"), ALU.add, tDT)
                    b, pv, tk = batch(DT, Dn, tDT, tDn)
                    t2 = cp(AE, D2, pv, tk)
                    release(b, t2)
                    b, pv, tk = batch(Dn, DT, tDT, tDn)
                    t2T = cp(VE, D2T, pv, tk)
                    release(b, t2T)
                    yield
                    b, pv, tk = batch(D2T, D2, t2, t2T)
                    t4 = cp(AE, D4, pv, tk)
                    release(b, t4)
                    b, pv, tk = batch(D2, D2T, t2, t2T)
                    t4T = cp(AE, D4T, pv, tk)
                    release(b, t4T)
                    b, pv, tk = batch(D2, XA, tX)
                    tX2 = tt(XB, pv, XA, ALU.add, tk)
                    release(b, tX2)
                    yield
                    b, pv, tk = batch(D4T, D4, t4, t4T)
                    t8 = cp(AE, D8, pv, tk)
                    release(b, t8)
                    b, pv, tk = batch(D4, XB, t4, tX2)
                    tX3 = tt(XA, pv, XB, ALU.add, tk)
                    release(b, tX3)
                    yield
                    b, pv, tk = batch(D8, XA, t8, tX3)
                    tX4 = tt(XB, pv, XA, ALU.add, tk)
                    release(b, tX4)
                    yield
                    b, pv, tk = batch(XB, An, tX4, tA)
                    tF = tt(Fn, pv, b4(oN), ALU.mult, tk)
                    release(b, tF)
                    b, pv, tk = batch(An, XB, tX4, tA)
                    tFT = tt(FT, pv, b4(oT), ALU.mult, tk)
                    release(b, tFT)
                    b, pv, tk = apply(XB, Z0[u], tX4, tAV, t_A)
                    tZ = cp(AE, ZA, pv, tk)
                    release(b, tZ)
                    yield
                    b, pv, tk = batch(FT, Fn, tF, tFT)
                    tF2 = cp(AE, F2, pv, tk)
                    release(b, tF2)
                    b, pv, tk = batch(Fn, FT, tF, tFT)
                    tF2T = cp(VE, F2T, pv, tk)
                    release(b, tF2T)
                    b, pv, tk = apply(FT, ZA, tZ)
                    tZ2 = tt(ZB, pv, ZA, ALU.add, tk)
                    release(b, tZ2)
                    yield
                    b, pv, tk = batch(F2, F2T, tF2, tF2T)
                    tF4T = cp(AE, F4T, pv, tk)
                    release(b, tF4T)
                    b, pv, tk = apply(F2T, ZB, tZ2)
                    tZ3 = tt(ZA, pv, ZB, ALU.add, tk)
                    release(b, tZ3)
                    yield
                    b, pv, tk = apply(F4T, ZA, tF4T, tZ3)
                    tZ4 = tt(ZB, pv, ZA, ALU.add, tk)
                    release(b, tZ4)
                    yield
                    b, fr = acquire()
                    for h in range(4):
                        lo = 64 * (h % 2)
                        tk = mm(ps[lo:lo + 64, b, (h // 2) * P:(h // 2 + 1) * P], ZB[:, 0, h, :], M4[:, h, 1, :],
                                True, True, tZ4, fr, mark=(h == 3))
                    tQ = tt(QT_, v3(ps[:, b, 0:256], 2), ART[:, 2 * u:2 * u + 2, 1, :], ALU.add, tk)
                    release(b, tQ)
                    b, fr = acquire()
                    for q in range(2):
                        p = 2 * u + q
                        tk = mm(ps[:, b, q * P:(q + 1) * P], ZB[:, 0, 2 * q:2 * q + 2, :].rearrange("p h n -> p (h n)"), Bt[:, p * P:(p + 1) * P],
                                True, True, fr, mark=(q == 1))
                    tP = tt(PT_, v3(ps[:, b, 0:256], 2), bc(cst["BD"], 2), ALU.mult, tk)
                    release(b, tP)
                    tP = tt(PT_, PT_, bc(ident, 2), ALU.add, tP)
                    yield
                    b, fr = acquire()
                    for q in range(2):
                        p = 2 * u + q
                        mm(ps[:, b, q * P:(q + 1) * P], QT_[:, q, :], SS[:, p, :], True, False, tQ, t_s[p], fr, lax=True)
                        for hh in range(2):
                            h = 2 * q + hh
                            c = (4 * u + h) * 64
                            o = ps[:, b, h * 64:(h + 1) * 64]
                            mm(o, M4[:, h, 1, :], ZB[:, 1, h, :], False, False, lax=True)
                            tk = mm(o, M4[:, h, 3, :], v_[:, c:c + 64], False, hh == 1, lax=True, mark=(h == 3))
                    tO = cp(AE, OB[:, u * 256:(u + 1) * 256], ps[:, b, 0:256], tk, o_free)
                    release(b, tO)
                    b, fr = acquire()
                    for q in range(2):
                        p = 2 * u + q
                        o = ps[:, b, q * P:(q + 1) * P]
                        mm(o, PT_[:, q, :], SS[:, p, :], True, False, tP, fr)
                        mm(o, Bt[:, p * P:(p + 1) * P], ZB[:, 1, 2 * q:2 * q + 2, :], False, False)
                        tk = mm(o, Kt[:, p * P:(p + 1) * P], v_[:, p * P:(p + 1) * P], False, True, mark=(q == 1))
                    for q in range(2):
                        p = 2 * u + q
                        t_s[p] = stt(SS[:, p, :], ps[:, b, q * P:(q + 1) * P], G4[:, d, i, p:p + 1], cst["BD"],
                                     ALU.mult, ALU.mult, tk)
                    release(b, t_s[p])
                    yield
                ld_free = [last(PE), last(VE), last(GE)]
                o_free = s_o.dma(GE, o_d[d, t], OB, tO)
                o_marks[d][t] = o_free

        interleave(stream(0), stream(1))

        done = all_done() + [o_marks[0][7], o_marks[1][0]]
        for e in (PE, VE, AE, GE):
            e.wait(done)
        OF = [X[:, 0:4096], X[:, 4096:8192]]
        VV = AR[:, 0:4096]
        LG, LB_ = AR[:, 4096:4608], AR[:, 4608:5120]
        G2 = [AR[:, 5120:5632], AR[:, 5632:6144]]
        s_of = slot()
        for d in range(2):
            t_of = s_of.dma(SP, v3(OF[d], 8), o_d[d].rearrange("t p n -> p t n"), done)
        t_of = s_of.dma(SP, v3(VV, 8), rw_d[:, 2].rearrange("t p n -> p t n"))
        t_of = s_of.dma(SP, LG, a["ln_x_g"].partition_broadcast(P).rearrange("p a n -> p (a n)"))
        t_of = s_of.dma(SP, LB_, a["ln_x_b"].partition_broadcast(P).rearrange("p a n -> p (a n)"))
        t_of = s_of.dma(SP, G2[0], a["g2"][0:128, :])
        t_of = s_of.dma(SP, G2[1], a["g2"][128:256, :])
        MU, VR = sm(620, 128), sm(748, 128)
        SQT = AR[:, 6144:10240]
        VE.wait(t_of)
        for d in range(2):
            o3 = OF[d].rearrange("p (g n) -> p g n", n=64)
            mu, vr = MU[:, d * 64:(d + 1) * 64], VR[:, d * 64:(d + 1) * 64]
            t1 = red(mu, o3)
            t1 = ts(mu, mu, 1.0 / 64, None, ALU.mult, None, t1)
            t1 = tt(o3, o3, bl(mu, 64), ALU.subtract, t1)
            t1 = act(SQT, OF[d], ACT.Square, t1, last(VE))
            t1 = red(vr, SQT.rearrange("p (g n) -> p g n", n=64), t1)
        tv = ts(VR, VR, 1.0 / 64, GN_EPS, ALU.mult, ALU.add, t1)
        tv = act(VR, VR, ACT.Sqrt, tv)
        tv = recip(VR, VR, tv)
        OBT = AR[:, 10240:14336]
        GSL = GS
        OBT3 = v3(OBT, 4)
        tb_free = [None, None]
        for t in range(NT):
            bon = SQT[:, 0:512]
            acc = SQT[:, 512 + 512 * (t % 2):1024 + 512 * (t % 2)]
            tb = tt(v3(bon, 8), v3(VV[:, t * 512:(t + 1) * 512], 8), bl(BS3[:, t, :], 64), ALU.mult, last(VE))
            tb = tt(bon, bon, LB_, ALU.add, tb)
            for d in range(2):
                b, fr = acquire()
                tk = mm(ps[:, b, :], GSL[d][:, t * P:(t + 1) * P], G2[d], True, True, t_of, fr, mark=True)
                ot = OF[d][:, t * 512:(t + 1) * 512]
                v = VR[:, d * 64 + t * 8:d * 64 + t * 8 + 8]
                t1 = tt(v3(ot, 8), v3(ot, 8), bl(v, 64), ALU.mult, tv)
                t1 = tt(ot, ot, LG, ALU.mult, t1)
                t1 = tt(ot, ot, bon, ALU.add, t1, tb)
                t1 = tt(acc if d == 0 else ot, ot, ps[:, b, :], ALU.mult, tk, t1, tb_free[t % 2])
                release(b, t1)
            t1 = tt(acc, acc, OF[1][:, t * 512:(t + 1) * 512], ALU.add, t1)
            b, fr = acquire()
            for p in range(4):
                tk = tr(ps[:, b, p * P:(p + 1) * P], acc[:, p * P:(p + 1) * P], t1, fr, mark=(p == 3))
            tb_free[t % 2] = tk
            te = cp(AE, OBT3[:, :, t * P:(t + 1) * P], v3(ps[:, b, :], 4), tk)
            release(b, te)
        t_ob = te

        done = all_done()
        OAT = AR[:, 0:4096]
        OAT3 = v3(OAT, 4)
        MIX = AR[:, 14336:22528]
        MIX3 = v3(MIX, 8)
        for e in (PE, VE, AE, GE, SP):
            e.wait(done)
        s_r = slot()
        t_oat = s_r.dma(SP, OAT3, oa_d.rearrange("(k p) n -> p k n", p=P), t_oa)
        t_xr = [xsl[t].dma(SP, X[:, t * D:(t + 1) * D], a["x"][t * P:(t + 1) * P, :]) for t in range(NT)]
        GT = [AR[:, 4096 + 512 * i:4608 + 512 * i] for i in range(8)]
        gfree = [None] * 4
        tm = None
        for n in range(8):
            r0, w0 = load_w(a["w_g"][n])
            r1, w1 = load_w(a["w_g"][8 + n])
            r2, w2 = load_w(a["w_o"][n])
            for h in range(2):
                s = (2 * n + h) % 2
                hs = slice(512 * h, 512 * h + 512)
                gt = []
                for i, (r, w) in enumerate(((r0, w0), (r1, w1))):
                    b, fr = acquire()
                    w3 = v3(r.ap, 8)
                    for k in range(8):
                        tk = mm(ps[:, b, :], w3[:, k, :], HT3[:, k, hs], k == 0, k == 7, w, fr, mark=(k == 7))
                    r.free = tk
                    te = act(GT[2 * s + i], ps[:, b, :], ACT.Sigmoid, tk, gfree[s],
                             bias=pc["bg"][:, 8 * i + n:8 * i + n + 1])
                    release(b, te)
                    gt.append(te)
                w3 = v3(r2.ap, 8)
                ty = []
                for i, src in enumerate((OAT3, OBT3)):
                    b, fr = acquire()
                    for k in range(4):
                        tk = mm(ps[:, b, :], w3[:, 4 * i + k, :], src[:, k, hs], k == 0, k == 3, w2, t_oat, t_ob, fr,
                                mark=(k == 3))
                    te = tt(GT[2 * s + i], GT[2 * s + i], ps[:, b, :], ALU.mult, tk, gt[i])
                    release(b, te)
                    ty.append(te)
                r2.free = tk
                tm = tt(MIX3[:, n, hs], GT[2 * s], GT[2 * s + 1], ALU.add, ty)
                gfree[s] = tm
        t_x1 = {}

        def add_x(t, nh, b, tk):
            xt = X[:, t * D + nh * 512:t * D + nh * 512 + 512]
            te = tt(xt, xt, b, ALU.add, tk, t_xr[t])
            t_x1[t] = te
            return te

        tokmajor(lambda nh, s: a["w_merge"][nh, s], MIX3, 8, 2, tm, add_x)

        def ffn(no, gain, wg, wu, wd, conv):
            st = ExitStack()
            FR = mybir.dt.float32r
            HH = region(st, f"HH_{no}", 8192, FR)[:, :]
            HL = region(st, f"HL_{no}", 8192, FR)[:, :]
            HAB = region(st, f"HA_{no}", 12 * 1024)
            WS = region(st, f"WS_{no}", 4096, FR)
            SA = region(st, f"SA_{no}", 2048, FR)
            tok_h = norm_all(gain, t_x1, [W1[:, 0:1024]], [last(PE), last(VE), last(AE), last(GE)], HH, HL)
            HH3, HL3 = v3(HH, 8), v3(HL, 8)
            HA = HAB[:, :].rearrange("p (f n) -> p f n", f=12)

            split_at = [0]
            split_free = [None, None]

            def split(src):
                r, tw = load_w(src)
                s = split_at[0] % 2
                split_at[0] += 1
                hi, lo = WS[:, s * 2048:s * 2048 + 1024], WS[:, s * 2048 + 1024:s * 2048 + 2048]
                t1 = act(hi, r.ap, ACT.Copy, tw, split_free[s])
                t2 = tt(lo, r.ap, hi.bitcast(F32), ALU.subtract, t1)
                r.free = t2
                return s, hi, lo, t2

            ahead = []
            todo = []

            def split_ahead():
                if todo:
                    ahead.append(split(todo.pop(0)))

            def next_split():
                if not ahead:
                    split_ahead()
                return ahead.pop(0)

            def three(o, ah, al, bh, bl_, first, lst, *toks):
                mm(o, ah, bl_, first, False, *toks)
                mm(o, al, bh, False, False)
                return mm(o, ah, bh, False, lst, mark=lst)

            def featr():
                s, wh, wl, tw = next_split()
                split_ahead()
                wh, wl = v3(wh, 8), v3(wl, 8)
                res = []
                for h in range(2):
                    hs = slice(h * 512, h * 512 + 512)
                    b, fr = acquire()
                    for k in range(8):
                        tk = three(ps[:, b, :], wh[:, k, :], wl[:, k, :], HH3[:, k, hs], HL3[:, k, hs], k == 0, k == 7,
                                   tw, tok_h, fr)
                    res.append((b, tk))
                split_free[s] = tk
                return res

            def down(f0, nf, tok_a):
                sa_free = [None, None]
                for tg in range(2):
                    for nh in range(2):
                        banks = [acquire() for _ in range(4)]
                        marks = [None] * 4
                        for q in range(nf // 2):
                            s, wh, wl, tw = next_split()
                            wh, wl = v3(wh, 2), v3(wl, 2)
                            parts = []
                            for x in range(2):
                                src = HA[:, 2 * q + x, tg * 512:tg * 512 + 512]
                                ah, al = SA[:, x * 1024:x * 1024 + 512], SA[:, x * 1024 + 512:x * 1024 + 1024]
                                t1 = act(ah, src, ACT.Copy, tok_a, sa_free[x])
                                t1 = tt(al, src, ah.bitcast(F32), ALU.subtract, t1)
                                parts.append((ah, al, t1))
                            split_ahead()
                            for kk in range(2):
                                k = 2 * q + kk
                                ah, al, t1 = parts[kk]
                                for j in range(4):
                                    b, fr = banks[j]
                                    lk = k == nf - 1
                                    o = ps[:, b, :]
                                    js = slice(j * P, (j + 1) * P)
                                    mm(o, ah[:, js], wl[:, kk, :], k == 0, False, t1, tw, fr)
                                    mm(o, al[:, js], wh[:, kk, :], False, False)
                                    m = mm(o, ah[:, js], wh[:, kk, :], False, lk, mark=(lk or j == 3))
                                    if lk:
                                        marks[j] = m
                                sa_free[kk] = m
                            split_free[s] = m
                        for j in range(4):
                            t = tg * 4 + j
                            xt = X[:, t * D + nh * 512:t * D + nh * 512 + 512]
                            te = tt(xt, xt, ps[:, banks[j][0], :], ALU.add, marks[j])
                            t_x1[t] = te
                            release(banks[j][0], te)

            for f0, nf in ((0, 12), (12, 10)):
                for f in range(f0, f0 + nf):
                    todo += [wg[f], wu[f]]
                todo += [wd[nh, f0 // 2 + q] for tg in range(2) for nh in range(2) for q in range(nf // 2)]
            rawf = [W1[:, 0:1026], W1[:, 1026:2052]]
            AE.wait(last(VE), last(PE))
            fr_raw = [None, None]
            fr_s = [None, None]
            if conv:
                for i in range(2):
                    memset(VE, rawf[i][:, 0:1], 0.0, last(PE), last(AE), last(VE))
                    tz = memset(VE, rawf[i][:, 1025:1026], 0.0)
            ha_free = None
            for f in range(NF):
                s = f % 2
                gb = featr()
                ub = featr()
                dst = HA[:, f % 12, :]
                if f == 12:
                    VE.wait(ha_free)
                if conv:
                    for h, (b, tk) in enumerate(gb):
                        te = cp(AE, rawf[s][:, 1 + 512 * h:513 + 512 * h], ps[:, b, :], tk, fr_raw[s])
                        release(b, te)
                    t1 = ts(dst, rawf[s][:, 1:1025], pc["cw1"][:, f:f + 1], pc["cb"][:, f:f + 1], ALU.mult, ALU.add, te)
                    t1 = stt(dst, rawf[s][:, 0:1024], pc["cw0"][:, f:f + 1], dst, ALU.mult, ALU.add, t1)
                    t1 = stt(dst, rawf[s][:, 2:1026], pc["cw2"][:, f:f + 1], dst, ALU.mult, ALU.add, t1)
                    fr_raw[s] = t1
                    sg = act(rawf[s][:, 1:1025], dst, ACT.Sigmoid, t1)
                    t1 = tt(dst, dst, rawf[s][:, 1:1025], ALU.mult, sg)
                    fr_raw[s] = t1
                    for h, (b, tk) in enumerate(ub):
                        te = tt(dst[:, 512 * h:512 * h + 512], dst[:, 512 * h:512 * h + 512], ps[:, b, :], ALU.mult, tk, t1)
                        release(b, te)
                else:
                    for h, (b, tk) in enumerate(gb):
                        hs = slice(512 * h, 512 * h + 512)
                        sg = act(rawf[s][:, hs], ps[:, b, :], ACT.Sigmoid, tk, fr_raw[s])
                        t1 = tt(dst[:, hs], rawf[s][:, hs], ps[:, b, :], ALU.mult, sg)
                        release(b, t1)
                        b2, tk2 = ub[h]
                        te = tt(dst[:, hs], dst[:, hs], ps[:, b2, :], ALU.mult, tk2, t1)
                        release(b2, te)
                    fr_raw[s] = te
                if f == 11:
                    down(0, 12, te)
                    ha_free = [last(PE), last(VE), last(AE)]
            down(12, 10, te)
            st.close()

        room.close()
        ffn(1, pc["g_ffn"], a["w_fg"], a["w_fu"], a["w_fd"], True)

        room = ExitStack()
        HT = region(room, "HT_2", 8192)
        AR = region(room, "AR_2", 22528)
        EX = region(room, "EX_2", 1024)
        HT3 = v3(HT[:, :], 8)
        tmpx = [W1[:, 0:1024], W1[:, 1024:2048]]
        t_h = norm_all(pc["g_n1"], t_x1, tmpx, [last(PE), last(VE), last(AE)], HT[:, :])
        QK = AR[:, 0:4096]
        V2 = AR[:, 4096:8192]
        GP = AR[:, 8192:12288]
        OG = AR[:, 12288:16384]
        OC = AR[:, 16384:20480]
        ZL = AR[:, 20480:22528]
        QK3, V23, GP3, OG3, OC3, ZL3 = [v3(r, k) for r, k in ((QK, 8), (V2, 8), (GP, 8), (OG, 8), (OC, 4), (ZL, 8))]
        WAG = EX[:, 0:640]
        s_g = slot()
        t_wg = s_g.dma(SP, v3(WAG[:, 0:128], 8), a["w_a"], all_done())
        t_wg = s_g.dma(SP, WAG[0:16, 128:384], a["w_gate_up"])
        t_wg = s_g.dma(SP, WAG[:, 384:640], a["b_gate_2"].partition_broadcast(P).rearrange("p a n -> p (a n)"))
        tv2 = [None]
        pre = last(PE)

        def ev2(t, nh, b, tk):
            dst = (QK3, V23, GP3)[nh][:, t, :]
            tv2[0] = cp(AE, dst, b, tk, pre)
            return tv2[0]
        tokmajor(lambda nh, s: a["w_tok2"][nh, s], HT3, 8, 3, t_h, ev2)
        t_qkv = tv2[0]
        PA = OG
        WA3 = v3(WAG[:, 0:128], 8)
        for h in range(2):
            b, fr = acquire()
            for k in range(8):
                tk = mm(ps[0:16, b, :], WA3[:, k, :], HT3[:, k, 512 * h:512 * h + 512], k == 0, k == 7, t_wg, fr,
                        mark=(k == 7))
            te = cp(VE, PA[0:16, 512 * h:512 * h + 512], ps[0:16, b, :], tk, pre)
            release(b, te)
        t_pa = te
        for t in range(NT):
            b, fr = acquire()
            tk = mm(ps[:, b, 0:256], PA[0:16, t * P:(t + 1) * P], WAG[0:16, 128:384], True, True, t_pa, fr, mark=True)
            te = tt(ZL3[:, t, :], ps[:, b, 0:256], WAG[:, 384:640], ALU.add, tk, t_wg)
            release(b, te)
        ZT = OG[:, 1024:3072]
        t1 = stt(ZT, ZL, -1.0, ZL, ALU.mult, ALU.max, te)
        t1 = act(ZT, ZT, ACT.Exp, t1, scale=-1.0)
        t1 = act(ZT, ZT, ACT.Ln, t1, bias=1.0)
        t_la = stt(ZL, ZL, 0.0, ZT, ALU.min, ALU.subtract, t1)

        UC = W1[:, 0:1026]
        CC = OG[:, 3072:4096]
        tz = memset(VE, UC[:, 0:2], 0.0, last(PE))
        uc_free = None
        for j in range(4):
            cc = feat(a["w_cv"][4 + j], P, t_h, HT3)
            ch = feat(a["w_cv"][8 + j], P, t_h, HT3)
            for h in range(2):
                hs = slice(512 * h, 512 * h + 512)
                te = cp(AE, CC[:, hs], ps[:, cc[h][0], :], cc[h][1], uc_free)
                release(cc[h][0], te)
                te = tt(UC[:, 2 + 512 * h:514 + 512 * h], CC[:, hs], ps[:, ch[h][0], :], ALU.mult, te, ch[h][1], uc_free)
                release(ch[h][0], te)
            cb = feat(a["w_cv"][j], P, t_h, HT3)
            dst = OC3[:, j, :]
            t1 = ts(dst, UC[:, 2:1026], pc["gw2"][:, j:j + 1], None, ALU.mult, None, te, tz)
            t1 = stt(dst, UC[:, 1:1025], pc["gw1"][:, j:j + 1], dst, ALU.mult, ALU.add, t1)
            t1 = stt(dst, UC[:, 0:1024], pc["gw0"][:, j:j + 1], dst, ALU.mult, ALU.add, t1)
            uc_free = t1
            for h in range(2):
                hs = slice(512 * h, 512 * h + 512)
                te = tt(dst[:, hs], dst[:, hs], ps[:, cb[h][0], :], ALU.mult, t1, cb[h][1])
                release(cb[h][0], te)
        t_oc = te

        done = all_done()
        for e in (PE, VE, AE, GE):
            e.wait(done)
        hat = [0]

        def hb(n):
            hat[0] += n
            return HT[:, hat[0] - n:hat[0]]
        sets = []
        for i in range(2):
            sets.append([hb(256) for _ in range(3)] + [hb(256) for _ in range(4)] + [hb(512), hb(512)])
        SG = hb(512)
        TS = hb(512)
        GD = sm(876, 32)
        t_sg = memset(VE, SG, 0.0)
        t_og = None
        prev = None
        for t in range(NT):
            Eb, Enb, Er, qi, ki, ks0, ks1, QKT, ST = sets[t % 2]
            la = ZL3[:, t, :]
            b, fr = acquire()
            mm(ps[:, b, 0:256], cst["TRI"], la, True, True, t_la, fr)
            tk = mm(ps[:, b, 256:512], cst["REST"], la, True, True, mark=True)
            fo = [last(PE)]
            t0 = act(Eb, ps[:, b, 0:256], ACT.Exp, tk, last(VE), scale=1.0 / 16)
            t1 = act(Enb, ps[:, b, 0:256], ACT.Exp, scale=-1.0 / 16)
            t2 = act(Er, ps[:, b, 256:512], ACT.Exp, scale=1.0 / 16)
            release(b, t2)
            b, fr = acquire()
            for q in range(2):
                tk = mm(ps[:, b, 2 * q:2 * q + 2], la[:, q * P:(q + 1) * P], cst["col"], True, True, fr, mark=(q == 1))
            gd = GD[:, 4 * t:4 * t + 4]
            t_gd = act(gd, ps[:, b, 0:4], ACT.Exp, tk, scale=1.0 / 16)
            release(b, t_gd)
            qq, kk = QK3[:, t, 0:256], QK3[:, t, 256:512]
            m0 = stt(qi, qq, 0.125, Eb, ALU.mult, ALU.mult, t0, fo)
            m1 = tt(ki, kk, Enb, ALU.mult, t1)
            m2 = stt(ks0, kk, cst["col"][:, 0:1], Er, ALU.mult, ALU.mult, t2)
            m3 = stt(ks1, kk, cst["col"][:, 1:2], Er, ALU.mult, ALU.mult, t2)
            b, fr = acquire()
            for q in range(2):
                tr(ps[:, b, q * P:(q + 1) * P], qi[:, q * P:(q + 1) * P], m0, m1, fr)
            for q in range(2):
                tk = tr(ps[:, b, (2 + q) * P:(3 + q) * P], ki[:, q * P:(q + 1) * P], mark=(q == 1))
            te = cp(AE, QKT, ps[:, b, :], tk)
            release(b, te)
            QT4 = v3(QKT, 4)
            (b0, f0), (b1, f1) = acquire(), acquire()
            for h in range(4):
                lo = 64 * (h % 2)
                b = (b0, b1)[h % 2]
                tk = mm(ps[:, b, (h // 2) * P:(h // 2 + 1) * P], QT4[lo:lo + 64, 2 + h // 2, :],
                        QT4[lo:lo + 64, h // 2, :], True, True, te, f0, f1, mark=(h == 3))
            ST3 = v3(ST, 4)
            for h in range(2):
                t_st = tt(ST3[:, h::2, :], v3(ps[:, (b0, b1)[h], 0:256], 2), bc(cst["TRI"], 2), ALU.mult, tk)
                release((b0, b1)[h], t_st)
            bo, fr = acquire()
            vt = V23[:, t, :]
            for h in range(4):
                mm(ps[:, bo, h * P:(h + 1) * P], ST3[:, h, :], vt[:, h * P:(h + 1) * P], h == 0, False, t_st, fr,
                   lax=True)
            for c in range(2):
                for q in range(2):
                    tk = mm(ps[64 * c:64 * c + 64, bo, q * 256:(q + 1) * 256], QT4[:, q, 64 * c:64 * c + 64],
                            SG[:, q * 256:(q + 1) * 256], False, True, t_sg, lax=True, mark=True)
                bs, fs = acquire()
                ksc = (ks0, ks1)[c]
                for q in range(2):
                    tk2 = mm(ps[:, bs, q * 256:(q + 1) * 256], ksc[:, q * P:(q + 1) * P], vt[:, q * 256:(q + 1) * 256],
                             True, True, m3, fs, mark=(q == 1))
                bd = cst["BD"].rearrange("p (a b) -> p a b", a=2)
                bdv = bd[:, :, 0:1].unsqueeze(1).broadcast_to([P, 2, 2, 128])
                psv = ps[:, bs, :].rearrange("p (q a n) -> p q a n", q=2, a=2)
                tsv = TS.rearrange("p (q a n) -> p q a n", q=2, a=2)
                t1 = None
                for q in range(2):
                    t1 = tt(tsv[:, q], psv[:, q], bl(cst["BD"][:, 0:128:64], 128), ALU.mult, tk2, t_sg)
                release(bs, t1)
                for q in range(2):
                    t_sg = stt(SG[:, q * 256:(q + 1) * 256], SG[:, q * 256:(q + 1) * 256], gd[:, 2 * q + c:2 * q + c + 1],
                               TS[:, q * 256:(q + 1) * 256], ALU.mult, ALU.add, t1, tk, t_gd)
            t_og = cp(AE, OG3[:, t, :], ps[:, bo, :], tk)
            release(bo, t_og)
        RS2 = sm(908, 32)
        done = all_done()
        for e in (PE, VE, AE, GE):
            e.wait(done)
        GN = EX[:, 640:768]
        t_gn = s_g.dma(SP, GN[:, :], a["gla_norm_g_2"].partition_broadcast(P).rearrange("p a n -> p (a n)"))
        SQ2 = AR[:, 0:4096]
        t1 = act(SQ2, OG, ACT.Square)
        t1 = red(RS2, SQ2.rearrange("p (g n) -> p g n", n=128), t1)
        t1 = rstd(RS2, 128, EPS, t1)
        og3 = OG.rearrange("p (g n) -> p g n", n=128)
        t1 = tt(og3, og3, bl(RS2, 128), ALU.mult, t1)
        t1 = tt(og3, og3, bc(GN[:, :], 32), ALU.mult, t1, t_gn)
        t2 = act(SQ2, GP, ACT.Sigmoid, t1)
        t2 = tt(SQ2, SQ2, GP, ALU.mult, t2)
        t2 = tt(OG, OG, SQ2, ALU.mult, t2, t1)
        OGT = AR[:, 4096:8192]
        OGT3 = v3(OGT, 4)
        for t in range(NT):
            b, fr = acquire()
            for p in range(4):
                tk = tr(ps[:, b, p * P:(p + 1) * P], OG3[:, t, p * P:(p + 1) * P], t2, fr, mark=(p == 3))
            te = cp(AE, OGT3[:, :, t * P:(t + 1) * P], v3(ps[:, b, :], 4), tk)
            release(b, te)

        class Two:
            def __getitem__(self, key):
                p, k, n = key
                return OGT3[p, k, n] if k < 4 else OC3[p, k - 4, n]

        def add2(t, nh, b, tk):
            xt = X[:, t * D + nh * 512:t * D + nh * 512 + 512]
            t_x1[t] = tt(xt, xt, b, ALU.add, tk)
            return t_x1[t]
        tokmajor(lambda nh, s: a["w_out"][nh, s], Two(), 8, 2, te, add2)
        room.close()
        ffn(2, pc["g_n2"], a["w_fg2"], a["w_fu2"], a["w_fd2"], False)

        FN = sb("FN", 3072)
        NFB = FN[:, 0:1024]
        s_f = slot()
        t_nf = s_f.dma(SP, NFB, a["norm_f"].partition_broadcast(P).rearrange("p a n -> p (a n)"), all_done())
        s_out = slot()
        for t in range(NT):
            xt = X[:, t * D:(t + 1) * D]
            ss = sm(940 + t, 1)
            tq = act(FN[:, 1024 + 1024 * (t % 2):2048 + 1024 * (t % 2)], xt, ACT.Square, t_x1[t], last(AE), last(PE), accum_out=ss)
            tq = rstd(ss, D, EPS, tq)
            tq = stt(xt, xt, ss, NFB, ALU.mult, ALU.mult, tq, t_nf)
            t_o = s_out.dma(SP, out[t * P:(t + 1) * P, :], xt, tq)
        SP.wait(t_o)
        SP.wait(t_oa)

        block = ctx.enter_context(nc.Block())

        @block.tensor
        def _(e):
            PE.run(e)

        @block.vector
        def _(e):
            VE.run(e)

        @block.scalar
        def _(e):
            AE.run(e)

        @block.gpsimd
        def _(e):
            GE.run(e)

        @block.sync
        def _(e):
            SP.run(e)


def kernel(**inputs):
    import concourse.bacc as _bacc
    from concourse.bass_utils import run_bass_kernel_spmd as _run

    g = {n: np.ascontiguousarray(v) for n, v in inputs.items()}
    asc = np.ascontiguousarray

    def feat(w, n=P):
        return asc(w.reshape(8, P, -1, n).transpose(2, 1, 0, 3).reshape(-1, P, 8 * n))

    def tok(w):
        k, n = w.shape
        return asc(w.reshape(k // 256, 2, P, n // 512, 512).transpose(3, 0, 2, 1, 4).reshape(n // 512, k // 256, P, 1024))

    def cols(v):
        return v.reshape(-1, P).T

    w_in, w2in = g["w_in"][0], g["w_in_2"][0]
    rw = w_in[:, 416:2400]
    zpad = lambda v: np.concatenate([v[..., :1728], v[..., :64], v[..., 1728:]], -1)
    mu = zpad(g["shift_mu"][0])
    order = {
        "g_mix": cols(g["norm_mix_g"][0]), "g_qa": cols(g["q_a_norm_g"][0]), "g_kva": cols(g["kv_a_norm_g"][0]),
        "mup": cols(mu[0]), "mun": cols(mu[1]), "bg": cols(g["b_gate"][0].reshape(-1)),
        "g_ffn": cols(g["norm_ffn_g"][0]), "cw0": cols(g["ffn_conv_w"][0, 0]), "cw1": cols(g["ffn_conv_w"][0, 1]),
        "cw2": cols(g["ffn_conv_w"][0, 2]), "cb": cols(g["ffn_conv_b"][0]), "g_n1": cols(g["norm1_g_2"][0]),
        "g_n2": cols(g["norm2_g_2"][0]), "gw0": cols(g["conv_w_2"][0, 0]), "gw1": cols(g["conv_w_2"][0, 1]),
        "gw2": cols(g["conv_w_2"][0, 2]),
    }
    ins = {
        "x": g["x"][0], "pos": asc(g["positions"].reshape(8, P).T), "cst": const_table(),
        "pcols": asc(np.concatenate([order[n] for n, _ in PCOLS], 1)),
        "w_mla": asc(w_in[:, 0:416].reshape(8, P, 416).transpose(1, 0, 2)),
        "w_rw": feat(zpad(rw)), "w_g": feat(w_in[:, 2400:]), "w_uq": g["w_uq"][0], "w_ukv": g["w_ukv"][0],
        "qn_norm_g": g["qn_norm_g"], "qr_norm_g": g["qr_norm_g"], "kn_norm_g": g["kn_norm_g"],
        "kr_norm_g": g["kr_norm_g"], "k_k": g["k_k"], "k_a": g["k_a"], "r_k": g["r_k"].reshape(1, 512),
        "a0": g["a0"], "w0": g["w0"][0], "a2": g["a2"][0], "w2": g["w2"][0].reshape(128, 512),
        "g2": g["g2"][0].reshape(256, 512), "ln_x_g": g["ln_x_g"], "ln_x_b": g["ln_x_b"],
        "w_o": feat(g["w_o"][0]), "w_merge": tok(g["w_merge"][0]),
        "w_fg": feat(g["w_ffn_gate"][0]), "w_fu": feat(g["w_ffn_up"][0]), "w_fd": tok(g["w_ffn_down"][0]),
        "w_tok2": tok(w2in[:, 0:1536]), "w_a": asc(w2in[:, 1536:1552].reshape(8, P, 16).transpose(1, 0, 2)),
        "w_cv": feat(w2in[:, 1552:]), "w_gate_up": g["w_gate_up_2"][0], "b_gate_2": g["b_gate_2"],
        "gla_norm_g_2": g["gla_norm_g_2"], "w_out": tok(g["w_out_2"][0]),
        "w_fg2": feat(g["w_ffn_gate_2"][0]), "w_fu2": feat(g["w_ffn_up_2"][0]), "w_fd2": tok(g["w_ffn_down_2"][0]),
        "norm_f": g["norm_f_g_2"].reshape(1, 1024),
    }
    nc = _bacc.Bacc("TRN2", target_bir_lowering=False, num_devices=1)
    arrays, a = {}, {}
    for n, v in ins.items():
        v = asc(v)
        arrays[f"in_{n}"] = v
        a[n] = nc.dram_tensor(f"in_{n}", v.shape, mybir.dt.from_np(v.dtype), kind="ExternalInput").ap()
    a["oa_d"] = nc.dram_tensor("oa_d", [512, 1024], F32, kind="Internal").ap()
    a["ob_d"] = None
    a["rw_d"] = nc.dram_tensor("rw_d", [8, 7, P, 512], F32, kind="Internal").ap()
    a["o_d"] = nc.dram_tensor("o_d", [2, 8, P, 512], F32, kind="Internal").ap()
    out = nc.dram_tensor("out_0", [1024, 1024], F32, kind="ExternalOutput").ap()
    program(nc, a, out)
    r = _run(nc, [arrays], core_ids=[0])
    return r.results[0]["out_0"].reshape(1, 1024, 1024)
```

```python
from contextlib import ExitStack
import math

import numpy as np

import concourse.bass as bass
from concourse import mybir

F32 = mybir.dt.float32
I32 = mybir.dt.int32
ACT = mybir.ActivationFunctionType
ALU = mybir.AluOpType
AX = mybir.AxisListType

P = 128
S = 1024
D = 1024
NT = S // P
FF = 2816
NF = FF // P
EPS = 1e-6
GN_EPS = 64e-5
EH = math.exp(-0.5)
SCALE = 1.0 / math.sqrt(96.0)

CONST = ["ident", "SU", "IU", "SL", "IL", "DU", "DL", "OU", "OL", "BD", "TCF", "TCB", "TRI", "REST"]
COLS = [("col", 2), ("invf", 16)]
PCOLS = [("g_mix", 8), ("g_qa", 2), ("g_kva", 1), ("mup", 16), ("mun", 16), ("bg", 16), ("g_ffn", 8),
         ("cw0", NF), ("cw1", NF), ("cw2", NF), ("cb", NF), ("g_n1", 8), ("g_n2", 8),
         ("gw0", 4), ("gw1", 4), ("gw2", 4)]


def const_table():
    i = np.arange(P)
    p, f = i[:, None], i[None, :]
    blk = (p // 16) == (f // 16)
    half = (p // 64) == (f // 64)
    mid_f = (p <= 63).astype(np.float32)
    mid_b = (p >= 64).astype(np.float32)
    m = {
        "ident": p == f, "SU": p < f, "SL": p > f, "IU": p <= f, "IL": p >= f,
        "DU": (p < f) & blk, "DL": (p > f) & blk, "OU": (p < f) & ~blk, "OL": (p > f) & ~blk,
        "BD": half,
        "TCF": (p <= f).astype(np.float32) - mid_f, "TCB": (p >= f).astype(np.float32) - mid_b,
        "TRI": (p <= f) & half, "REST": (p > f) & half,
    }
    parts = [np.broadcast_to(m[n], (P, P)).astype(np.float32) for n in CONST]
    parts.append(np.stack([(i <= 63), (i > 63)], 1).astype(np.float32))
    inv = 10000.0 ** (-np.arange(0, 32, 2, dtype=np.float64) / 32)
    parts.append(np.broadcast_to(inv.astype(np.float32), (P, 16)))
    return np.ascontiguousarray(np.concatenate(parts, 1))


class Eng:

    def __init__(self, sem):
        self.sem, self.n, self.q, self.seen = sem, 0, [], {}

    def wait(self, *toks):
        for t in toks:
            if t is None:
                continue
            if isinstance(t, list):
                self.wait(*t)
            elif self.seen.get(id(t[0]), 0) < t[1]:
                self.seen[id(t[0])] = t[1]
                self.q.append(lambda e, t=t: e.wait_ge(t[0], t[1]))

    def do(self, fn, *toks):
        self.wait(*toks)
        self.n += 1
        self.q.append(lambda e: fn(e).then_inc(self.sem, 1))
        return (self.sem, self.n)

    def quiet(self, fn, *toks):
        self.wait(*toks)
        self.q.append(lambda e: fn(e))

    def run(self, e):
        for f in self.q:
            f(e)


class Slot:

    def __init__(self, sem, ap=None):
        self.sem, self.n, self.ap, self.free = sem, 0, ap, None

    def dma(self, eng, out, in_, *toks):
        eng.wait(*toks)
        self.n += 16
        eng.q.append(lambda e: e.dma_start(out, in_).then_inc(self.sem, 16))
        return (self.sem, self.n)


def interleave(*gens):
    gens = list(gens)
    while gens:
        for g in list(gens):
            try:
                next(g)
            except StopIteration:
                gens.remove(g)


class K:
    pass


def program(nc, a, out):
    ctx = ExitStack()
    with ctx:
        nsem = [0]

        def sem(name):
            return ctx.enter_context(nc.semaphore(name))

        def sb(name, n):
            return ctx.enter_context(nc.sbuf_tensor(name, [P, n], F32))

        PE, VE, AE, GE, SP = [Eng(sem(f"s_{n}")) for n in ("pe", "ve", "ae", "ge", "sp")]

        def slot(ap=None):
            nsem[0] += 1
            return Slot(sem(f"d{nsem[0]}"), ap)

        X = sb("X", 8192)
        W = sb("W", 4096)
        W1 = sb("W1", 2052)
        NCST = len(CONST) * P + 18
        CS = sb("CS", NCST)
        NPC = sum(n for _, n in PCOLS)
        PC = sb("PC", NPC)
        SM = sb("SM", 1024)
        OTB = sb("OTB", 512)

        def region(st, name, n, dt=F32):
            return st.enter_context(nc.sbuf_tensor(name, [P, n], dt))

        room = ExitStack()
        HT = region(room, "HT_1", 8192)
        AR = region(room, "AR_1", 22528)
        EX = region(room, "EX_1", 4096)
        ps = ctx.enter_context(nc.psum_tensor("ps", [P, 8, 512], F32))

        cst = {n: CS[:, i * P:(i + 1) * P] for i, n in enumerate(CONST)}
        cst["col"] = CS[:, len(CONST) * P:len(CONST) * P + 2]
        cst["invf"] = CS[:, len(CONST) * P + 2:len(CONST) * P + 18]
        pc = {}
        at = 0
        for n, w in PCOLS:
            pc[n] = PC[:, at:at + w]
            at += w

        def v3(ap, k):
            return ap.rearrange("p (a b) -> p a b", a=k)

        def bc(ap, k):
            return ap.unsqueeze(1).broadcast_to([P, k, ap.shape[1]])

        def bl(ap, k):
            return ap.unsqueeze(2).broadcast_to([P, ap.shape[1], k])

        sc = slot()
        t_cst = sc.dma(SP, CS[:, :], a["cst"])
        t_cst = sc.dma(SP, PC[:, :], a["pcols"])
        ident = cst["ident"]

        bank_free = [None] * 8
        bank_at = [0]

        def acquire(n=1):
            if n == 2 and bank_at[0] % 2:
                bank_at[0] += 1
            b = bank_at[0] % 8
            bank_at[0] += n
            toks = [bank_free[b + i] for i in range(n)]
            return b, toks

        def release(b, tok, n=1):
            for i in range(n):
                bank_free[b + i] = tok

        ring = [slot(W[:, i * 1024:(i + 1) * 1024]) for i in range(4)]
        ring_at = [0]

        def load_w(src, n=1024):
            r = ring[ring_at[0] % 4]
            ring_at[0] += 1
            t = r.dma(SP, r.ap[:, 0:n], src, r.free)
            r.free = None
            return r, t

        def mm(o, l, r, start, stop, *toks, mark=False, lax=False):
            f = lambda e: e.matmul(o, l, r, start=start, stop=stop, **({"skip_group_check": True} if lax else {}))
            if mark:
                return PE.do(f, *toks)
            PE.quiet(f, *toks)

        def tr(o, i, *toks, mark=False):
            f = lambda e: e.transpose(o, i, ident)
            if mark:
                return PE.do(f, *toks)
            PE.quiet(f, *toks)

        def act(o, i, f, *toks, **kw):
            return AE.do(lambda e: e.activation(o, i, f, **kw), *toks)

        def tt(o, x, y, op, *toks, eng=None):
            return (eng or VE).do(lambda e: e.tensor_tensor(o, x, y, op), *toks)

        def ts(o, x, s1, s2, o1, o2, *toks, eng=None):
            if s2 is None:
                return (eng or VE).do(lambda e: e.tensor_scalar(o, x, s1, None, o1), *toks)
            return (eng or VE).do(lambda e: e.tensor_scalar(o, x, s1, s2, o1, o2), *toks)

        def stt(o, x, s, y, o1, o2, *toks):
            return VE.do(lambda e: e.scalar_tensor_tensor(out=o, in0=x, scalar=s, in1=y, op0=o1, op1=o2), *toks)

        def red(o, x, *toks, op=ALU.add):
            return VE.do(lambda e: e.tensor_reduce(o, x, AX.X, op), *toks)

        def recip(o, x, *toks):
            return VE.do(lambda e: e.reciprocal(o, x), *toks)

        def cp(eng, o, x, *toks):
            if eng is AE:
                return act(o, x, ACT.Copy, *toks)
            return eng.do(lambda e: e.tensor_copy(o, x), *toks)

        def memset(eng, o, v, *toks):
            return eng.do(lambda e: e.memset(o, v), *toks)

        def last(eng):
            return (eng.sem, eng.n) if eng.n else None

        def all_done():
            return [last(e) for e in (PE, VE, AE, GE)]

        def sm(at, n):
            return SM[:, at:at + n]

        def rstd(o, n, eps, *toks):
            t = ts(o, o, 1.0 / n, eps, ALU.mult, ALU.add, *toks)
            t = act(o, o, ACT.Sqrt, t)
            return recip(o, o, t)

        def norm_tile(t, gain, xs, ss, tok, xs_free, HT, lo):
            xt = X[:, t * D:(t + 1) * D]
            tq = act(xs, xt, ACT.Square, tok, xs_free, accum_out=ss)
            tq = rstd(ss, D, EPS, tq)
            tq = ts(xs, xt, ss, None, ALU.mult, None, tq)
            toks = []
            for h in range(2):
                b, fr = acquire()
                for j in range(4):
                    k = 4 * h + j
                    tp = tr(ps[:, b, j * P:(j + 1) * P], xs[:, k * P:(k + 1) * P], tq, fr, t_cst, mark=(j == 3))
                o = v3(HT, 8)[:, 4 * h:4 * h + 4, t * P:(t + 1) * P]
                gb = bl(gain[:, 4 * h:4 * h + 4], P)
                if lo is None:
                    te = tt(o, v3(ps[:, b, :], 4), gb, ALU.mult, tp)
                    release(b, te)
                    continue
                nt = v3(W1[:, 1024:1536], 4)
                te = tt(nt, v3(ps[:, b, :], 4), gb, ALU.mult, tp, nfree[0])
                release(b, te)
                th = act(o, nt, ACT.Copy, te)
                te = tt(v3(lo, 8)[:, 4 * h:4 * h + 4, t * P:(t + 1) * P], nt, o.bitcast(F32), ALU.subtract, th)
                nfree[0] = te
            return te, tp

        nfree = [None]

        def norm_all(gain, tok_of, tmp, free_ht, HT, lo=None):
            VE.wait(free_ht)
            AE.wait(free_ht)
            fr = [None] * len(tmp)
            for t in range(NT):
                s = t % len(tmp)
                te, fr[s] = norm_tile(t, gain, tmp[s], sm(t, 1), tok_of[t], fr[s], HT, lo)
                if t == 3:
                    half = te
            return (half, te)

        HT3 = v3(HT[:, :], 8)

        def feat(src, ncol, tok_h, HT3):
            r, tw = load_w(src)
            w3 = v3(r.ap, 8)
            res = []
            for h in range(2):
                b, fr = acquire()
                for k in range(8):
                    tk = mm(ps[0:ncol, b, :], w3[:, k, 0:ncol], HT3[:, k, h * 512:(h + 1) * 512],
                            k == 0, k == 7, tw, tok_h[h], fr, mark=(k == 7))
                res.append((b, tk))
            r.free = tk
            return res

        def tokmajor(src_of, A3, nk, ncols, tok_a, evac):
            for tg in range(2):
                for nh in range(ncols):
                    banks = [acquire() for _ in range(4)]
                    marks = [None] * 4
                    for s in range(nk // 2):
                        r, tw = load_w(src_of(nh, s))
                        w3 = v3(r.ap, 2)
                        for kk in range(2):
                            k = 2 * s + kk
                            for j in range(4):
                                t = tg * 4 + j
                                b, fr = banks[j]
                                lastk = k == nk - 1
                                tk = mm(ps[:, b, :], A3[:, k, t * P:(t + 1) * P], w3[:, kk, :], k == 0, lastk,
                                        tw, tok_a[tg], fr, mark=(lastk or (kk == 1 and j == 3)))
                                if lastk:
                                    marks[j] = tk
                        r.free = tk
                    for j in range(4):
                        release(banks[j][0], evac(tg * 4 + j, nh, ps[:, banks[j][0], :], marks[j]))

        xsl = [slot() for _ in range(NT)]
        t_x = [xsl[t].dma(SP, X[:, t * D:(t + 1) * D], a["x"][t * P:(t + 1) * P, :]) for t in range(NT)]

        A = 0
        MC = AR[:, 0:3328]
        CQT = AR[:, 3328:5376]
        CKT = AR[:, 5376:6400]
        WUQ = AR[:, 6400:7936]
        WUKV = AR[:, 7936:8960]
        Q = AR[:, 8960:15104]
        WM = AR[:, 15104:18432]
        tmpn = [AR[:, 18432:19456], AR[:, 19456:20480]]
        s_m = slot()
        t_wm = s_m.dma(SP, v3(WM, 8), a["w_mla"])
        t_wm = s_m.dma(SP, v3(WUQ, 2), a["w_uq"].rearrange("(k p) n -> p k n", p=P))
        t_wm = s_m.dma(SP, WUKV, a["w_ukv"])
        GB = AR[:, 20480:20480 + 192]
        t_wm = s_m.dma(SP, GB[:, 0:64], a["qn_norm_g"].partition_broadcast(P).rearrange("p a n -> p (a n)"))
        t_wm = s_m.dma(SP, GB[:, 64:96], a["qr_norm_g"].partition_broadcast(P).rearrange("p a n -> p (a n)"))
        t_wm = s_m.dma(SP, GB[:, 96:160], a["kn_norm_g"].partition_broadcast(P).rearrange("p a n -> p (a n)"))
        t_wm = s_m.dma(SP, GB[:, 160:192], a["kr_norm_g"].partition_broadcast(P).rearrange("p a n -> p (a n)"))
        POS = AR[:, 20672:20680].bitcast(I32)
        t_wm = s_m.dma(SP, POS, a["pos"])

        AE.wait(t_cst)
        VE.wait(t_cst)
        t_h = norm_all(pc["g_mix"], t_x, tmpn, None, HT[:, :])

        g_d = a["g_d"]
        gst = [slot(W1[:, 512 * i:512 * i + 512]) for i in range(4)]

        def gates_gen():
            i = 0
            for n in range(16):
                r, tw = load_w(a["w_g"][n])
                w3 = v3(r.ap, 8)
                for h in range(2):
                    b, fr = acquire()
                    for k in range(8):
                        tk = mm(ps[:, b, :], w3[:, k, :], HT3[:, k, h * 512:(h + 1) * 512], k == 0, k == 7, tw, t_h[h],
                                fr, mark=(k == 7))
                    r.free = tk
                    st_ = gst[i % 4]
                    te = act(st_.ap, ps[:, b, :], ACT.Sigmoid, tk, st_.free, bias=pc["bg"][:, n:n + 1])
                    release(b, te)
                    st_.free = st_.dma(GE, g_d[n, h], st_.ap, te, st_.free)
                    i += 1
                    yield

        gates = gates_gen()

        def run_gates(n):
            for _ in range(n):
                next(gates, None)

        MC3 = v3(MC, 8)
        WM3 = v3(WM, 8)
        for t in range(NT):
            b, fr = acquire()
            for k in range(8):
                tk = mm(ps[:, b, 0:416], HT3[:, k, t * P:(t + 1) * P], WM3[:, k, :], k == 0, k == 7, t_h[t // 4], t_wm, fr,
                        mark=(k == 7))
            te = cp(AE, MC3[:, t, :], ps[:, b, 0:416], tk)
            release(b, te)
        t_mc = te
        tk_m = tk
        run_gates(4)
        SQ = WM
        SQ3 = v3(SQ, 8)
        tq = tt(SQ, MC, MC, ALU.mult, t_mc, tk_m)
        ss = v3(sm(16, 24), 3)
        tq1 = red(ss[:, 0, :], SQ3[:, :, 0:256], tq)
        tq2 = red(ss[:, 1, :], SQ3[:, :, 256:384], tq)
        tq3 = red(ss[:, 2, :], SQ3[:, :, 384:416], tq)
        ts(ss[:, 0, :], ss[:, 0, :], 1.0 / 256, EPS, ALU.mult, ALU.add, tq1)
        ts(ss[:, 1, :], ss[:, 1, :], 1.0 / 128, EPS, ALU.mult, ALU.add, tq2)
        tq = ts(ss[:, 2, :], ss[:, 2, :], 1.0 / 32, EPS, ALU.mult, ALU.add, tq3)
        tq = act(sm(16, 24), sm(16, 24), ACT.Sqrt, tq)
        tq = recip(sm(16, 24), sm(16, 24), tq)
        tn = None
        for i, (lo, hi) in enumerate(((0, 256), (256, 384), (384, 416))):
            tn = tt(MC3[:, :, lo:hi], MC3[:, :, lo:hi], bl(ss[:, i, :], hi - lo), ALU.mult, tq)
        CQ3 = v3(CQT, 2)
        for t in range(NT):
            b, fr = acquire()
            for j in range(3):
                tk = tr(ps[:, b, j * P:(j + 1) * P], MC3[:, t, j * P:(j + 1) * P], tn, fr, mark=(j == 2))
            te = tt(CQ3[:, :, t * P:(t + 1) * P], v3(ps[:, b, 0:256], 2), bl(pc["g_qa"], P), ALU.mult, tk)
            te = ts(CKT[:, t * P:(t + 1) * P], ps[:, b, 256:384], pc["g_kva"], None, ALU.mult, None)
            release(b, te)
        t_cT = te

        POSF = sm(40, 8)
        ANG, COS, SIN, TMP = [AR[:, 20700 + 128 * i:20828 + 128 * i] for i in range(4)]
        tr0 = cp(VE, POSF, POS, t_wm)
        tr0 = tt(v3(ANG, 8), bl(POSF, 16), bc(cst["invf"], 8), ALU.mult, tr0)
        MAGIC = 12582912.0
        tr0 = ts(TMP, ANG, 1.0 / (2 * math.pi), MAGIC, ALU.mult, ALU.add, tr0)
        tr0 = ts(TMP, TMP, -MAGIC, None, ALU.add, None, tr0)
        C1 = 6.28125
        C2 = float(np.float32(int((2 * math.pi - C1) * 2 ** 20) / 2 ** 20))
        C3 = 2 * math.pi - C1 - C2
        for c in (C1, C2, C3):
            tr0 = stt(ANG, TMP, -c, ANG, ALU.mult, ALU.add, tr0)
        LIM = 3.1415925
        tr0 = ts(ANG, ANG, LIM, -LIM, ALU.min, ALU.max, tr0)
        tr1 = stt(TMP, ANG, -1.0, ANG, ALU.mult, ALU.max, tr0)
        tr1 = ts(TMP, TMP, -1.0, math.pi / 2, ALU.mult, ALU.add, tr1)
        act(SIN, ANG, ACT.Sin, tr0)
        t_rope = act(COS, TMP, ACT.Sin, tr1)

        Q4 = Q.rearrange("p (t h d) -> p t h d", t=8, h=8)
        Q3 = v3(Q, 8)
        KV3 = v3(X[:, :], 8)
        KV4 = X[:, :].rearrange("p (t h d) -> p t h d", t=8, h=8)
        WUQ3 = v3(WUQ, 2)
        for t in range(NT):
            for hh in range(2):
                b, fr = acquire()
                for k in range(2):
                    tk = mm(ps[:, b, 0:384], CQ3[:, k, t * P:(t + 1) * P], WUQ3[:, k, hh * 384:(hh + 1) * 384],
                            k == 0, k == 1, t_cT, fr, mark=(k == 1))
                te = cp(AE, Q3[:, t, hh * 384:(hh + 1) * 384], ps[:, b, 0:384], tk)
                release(b, te)
                b, fr = acquire()
                tk = mm(ps[:, b, :], CKT[:, t * P:(t + 1) * P], WUKV[:, hh * 512:(hh + 1) * 512], True, True, fr,
                        t_cT, mark=True)
                tv = cp(VE, KV3[:, t, hh * 512:(hh + 1) * 512], ps[:, b, :], tk, last(GE))
                release(b, tv)
        t_q, t_kv = te, tv
        s_v = slot()
        for h in range(8):
            t_vd = s_v.dma(GE, a["v_d"][h].rearrange("p (t n) -> p t n", t=8), KV4[:, :, h, 64:128], t_kv)
        run_gates(3)
        SQ = AR[:, 0:4096]
        SQn = SQ.rearrange("p (t h d) -> p t h d", t=8, h=8)
        ssq = [v3(sm(64 + 64 * i, 64), 8) for i in range(3)]
        KR = AR[:, 21300:21556]
        KR3 = v3(KR, 8)
        tkr = tt(KR3, MC3[:, :, 384:416], bc(GB[:, 160:192], 8), ALU.mult, tn, t_wm)
        PE_t = last(PE)
        g3 = lambda ap, o: ap.rearrange("p t h d -> p (t h) d")
        tq = tt(g3(SQn, 0), g3(Q4[:, :, :, 0:64], 0), g3(Q4[:, :, :, 0:64], 0), ALU.mult, t_q, t_kv, tkr, PE_t)
        tq = red(sm(64, 64), g3(SQn, 0), tq)
        SQr = SQ[:, 0:2048].rearrange("p (g d) -> p g d", d=32)
        tq = tt(SQr, g3(Q4[:, :, :, 64:96], 0), g3(Q4[:, :, :, 64:96], 0), ALU.mult, tq)
        tq = red(sm(128, 64), SQr, tq)
        tq = tt(g3(SQn, 0), g3(KV4[:, :, :, 0:64], 0), g3(KV4[:, :, :, 0:64], 0), ALU.mult, tq)
        tq = red(sm(192, 64), g3(SQn, 0), tq)
        ts(sm(64, 64), sm(64, 64), 1.0 / 64, EPS, ALU.mult, ALU.add, tq)
        ts(sm(128, 64), sm(128, 64), 1.0 / 32, EPS, ALU.mult, ALU.add, tq)
        tq = ts(sm(192, 64), sm(192, 64), 1.0 / 64, EPS, ALU.mult, ALU.add, tq)
        tq = act(sm(64, 192), sm(64, 192), ACT.Sqrt, tq)
        run_gates(5)
        tq = recip(sm(64, 192), sm(64, 192), tq)
        qn, qr, kn = g3(Q4[:, :, :, 0:64], 0), g3(Q4[:, :, :, 64:96], 0), g3(KV4[:, :, :, 0:64], 0)
        t1 = tt(qn, qn, bl(sm(64, 64), 64), ALU.mult, tq)
        t2 = tt(qr, qr, bl(sm(128, 64), 32), ALU.mult, tq)
        t3 = tt(kn, kn, bl(sm(192, 64), 64), ALU.mult, tq)
        t1 = tt(qn, qn, bc(GB[:, 0:64], 64), ALU.mult, t1)
        t2 = tt(qr, qr, bc(GB[:, 64:96], 64), ALU.mult, t2)
        t3 = tt(kn, kn, bc(GB[:, 96:160], 64), ALU.mult, t3)
        RA, RB, RC, RD = [AR[:, 1024 * i:1024 * (i + 1)] for i in range(4)]

        def rotate(a4, b4, shp, tok):
            c4, s4 = COS, SIN
            if shp == "q":
                c4 = v3(COS, 8).unsqueeze(2).broadcast_to([P, 8, 8, 16])
                s4 = v3(SIN, 8).unsqueeze(2).broadcast_to([P, 8, 8, 16])
                w = [r.rearrange("p (t h d) -> p t h d", t=8, h=8) for r in (RA, RB, RC, RD)]
            else:
                c4, s4 = v3(COS, 8), v3(SIN, 8)
                w = [v3(r[:, 0:128], 8) for r in (RA, RB, RC, RD)]
            m0 = tt(w[0], a4, c4, ALU.mult, tok, t_rope)
            m1 = tt(w[1], b4, s4, ALU.mult, tok)
            m2 = tt(w[2], b4, c4, ALU.mult, tok)
            m3 = tt(w[3], a4, s4, ALU.mult, tok)
            tt(a4, w[0], w[1], ALU.subtract, m3)
            return tt(b4, w[2], w[3], ALU.add, m3)

        tkr = rotate(KR3[:, :, 0:16], KR3[:, :, 16:32], "k", t3)
        t_qf = rotate(Q4[:, :, :, 64:80], Q4[:, :, :, 80:96], "q", tkr)

        QT = [AR[0:96, 15104 + 1024 * i:16128 + 1024 * i] for i in range(2)]
        KT = [AR[0:96, 17152 + 1024 * i:18176 + 1024 * i] for i in range(2)]
        K96 = [v3(AR[:, 19200 + 768 * i:19968 + 768 * i], 8) for i in range(2)]
        oa_d = a["oa_d"]
        start_att = [t_qf, last(PE)]
        k_free = [None, None]
        t_kr = [cp(VE, K96[i][:, :, 64:96], KR3, start_att) for i in range(2)]
        s_qt = [slot(), slot()]
        q_out = [None, None]
        for h in range(8):
            s_ = h % 2
            K3 = K96[s_]
            tc = [cp(GE, K3[:, :, 0:64], KV4[:, :, h, 0:64], start_att, k_free[s_]), t_kr[s_]]
            toks = []
            for (dst, src) in ((QT[s_], lambda t: Q4[:, t, h, :]), (KT[s_], lambda t: K3[:, t, :])):
                for g in range(2):
                    b, fr = acquire()
                    for j in range(4):
                        tk = tr(ps[0:96, b, j * P:(j + 1) * P], src(4 * g + j), tc, start_att, fr, mark=(j == 3))
                    te = cp(AE if g else VE, dst[:, g * 512:(g + 1) * 512], ps[0:96, b, :], tk, q_out[s_])
                    release(b, te)
                    toks.append(te)
            k_free[s_] = tk
            s_qt[s_].dma(SP, a["qk_d"][h, 0], QT[s_], toks)
            q_out[s_] = s_qt[s_].dma(SP, a["qk_d"][h, 1], KT[s_])
        t_mla = [t_vd] + q_out


        def attention(start):
            QT = [HT[0:96, 2048 * i:2048 * i + 1024] for i in range(2)]
            KT = [HT[0:96, 2048 * i + 1024:2048 * i + 2048] for i in range(2)]
            VH = [v3(HT[:, 4096 + 512 * i:4608 + 512 * i], 8) for i in range(2)]
            PB = [HT[:, 5120 + 1024 * i:6144 + 1024 * i] for i in range(2)]
            OP = HT[:, 7168:8192]
            PT = [W1[:, 1024 * i:1024 * (i + 1)] for i in range(2)]
            s_h = [slot(), slot()]
            h_tok, h_free = {}, [None, None]
            s_oa = slot()
            att = {}
            pb_free, pt_free = [None, None], [None, None]
            fr_o = {"op": None, "ot": None}

            def load(h):
                x = h % 2
                s_h[x].dma(SP, QT[x], a["qk_d"][h, 0], start, h_free[x])
                s_h[x].dma(SP, KT[x], a["qk_d"][h, 1])
                h_tok[h] = s_h[x].dma(SP, VH[x], a["v_d"][h].rearrange("p (t n) -> p t n", t=8))

            def a_scores(i):
                h, q = divmod(i, 8)
                b, fr = acquire(2)
                for j in range(2):
                    tk = mm(ps[:, b + j, :], QT[h % 2][:, q * P:(q + 1) * P], KT[h % 2][:, j * 512:(j + 1) * 512],
                            True, True, h_tok[h], fr, mark=(j == 1))
                m, nb, rs = sm(256 + i % 4, 1), sm(264 + i % 4, 1), sm(272 + i % 4, 1)
                src = ps[:, b:b + 2, :].rearrange("p a b -> p (a b)")
                tm = red(m, src, tk, op=ALU.max)
                tm = ts(nb, m, -SCALE, None, ALU.mult, None, tm)
                te = act(PB[i % 2], src, ACT.Exp, tm, pb_free[i % 2], bias=nb, scale=SCALE, accum_out=rs)
                release(b, te, 2)
                att[i] = te

            def a_transp(i):
                b, fr = acquire(2)
                for j in range(8):
                    tk = tr(ps[:, b + j // 4, (j % 4) * P:(j % 4 + 1) * P], PB[i % 2][:, j * P:(j + 1) * P],
                            att[i], fr, mark=(j in (3, 7)))
                    if j == 3:
                        tk0 = tk
                pb_free[i % 2] = tk
                t0 = cp(AE, PT[i % 2][:, 0:512], ps[:, b, :], tk0, pt_free[i % 2])
                t1 = cp(AE, PT[i % 2][:, 512:1024], ps[:, b + 1, :], tk, pt_free[i % 2])
                release(b, t0)
                release(b + 1, t1)
                att[i] = [att[i], t0, t1]

            def a_pv(i):
                h, q = divmod(i, 8)
                b, fr = acquire()
                for j in range(8):
                    tk = mm(ps[:, b, 0:64], PT[i % 2][:, j * P:(j + 1) * P], VH[h % 2][:, j, :], j == 0, j == 7,
                            att[i], fr, mark=(j == 7))
                pt_free[i % 2] = tk
                if q == 7:
                    h_free[h % 2] = tk
                rs = sm(272 + i % 4, 1)
                tq = recip(rs, rs, att[i])
                dst = v3(OP, 8)[:, q, (h % 2) * 64:(h % 2) * 64 + 64]
                te = ts(dst, ps[:, b, 0:64], rs, None, ALU.mult, None, tq, tk, fr_o["op"])
                release(b, te)
                if i % 16 == 15:
                    pr = h // 2
                    for g in range(2):
                        b, fr = acquire()
                        for j in range(4):
                            tk = tr(ps[:, b, j * P:(j + 1) * P], OP[:, (4 * g + j) * P:(4 * g + j + 1) * P], te, fr,
                                    mark=(j == 3))
                        tw = cp(VE, OTB[:, :], ps[:, b, :], tk, fr_o["ot"])
                        release(b, tw)
                        fr_o["ot"] = s_oa.dma(GE, oa_d[pr * P:(pr + 1) * P, 512 * g:512 * g + 512], OTB[:, :], tw)
                    fr_o["op"] = tk

            load(0)
            yield
            for i in range(64 + 2):
                if i % 8 == 2 and i // 8 + 1 < 8:
                    load(i // 8 + 1)
                if i < 64:
                    a_scores(i)
                    yield
                if 1 <= i <= 64:
                    a_transp(i - 1)
                    yield
                if i >= 2:
                    a_pv(i - 2)
                    yield
            t_att.append(fr_o["ot"])

        t_att = []

        done = all_done() + t_mla
        for e in (PE, VE, AE, GE):
            e.wait(done)
        U = AR[:, 0:12288]
        U3 = v3(U, 8)
        UL = [AR[:, 12288 + 1024 * i:13312 + 1024 * i] for i in range(4)]
        BCT = AR[:, 16384:19456]
        KKB, KAB, RKB, A0B, W0F, W0B = [BCT[:, 512 * i:512 * (i + 1)] for i in range(6)]
        LW = AR[:, 19456:20480]
        A2W, W2B = LW[:, 0:512], LW[:, 512:1024]
        s_b = slot()
        rows = [(KKB, a["k_k"][0:1, :]), (KAB, a["k_a"][0:1, :]), (RKB, a["r_k"][0:1, :]), (A0B, a["a0"][0:1, :]),
                (W0F, a["w0"][0:1, :]), (W0B, a["w0"][1:2, :])]
        for dst, src in rows:
            t_b = s_b.dma(SP, dst, src.partition_broadcast(P).rearrange("p a n -> p (a n)"), done)
        t_b = s_b.dma(SP, A2W[0:64, :], a["a2"])
        t_b = s_b.dma(SP, A2W[64:128, :], a["w2"][0:64, :])
        t_b = s_b.dma(SP, W2B[0:64, :], a["w2"][64:128, :])
        RAW = [X[:, 1100 * i:1100 * i + 1026] for i in range(2)]
        U1 = [X[:, 2200 + 1024 * i:3224 + 1024 * i] for i in range(2)]
        U2 = [X[:, 4300 + 1024 * i:5324 + 1024 * i] for i in range(2)]
        C0 = sm(280, 16)
        tc0 = tt(C0, pc["mup"], pc["mun"], ALU.add)
        tc0 = ts(C0, C0, -1.0, 1.0, ALU.mult, ALU.add, tc0)
        for i in range(2):
            memset(VE, RAW[i][:, 0:1], 0.0)
            tz = memset(VE, RAW[i][:, 1025:1026], 0.0)
        raw_free, u2_free = [None, None], [None, None]
        pend = []

        def fin_shift(ft, n, dst, tok):
            s = ft % 2
            for g in range(2):
                b, fr = acquire()
                for j in range(4):
                    tk = tr(ps[:, b, j * P:(j + 1) * P], U2[s][:, (4 * g + j) * P:(4 * g + j + 1) * P], tok, fr,
                            mark=(j == 3))
                te = cp(AE, U3[:, 4 * g:4 * g + 4, ft * P:(ft + 1) * P], v3(ps[:, b, :], 4), tk)
                release(b, te)
            u2_free[s] = tk

        for ft in range(16):
            n = 64 if ft == 13 else 128
            s = ft % 2
            res = feat(a["w_rw"][ft], n, t_h, HT3)
            for h, (b, tk) in enumerate(res):
                te = cp(AE, RAW[s][0:n, 1 + 512 * h:513 + 512 * h], ps[0:n, b, :], tk, raw_free[s])
                release(b, te)
            t1 = act(U1[s][0:n, :], RAW[s][0:n, 1:1025], ACT.Copy, te, tc0, raw_free[s], scale=C0[0:n, ft:ft + 1])
            t2 = stt(U1[s][0:n, :], RAW[s][0:n, 0:1024], pc["mup"][0:n, ft:ft + 1], U1[s][0:n, :], ALU.mult, ALU.add,
                     t1, tz)
            dst = U2[s] if ft < 12 else UL[ft - 12]
            t3 = stt(dst[0:n, :], RAW[s][0:n, 2:1026], pc["mun"][0:n, ft:ft + 1], U1[s][0:n, :], ALU.mult, ALU.add,
                     t2, u2_free[s] if ft < 12 else None)
            raw_free[s] = t3
            if pend:
                fin_shift(*pend.pop())
            if ft < 12:
                pend.append((ft, n, dst, t3))
            elif ft == 12:
                tl = act(dst[64:128, :], dst[64:128, :], ACT.Tanh, t3)
            elif ft == 13:
                tl = act(dst[0:64, :], dst[0:64, :], ACT.Tanh, t3)
            else:
                tl = act(dst, dst, ACT.Sigmoid, t3)
        t_ul = [tl, t3]
        t_u = te
        t_u = last(AE)

        names = ["r", "k2", "v", "kkn", "b", "sgf", "sgb"]
        rw_d = a["rw_d"]
        RN = sm(300, 64)
        RN3 = v3(RN, 8)
        BS = sm(364, 64)
        BS3 = v3(BS, 8)
        CT = sm(428, 128)
        CT3 = v3(CT, 8)
        KT0, KT1 = X[:, 0:512], X[:, 512:1024]
        VE.wait(t_u, t3, last(PE))
        VE.wait(t_b)
        for t in range(NT):
            tq = tt(KT0, U3[:, t, 512:1024], KKB, ALU.mult, last(VE))
            tq = tt(KT0, KT0, KT0, ALU.mult, tq)
            tq = red(RN3[:, t, :], v3(KT0, 8), tq)
        tq = act(RN, RN, ACT.Sqrt, tq)
        tq = ts(RN, RN, 1e-12, None, ALU.max, None, tq)
        tq = recip(RN, RN, tq)
        t_rn = ts(RN, RN, -1.0, None, ALU.mult, None, tq)
        wb = [[X[:, 1024 + 3584 * i + 512 * j:1536 + 3584 * i + 512 * j] for j in range(7)] for i in range(2)]
        s_st = [slot(), slot()]
        st_free = [None, None]
        st_all = {}
        for t in range(NT):
            s = t % 2
            aa, k2, kkn, bb, sgf, sgb, tm = wb[s]
            sl = slice(t * P, (t + 1) * P)
            fre = st_free[s]
            sig = []
            for (row, lh, wt, bias, dst) in ((0, UL[0][0:64, sl], A2W[0:64, :], A0B, aa),
                                             (64, UL[0][64:128, sl], A2W[64:128, :], W0F, sgf),
                                             (0, UL[1][0:64, sl], W2B[0:64, :], W0B, sgb)):
                b, fr = acquire()
                tk = mm(ps[:, b, :], lh, wt, True, True, t_ul, t_b, fr, mark=True)
                te = tt(dst, ps[:, b, :], bias, ALU.add, tk, fre)
                release(b, te)
                sig.append(act(dst, dst, ACT.Sigmoid, te))
            t_a, t_f, t_g = sig
            r_, k_, v_ = U3[:, t, 0:512], U3[:, t, 512:1024], U3[:, t, 1024:1536]
            t1 = tt(kkn, k_, KKB, ALU.mult, fre)
            t1 = tt(v3(kkn, 8), v3(kkn, 8), bl(RN3[:, t, :], 64), ALU.mult, t1, t_rn)
            t1 = stt(bb, kkn, -1.0, aa, ALU.mult, ALU.mult, t1, t_a)
            t2 = stt(tm, aa, -1.0, KAB, ALU.add, ALU.mult, t_a)
            t2 = stt(k2, tm, 1.0, k_, ALU.add, ALU.mult, t2)
            t3 = tt(tm, r_, RKB, ALU.mult, t2)
            t3 = tt(tm, tm, k2, ALU.mult, t3)
            t3 = red(BS3[:, t, :], v3(tm, 8), t3)
            b, fr = acquire()
            for d, (sg, tsg) in enumerate(((sgf, t_f), (sgb, t_g))):
                for p in range(4):
                    tk = mm(ps[:, b, d * 8 + 2 * p:d * 8 + 2 * p + 2], sg[:, p * P:(p + 1) * P], cst["col"], True, True,
                            tsg, fr, mark=(d == 1 and p == 3))
            te = cp(VE, CT3[:, t, :], ps[:, b, 0:16], tk)
            release(b, te)
            ss_ = s_st[s]
            for j, (src, tok) in enumerate(((r_, t_u), (k2, t2), (v_, t_u), (kkn, t1), (bb, t1), (sgf, t_f), (sgb, t_g))):
                tw = ss_.dma(GE, rw_d[t, j], src, tok, fre)
            st_free[s] = [tw, t3, tk]
            st_all[t] = tw
            run_gates(3 if t % 2 else 2)
        GG = sm(556, 64)
        G4 = GG.rearrange("p (d i q) -> p d i q", d=2, i=8)
        for d in range(2):
            for i in range(8):
                t = i if d == 0 else 7 - i
                o, r1 = G4[:, d, i, :], CT3[:, t, d * 8:d * 8 + 8].rearrange("p (q c) -> p q c", c=2)
                rest = r1[:, :, 1 - d]
                if i < 7:
                    nx = CT3[:, t + 1 - 2 * d, d * 8:d * 8 + 8].rearrange("p (q c) -> p q c", c=2)[:, :, d]
                    tg = tt(o, rest, nx, ALU.add, te)
                else:
                    tg = cp(VE, o, rest, te)
        t_g = act(GG, GG, ACT.Exp, tg, scale=-EH)

        run_gates(99)
        done = all_done() + list(st_all.values()) + [g.free for g in gst]
        for e in (PE, VE, AE, GE):
            e.wait(done)
        GS = [UL[2], UL[3]]
        spaces = [[AR[:, 0:14336], EX[:, 0:4096]], [X[:, 0:8192], AR[:, 16384:22528], W[:, 0:4096]]]

        def allocator(regions):
            left = [[r, 0] for r in regions]

            def take(n):
                for x in left:
                    if x[0].shape[1] - x[1] >= n:
                        o = x[0][:, x[1]:x[1] + n]
                        x[1] += n
                        return o
                raise RuntimeError("no room")
            return take

        o_d = a["o_d"]
        o_marks = [{}, {}]
        MU, VR = sm(620, 128), sm(748, 128)
        t_vr = {}

        def stream(d):
            take = allocator(spaces[d])
            M4 = take(2048).rearrange("p (h c n) -> p h c n", h=4, c=4)
            ART = take(1024).rearrange("p (q c n) -> p q c n", q=4, c=2)
            BT, KT = v3(take(1024), 8), v3(take(1024), 8)
            E = [take(512) for _ in range(3)]
            Rt, Kt, Bt = E[0], E[1], take(512)
            r_, k2, kkn, bb, sg = [take(512) for _ in range(5)]
            vb = [take(512) for _ in range(2)]
            Z0 = [take(512).rearrange("p (c h n) -> p c h n", c=2, h=4) for _ in range(2)]
            An, Dn, DT = [v3(take(512), 4) for _ in range(3)]
            D2, D2T, D4, D4T, D8 = [v3(take(512), 4) for _ in range(5)]
            Fn, FT, F2, F2T, F4T = D2, D2T, D4, D4T, D8
            XA, XB = [v3(take(512), 4) for _ in range(2)]
            zv = lambda z: z.rearrange("p h n -> p (h n)").rearrange("p (c h n) -> p c h n", c=2, h=4)
            ZA, ZB = zv(Dn), zv(DT)
            QT_, PT_ = v3(take(256), 2), v3(take(256), 2)
            SS = v3(take(512), 4)
            OB = take(512)
            s_ld, s_o = slot(), slot()
            s_v = [slot(), slot()]
            v_free = [None, None]
            TC = cst["TCF"] if d == 0 else cst["TCB"]
            sT, iT, sN = ("SU", "IU", "SL") if d == 0 else ("SL", "IL", "SU")
            at2 = CONST.index(sT) * P
            mask2 = CS[:, at2:at2 + 256]
            dN, dT, oN, oT = ("DL", "DU", "OL", "OU") if d == 0 else ("DU", "DL", "OU", "OL")
            t_s = [memset(GE, SS, 0.0)] * 4
            o_free = e2_free = None
            b4 = lambda n: bc(cst[n], 4)
            for z in (BT, KT):
                memset(GE, z, 0.0)
            t_zero = last(GE)

            def batch(lhs, rhs, *toks):
                b, fr = acquire()
                for h in range(4):
                    tk = mm(ps[:, b, h * P:(h + 1) * P], lhs[:, h, :], rhs[:, h, :], True, True, fr, *toks,
                            mark=(h == 3))
                return b, v3(ps[:, b, :], 4), tk

            def apply(lhs, z, *toks):
                b, fr = acquire()
                pv = ps[:, b, :].rearrange("p (c h n) -> p c h n", c=2, h=4)
                for h in range(4):
                    tk = mm(pv[:, :, h, :], lhs[:, h, :], z[:, :, h, :], True, True, fr, *toks, mark=(h == 3))
                return b, pv, tk

            def load(i, free):
                t = i if d == 0 else 7 - i
                for dst, jj in ((sg, 5 + d), (r_, 0), (k2, 1), (kkn, 3), (bb, 4)):
                    t1 = s_ld.dma(SP, dst, rw_d[t, jj], free)
                return t1, s_v[i % 2].dma(SP, vb[i % 2], rw_d[t, 2], v_free[i % 2])

            for i in range(8):
                t = i if d == 0 else 7 - i
                v_ = vb[i % 2]
                if i == 0:
                    t_ld, t_v = load(0, done)
                b, fr = acquire()
                tk = mm(ps[:, b, :], TC, sg, True, True, t_ld, fr, mark=True)
                te = tt(E[2], ps[:, b, :], sg, ALU.subtract, tk, e2_free)
                t0 = act(E[0], ps[:, b, :], ACT.Exp, te, scale=-EH)
                t1 = act(E[1], ps[:, b, :], ACT.Exp, te, scale=EH)
                t2 = act(E[2], E[2], ACT.Exp, te, scale=-EH)
                release(b, t1)
                yield
                for u in range(2):
                    c = slice(256 * u, 256 * u + 256)
                    t_A = tt(Z0[u][:, 0, :, :], v3(kkn[:, c], 4), v3(E[2][:, c], 4), ALU.mult, t2, t_ld)
                t_B = tt(Bt, bb, E[1], ALU.mult, t1, t_ld, eng=GE)
                pt = [t_A, tt(Rt, r_, E[0], ALU.mult, t0, t_ld), t_B,
                      tt(Kt, k2, E[1], ALU.mult, t_B, eng=GE)]
                tT = []
                az = lambda p: Z0[p // 2][:, 0, 2 * (p % 2):2 * (p % 2) + 2, :].rearrange("p h n -> p (h n)")
                for n, (src, dst) in enumerate(((None, ART[:, :, 0, :]), (Rt, ART[:, :, 1, :]), (Bt, BT), (Kt, KT))):
                    b, fr = acquire()
                    for p in range(4):
                        tk = tr(ps[:, b, p * P:(p + 1) * P], src[:, p * P:(p + 1) * P] if n else az(p), pt[n], fr,
                                mark=(p == 3))
                    if n < 2:
                        te = cp(AE if n else VE, dst, v3(ps[:, b, :], 4), tk)
                    else:
                        eng = AE if n == 3 else VE
                        cp(eng, dst[0:64, 0::2, :], v3(ps[0:64, b, :], 4), tk, t_zero)
                        te = cp(eng, dst[64:128, 1::2, :], v3(ps[64:128, b, :], 4))
                    release(b, te)
                    tT.append(te)
                t_vi = t_v
                if i < 7:
                    t_ld, t_v = load(i + 1, tT + pt)
                yield
                for u in range(2):
                    tM = []
                    for h in range(4):
                        p = 2 * u + h // 2
                        b, fr = acquire()
                        rr = ART[:, p, :, :].rearrange("k c n -> k (c n)")
                        mm(ps[:, b, 0:256], BT[:, 4 * u + h, :], rr, True, True, tT, fr)
                        tk = mm(ps[:, b, 256:512], KT[:, 4 * u + h, :], rr, True, True, mark=True)
                        ta = tt(M4[:, h, :, :].rearrange("p (a c) n -> p a (c n)", a=2), v3(ps[:, b, :], 2),
                                bc(mask2, 2), ALU.mult, tk)
                        release(b, ta)
                        tM.append(ta)
                    b, fr = acquire()
                    for q in range(2):
                        h = 4 * u + 2 * q
                        tk = mm(ps[:, b, 256 * q:256 * q + 256], ART[:, 2 * u + q, 0, :],
                                BT[:, h:h + 2, :].rearrange("p h n -> p (h n)"), True, True, fr, mark=(q == 1))
                    tA = tt(An, v3(ps[:, b, :], 4), b4(sN), ALU.mult, tk)
                    release(b, tA)
                    yield
                    b, fr = acquire()
                    for h in range(4):
                        c = (4 * u + h) * 64
                        tk = mm(ps[:, b, h * 64:(h + 1) * 64], M4[:, h, 2, :], v_[:, c:c + 64], True, True, tM, fr,
                                t_vi, mark=(h == 3))
                    tAV = cp(AE, Z0[u][:, 1, :, :], v3(ps[:, b, 0:256], 4), tk)
                    release(b, tAV)
                    tDT = tt(DT, M4[:, :, 0, :], b4(dT), ALU.mult, tM)
                    tDn = tt(Dn, An, b4(dN), ALU.mult, tA)
                    tX = tt(XA, DT, b4("ident"), ALU.add, tDT, tA, eng=GE)
                    b, pv, tk = batch(DT, Dn, tDT, tDn)
                    t2 = cp(AE, D2, pv, tk)
                    release(b, t2)
                    b, pv, tk = batch(Dn, DT, tDT, tDn)
                    t2T = cp(VE, D2T, pv, tk)
                    release(b, t2T)
                    yield
                    b, pv, tk = batch(D2T, D2, t2, t2T)
                    t4 = cp(AE, D4, pv, tk)
                    release(b, t4)
                    b, pv, tk = batch(D2, D2T, t2, t2T)
                    t4T = cp(AE, D4T, pv, tk)
                    release(b, t4T)
                    b, pv, tk = batch(D2, XA, tX)
                    tX2 = tt(XB, pv, XA, ALU.add, tk)
                    release(b, tX2)
                    yield
                    b, pv, tk = batch(D4T, D4, t4, t4T)
                    t8 = cp(AE, D8, pv, tk)
                    release(b, t8)
                    b, pv, tk = batch(D4, XB, t4, tX2)
                    tX3 = tt(XA, pv, XB, ALU.add, tk)
                    release(b, tX3)
                    yield
                    b, pv, tk = batch(D8, XA, t8, tX3)
                    tX4 = tt(XB, pv, XA, ALU.add, tk)
                    release(b, tX4)
                    yield
                    b, pv, tk = batch(XB, An, tX4, tA)
                    tF = tt(Fn, pv, b4(oN), ALU.mult, tk)
                    release(b, tF)
                    b, pv, tk = batch(An, XB, tX4, tA)
                    tFT = tt(FT, pv, b4(oT), ALU.mult, tk)
                    release(b, tFT)
                    b, pv, tk = apply(XB, Z0[u], tX4, tAV, t_A)
                    tZ = cp(AE, ZA, pv, tk)
                    release(b, tZ)
                    yield
                    b, pv, tk = batch(FT, Fn, tF, tFT)
                    tF2 = cp(AE, F2, pv, tk)
                    release(b, tF2)
                    b, pv, tk = batch(Fn, FT, tF, tFT)
                    tF2T = cp(VE, F2T, pv, tk)
                    release(b, tF2T)
                    b, pv, tk = apply(FT, ZA, tZ)
                    tZ2 = tt(ZB, pv, ZA, ALU.add, tk)
                    release(b, tZ2)
                    yield
                    b, pv, tk = batch(F2, F2T, tF2, tF2T)
                    tF4T = cp(AE, F4T, pv, tk)
                    release(b, tF4T)
                    b, pv, tk = apply(F2T, ZB, tZ2)
                    tZ3 = tt(ZA, pv, ZB, ALU.add, tk)
                    release(b, tZ3)
                    yield
                    b, pv, tk = apply(F4T, ZA, tF4T, tZ3)
                    tZ4 = tt(ZB, pv, ZA, ALU.add, tk)
                    release(b, tZ4)
                    yield
                    b, fr = acquire()
                    for h in range(4):
                        lo = 64 * (h % 2)
                        tk = mm(ps[lo:lo + 64, b, (h // 2) * P:(h // 2 + 1) * P], ZB[:, 0, h, :], M4[:, h, 1, :],
                                True, True, tZ4, fr, mark=(h == 3))
                    tQ = tt(QT_, v3(ps[:, b, 0:256], 2), ART[:, 2 * u:2 * u + 2, 1, :], ALU.add, tk)
                    release(b, tQ)
                    b, fr = acquire()
                    for q in range(2):
                        p = 2 * u + q
                        tk = mm(ps[:, b, q * P:(q + 1) * P], ZB[:, 0, 2 * q:2 * q + 2, :].rearrange("p h n -> p (h n)"), Bt[:, p * P:(p + 1) * P],
                                True, True, fr, mark=(q == 1))
                    tP = tt(PT_, v3(ps[:, b, 0:256], 2), bc(cst["BD"], 2), ALU.mult, tk)
                    release(b, tP)
                    tP = tt(PT_, PT_, bc(ident, 2), ALU.add, tP, eng=GE)
                    yield
                    b, fr = acquire()
                    for q in range(2):
                        p = 2 * u + q
                        mm(ps[:, b, q * P:(q + 1) * P], QT_[:, q, :], SS[:, p, :], True, False, tQ, t_s[p], fr, lax=True)
                        for hh in range(2):
                            h = 2 * q + hh
                            c = (4 * u + h) * 64
                            o = ps[:, b, h * 64:(h + 1) * 64]
                            mm(o, M4[:, h, 1, :], ZB[:, 1, h, :], False, False, lax=True)
                            tk = mm(o, M4[:, h, 3, :], v_[:, c:c + 64], False, hh == 1, lax=True, mark=(h == 3))
                    tO = cp(AE, OB[:, u * 256:(u + 1) * 256], ps[:, b, 0:256], tk, o_free)
                    release(b, tO)
                    b, fr = acquire()
                    for q in range(2):
                        p = 2 * u + q
                        o = ps[:, b, q * P:(q + 1) * P]
                        mm(o, PT_[:, q, :], SS[:, p, :], True, False, tP, fr)
                        mm(o, Bt[:, p * P:(p + 1) * P], ZB[:, 1, 2 * q:2 * q + 2, :], False, False)
                        tk = mm(o, Kt[:, p * P:(p + 1) * P], v_[:, p * P:(p + 1) * P], False, True, mark=(q == 1))
                    for q in range(2):
                        p = 2 * u + q
                        t_s[p] = stt(SS[:, p, :], ps[:, b, q * P:(q + 1) * P], G4[:, d, i, p:p + 1], cst["BD"],
                                     ALU.mult, ALU.mult, tk)
                    release(b, t_s[p])
                    yield
                v_free[i % 2] = last(PE)
                mu, vr = [q[:, d * 64 + t * 8:d * 64 + t * 8 + 8] for q in (MU, VR)]
                o3, e3 = v3(OB, 8), v3(E[2], 8)
                t1 = red(mu, o3, tO)
                t1 = ts(mu, mu, 1.0 / 64, None, ALU.mult, None, t1)
                tO = tt(o3, o3, bl(mu, 64), ALU.subtract, t1)
                t1 = tt(e3, o3, o3, ALU.mult, tO, eng=GE)
                e2_free = t_vr[d, t] = red(vr, e3, t1)
                o_marks[d][t] = s_o.dma(GE, o_d[d, t], OB, tO)
                o_free = [o_marks[d][t], t1]

        s0, s1, at_ = stream(0), stream(1), attention(done)
        for _ in range(7):
            next(s0)
            next(at_)
        interleave(s0, s1, at_)
        t_oa = t_att

        done = all_done() + [o_marks[0][7], o_marks[1][0]]
        for e in (PE, VE, AE, GE):
            e.wait(done)
        OF = [X[:, 0:4096], X[:, 4096:8192]]
        VV = AR[:, 0:4096]
        LG, LB_ = AR[:, 4096:4608], AR[:, 4608:5120]
        G2 = [AR[:, 5120:5632], AR[:, 5632:6144]]
        s_of = slot()
        for d in range(2):
            t_of = s_of.dma(SP, v3(OF[d], 8), o_d[d].rearrange("t p n -> p t n"), done)
        t_of = s_of.dma(SP, v3(VV, 8), rw_d[:, 2].rearrange("t p n -> p t n"))
        t_of = s_of.dma(SP, LG, a["ln_x_g"].partition_broadcast(P).rearrange("p a n -> p (a n)"))
        t_of = s_of.dma(SP, LB_, a["ln_x_b"].partition_broadcast(P).rearrange("p a n -> p (a n)"))
        t_of = s_of.dma(SP, G2[0], a["g2"][0:128, :])
        t_of = s_of.dma(SP, G2[1], a["g2"][128:256, :])
        SQT = AR[:, 6144:10240]
        tv = ts(VR, VR, 1.0 / 64, GN_EPS, ALU.mult, ALU.add, list(t_vr.values()))
        tv = act(VR, VR, ACT.Sqrt, tv)
        tv = recip(VR, VR, tv)
        OBT = AR[:, 10240:14336]
        OBT3 = v3(OBT, 4)
        OAT3 = v3(HT[:, 0:4096], 4)
        s_r = slot()
        t_oat = s_r.dma(SP, OAT3, oa_d.rearrange("(k p) n -> p k n", p=P), t_oa)
        GT = [slot(HT[:, 4096 + 512 * i:4608 + 512 * i]) for i in range(8)]

        class Mix:

            def __getitem__(self, key):
                p, k, n = key
                o = (AR[:, 16384 + 1024 * k:17408 + 1024 * k] if k < 6 else EX[:, 1024 * (k - 6):1024 * (k - 5)])
                return o[p, n]

        MIX3 = Mix()
        gi = [0]

        def gate_load(n, h):
            g = GT[gi[0] % 8]
            gi[0] += 1
            return g, g.dma(SP, g.ap, g_d[n, h], g.free)

        def out_a():
            for n in range(8):
                r, tw = load_w(a["w_o"][n][:, 0:512], 512)
                w3 = v3(r.ap[:, 0:512], 4)
                for h in range(2):
                    hs = slice(512 * h, 512 * h + 512)
                    g, tg = gate_load(n, h)
                    b, fr = acquire()
                    for k in range(4):
                        tk = mm(ps[:, b, :], w3[:, k, :], OAT3[:, k, hs], k == 0, k == 3, tw, t_oat, fr, mark=(k == 3))
                    r.free = tk
                    te = tt(MIX3[:, n, hs], g.ap, ps[:, b, :], ALU.mult, tk, tg)
                    g.free = te
                    release(b, te)
                    mix_tok[n, h] = te
                    yield

        mix_tok = {}

        def group_norm():
            tb_free = [None, None]
            for t in range(NT):
                bon = SQT[:, 0:512]
                acc = SQT[:, 512 + 512 * (t % 2):1024 + 512 * (t % 2)]
                tb = tt(v3(bon, 8), v3(VV[:, t * 512:(t + 1) * 512], 8), bl(BS3[:, t, :], 64), ALU.mult, last(VE),
                        eng=GE)
                tb = tt(bon, bon, LB_, ALU.add, tb, eng=GE)
                for d in range(2):
                    b, fr = acquire()
                    tk = mm(ps[:, b, :], GS[d][:, t * P:(t + 1) * P], G2[d], True, True, t_of, fr, mark=True)
                    ot = OF[d][:, t * 512:(t + 1) * 512]
                    v = VR[:, d * 64 + t * 8:d * 64 + t * 8 + 8]
                    t1 = tt(v3(ot, 8), v3(ot, 8), bl(v, 64), ALU.mult, tv, t_of)
                    t1 = tt(ot, ot, LG, ALU.mult, t1)
                    t1 = tt(ot, ot, bon, ALU.add, t1, tb)
                    t1 = tt(acc if d == 0 else ot, ot, ps[:, b, :], ALU.mult, tk, t1, tb_free[t % 2])
                    release(b, t1)
                t1 = tt(acc, acc, OF[1][:, t * 512:(t + 1) * 512], ALU.add, t1)
                yield
                b, fr = acquire()
                for p in range(4):
                    tk = tr(ps[:, b, p * P:(p + 1) * P], acc[:, p * P:(p + 1) * P], t1, fr, mark=(p == 3))
                tb_free[t % 2] = tk
                te = cp(AE, OBT3[:, :, t * P:(t + 1) * P], v3(ps[:, b, :], 4), tk)
                release(b, te)
            t_obs.append(te)

        t_obs = []
        oa_pass = out_a()
        for _ in range(4):
            next(oa_pass)
        interleave(oa_pass, group_norm())
        t_ob = t_obs[0]

        t_xr = [xsl[t].dma(SP, X[:, t * D:(t + 1) * D], a["x"][t * P:(t + 1) * P, :], last(VE), last(AE)) for t in range(NT)]
        TY = [AR[:, 512 * i:512 * i + 512] for i in range(2)]
        VE.wait(t_ob, last(PE), last(GE))
        for n in range(8):
            r, tw = load_w(a["w_o"][n][:, 512:1024], 512)
            w3 = v3(r.ap[:, 0:512], 4)
            for h in range(2):
                hs = slice(512 * h, 512 * h + 512)
                g, tg = gate_load(8 + n, h)
                b, fr = acquire()
                for k in range(4):
                    tk = mm(ps[:, b, :], w3[:, k, :], OBT3[:, k, hs], k == 0, k == 3, tw, t_ob, fr, mark=(k == 3))
                r.free = tk
                te = tt(TY[h], g.ap, ps[:, b, :], ALU.mult, tk, tg, mix_tok[n, h])
                release(b, te)
                g.free = te
                tm = tt(MIX3[:, n, hs], MIX3[:, n, hs], TY[h], ALU.add, te)
                mix_tok[n, h] = tm
        t_x1 = {}

        def add_x(t, nh, b, tk):
            xt = X[:, t * D + nh * 512:t * D + nh * 512 + 512]
            te = tt(xt, xt, b, ALU.add, tk, t_xr[t])
            t_x1[t] = te
            return te

        tokmajor(lambda nh, s: a["w_merge"][nh, s], MIX3, 8, 2, (tm, tm), add_x)

        def ffn(no, gain, wg, wu, wd, conv):
            st = ExitStack()
            FR = mybir.dt.float32r
            HH = region(st, f"HH_{no}", 8192, FR)[:, :]
            HL = region(st, f"HL_{no}", 8192, FR)[:, :]
            HAB = region(st, f"HA_{no}", 12 * 1024)
            WS = region(st, f"WS_{no}", 4096, FR)
            SA = region(st, f"SA_{no}", 2048, FR)
            tok_h = norm_all(gain, t_x1, [W1[:, 0:1024]], [last(PE), last(VE), last(AE), last(GE)], HH, HL)
            HH3, HL3 = v3(HH, 8), v3(HL, 8)
            HA = HAB[:, :].rearrange("p (f n) -> p f n", f=12)

            split_at = [0]
            split_free = [None, None]

            def split(src):
                r, tw = load_w(src)
                s = split_at[0] % 2
                split_at[0] += 1
                hi, lo = WS[:, s * 2048:s * 2048 + 1024], WS[:, s * 2048 + 1024:s * 2048 + 2048]
                t1 = act(hi, r.ap, ACT.Copy, tw, split_free[s])
                t2 = tt(lo, r.ap, hi.bitcast(F32), ALU.subtract, t1)
                r.free = t2
                return s, hi, lo, t2

            ahead = []
            todo = []

            def split_ahead():
                if todo:
                    ahead.append(split(todo.pop(0)))

            def next_split():
                if not ahead:
                    split_ahead()
                return ahead.pop(0)

            def three(o, ah, al, bh, bl_, first, lst, *toks):
                mm(o, ah, bl_, first, False, *toks)
                mm(o, al, bh, False, False)
                return mm(o, ah, bh, False, lst, mark=lst)

            def featr():
                s, wh, wl, tw = next_split()
                split_ahead()
                wh, wl = v3(wh, 8), v3(wl, 8)
                res = []
                for h in range(2):
                    hs = slice(h * 512, h * 512 + 512)
                    b, fr = acquire()
                    for k in range(8):
                        tk = three(ps[:, b, :], wh[:, k, :], wl[:, k, :], HH3[:, k, hs], HL3[:, k, hs], k == 0, k == 7,
                                   tw, tok_h[h], fr)
                    res.append((b, tk))
                split_free[s] = tk
                return res

            def down(f0, nf, tok_a):
                sa_free = [None, None]
                for tg in range(2):
                    for nh in range(2):
                        banks = [acquire() for _ in range(4)]
                        marks = [None] * 4
                        for q in range(nf // 2):
                            s, wh, wl, tw = next_split()
                            wh, wl = v3(wh, 2), v3(wl, 2)
                            parts = []
                            for x in range(2):
                                src = HA[:, 2 * q + x, tg * 512:tg * 512 + 512]
                                ah, al = SA[:, x * 1024:x * 1024 + 512], SA[:, x * 1024 + 512:x * 1024 + 1024]
                                t1 = act(ah, src, ACT.Copy, tok_a, sa_free[x])
                                t1 = tt(al, src, ah.bitcast(F32), ALU.subtract, t1)
                                parts.append((ah, al, t1))
                            split_ahead()
                            for kk in range(2):
                                k = 2 * q + kk
                                ah, al, t1 = parts[kk]
                                for j in range(4):
                                    b, fr = banks[j]
                                    lk = k == nf - 1
                                    o = ps[:, b, :]
                                    js = slice(j * P, (j + 1) * P)
                                    mm(o, ah[:, js], wl[:, kk, :], k == 0, False, t1, tw, fr)
                                    mm(o, al[:, js], wh[:, kk, :], False, False)
                                    m = mm(o, ah[:, js], wh[:, kk, :], False, lk, mark=(lk or j == 3))
                                    if lk:
                                        marks[j] = m
                                sa_free[kk] = m
                            split_free[s] = m
                        for j in range(4):
                            t = tg * 4 + j
                            xt = X[:, t * D + nh * 512:t * D + nh * 512 + 512]
                            te = tt(xt, xt, ps[:, banks[j][0], :], ALU.add, marks[j])
                            t_x1[t] = te
                            release(banks[j][0], te)

            for f0, nf in ((0, 12), (12, 10)):
                for f in range(f0, f0 + nf):
                    todo += [wg[f], wu[f]]
                todo += [wd[nh, f0 // 2 + q] for tg in range(2) for nh in range(2) for q in range(nf // 2)]
            rawf = [W1[:, 0:1026], W1[:, 1026:2052]]
            AE.wait(last(VE), last(PE))
            fr_raw = [None, None]
            fr_s = [None, None]
            if conv:
                for i in range(2):
                    memset(VE, rawf[i][:, 0:1], 0.0, last(PE), last(AE), last(VE))
                    tz = memset(VE, rawf[i][:, 1025:1026], 0.0)
            ha_free = None
            for f in range(NF):
                s = f % 2
                gb = featr()
                ub = featr()
                dst = HA[:, f % 12, :]
                if f == 12:
                    VE.wait(ha_free)
                if conv:
                    for h, (b, tk) in enumerate(gb):
                        te = cp(AE, rawf[s][:, 1 + 512 * h:513 + 512 * h], ps[:, b, :], tk, fr_raw[s])
                        release(b, te)
                    t1 = ts(dst, rawf[s][:, 1:1025], pc["cw1"][:, f:f + 1], pc["cb"][:, f:f + 1], ALU.mult, ALU.add, te)
                    t1 = stt(dst, rawf[s][:, 0:1024], pc["cw0"][:, f:f + 1], dst, ALU.mult, ALU.add, t1)
                    t1 = stt(dst, rawf[s][:, 2:1026], pc["cw2"][:, f:f + 1], dst, ALU.mult, ALU.add, t1)
                    fr_raw[s] = t1
                    sg = act(rawf[s][:, 1:1025], dst, ACT.Sigmoid, t1)
                    t1 = tt(dst, dst, rawf[s][:, 1:1025], ALU.mult, sg)
                    fr_raw[s] = t1
                    for h, (b, tk) in enumerate(ub):
                        te = tt(dst[:, 512 * h:512 * h + 512], dst[:, 512 * h:512 * h + 512], ps[:, b, :], ALU.mult, tk, t1)
                        release(b, te)
                else:
                    for h, (b, tk) in enumerate(gb):
                        hs = slice(512 * h, 512 * h + 512)
                        sg = act(rawf[s][:, hs], ps[:, b, :], ACT.Sigmoid, tk, fr_raw[s])
                        t1 = tt(dst[:, hs], rawf[s][:, hs], ps[:, b, :], ALU.mult, sg)
                        release(b, t1)
                        b2, tk2 = ub[h]
                        te = tt(dst[:, hs], dst[:, hs], ps[:, b2, :], ALU.mult, tk2, t1)
                        release(b2, te)
                    fr_raw[s] = te
                if f == 11:
                    down(0, 12, te)
                    ha_free = [last(PE), last(VE), last(AE)]
            down(12, 10, te)
            st.close()

        room.close()
        ffn(1, pc["g_ffn"], a["w_fg"], a["w_fu"], a["w_fd"], True)

        room = ExitStack()
        HT = region(room, "HT_2", 8192)
        AR = region(room, "AR_2", 22528)
        EX = region(room, "EX_2", 1024)
        HT3 = v3(HT[:, :], 8)
        tmpx = [W1[:, 0:1024], W1[:, 1024:2048]]
        t_h = norm_all(pc["g_n1"], t_x1, tmpx, [last(PE), last(VE), last(AE)], HT[:, :])
        QK = AR[:, 0:4096]
        V2 = AR[:, 4096:8192]
        GP = AR[:, 8192:12288]
        OG = AR[:, 12288:16384]
        OC = AR[:, 16384:20480]
        ZL = AR[:, 20480:22528]
        QK3, V23, GP3, OG3, OC3, ZL3 = [v3(r, k) for r, k in ((QK, 8), (V2, 8), (GP, 8), (OG, 8), (OC, 4), (ZL, 8))]
        WAG = EX[:, 0:640]
        s_g = slot()
        t_wg = s_g.dma(SP, v3(WAG[:, 0:128], 8), a["w_a"], all_done())
        t_wg = s_g.dma(SP, WAG[0:16, 128:384], a["w_gate_up"])
        t_wg = s_g.dma(SP, WAG[:, 384:640], a["b_gate_2"].partition_broadcast(P).rearrange("p a n -> p (a n)"))
        tv2 = [None]
        pre = last(PE)

        def ev2(t, nh, b, tk):
            dst = (QK3, V23, GP3)[nh][:, t, :]
            tv2[0] = cp(AE, dst, b, tk, pre)
            return tv2[0]
        tokmajor(lambda nh, s: a["w_tok2"][nh, s], HT3, 8, 3, t_h, ev2)
        t_qkv = tv2[0]
        PA = OG
        WA3 = v3(WAG[:, 0:128], 8)
        for h in range(2):
            b, fr = acquire()
            for k in range(8):
                tk = mm(ps[0:16, b, :], WA3[:, k, :], HT3[:, k, 512 * h:512 * h + 512], k == 0, k == 7, t_wg, t_h[h], fr,
                        mark=(k == 7))
            te = cp(VE, PA[0:16, 512 * h:512 * h + 512], ps[0:16, b, :], tk, pre)
            release(b, te)
        t_pa = te
        for t in range(NT):
            b, fr = acquire()
            tk = mm(ps[:, b, 0:256], PA[0:16, t * P:(t + 1) * P], WAG[0:16, 128:384], True, True, t_pa, fr, mark=True)
            te = tt(ZL3[:, t, :], ps[:, b, 0:256], WAG[:, 384:640], ALU.add, tk, t_wg)
            release(b, te)
        ZT = OG[:, 1024:3072]
        t1 = stt(ZT, ZL, -1.0, ZL, ALU.mult, ALU.max, te)
        t1 = act(ZT, ZT, ACT.Exp, t1, scale=-1.0)
        t1 = act(ZT, ZT, ACT.Ln, t1, bias=1.0)
        t_la = stt(ZL, ZL, 0.0, ZT, ALU.min, ALU.subtract, t1)

        UC = W1[:, 0:1026]
        CC = OG[:, 3072:4096]
        tz = memset(VE, UC[:, 0:2], 0.0, last(PE))
        uc_free = None
        for j in range(4):
            cc = feat(a["w_cv"][4 + j], P, t_h, HT3)
            ch = feat(a["w_cv"][8 + j], P, t_h, HT3)
            for h in range(2):
                hs = slice(512 * h, 512 * h + 512)
                te = cp(AE, CC[:, hs], ps[:, cc[h][0], :], cc[h][1], uc_free)
                release(cc[h][0], te)
                te = tt(UC[:, 2 + 512 * h:514 + 512 * h], CC[:, hs], ps[:, ch[h][0], :], ALU.mult, te, ch[h][1], uc_free)
                release(ch[h][0], te)
            cb = feat(a["w_cv"][j], P, t_h, HT3)
            dst = OC3[:, j, :]
            t1 = ts(dst, UC[:, 2:1026], pc["gw2"][:, j:j + 1], None, ALU.mult, None, te, tz)
            t1 = stt(dst, UC[:, 1:1025], pc["gw1"][:, j:j + 1], dst, ALU.mult, ALU.add, t1)
            t1 = stt(dst, UC[:, 0:1024], pc["gw0"][:, j:j + 1], dst, ALU.mult, ALU.add, t1)
            uc_free = t1
            for h in range(2):
                hs = slice(512 * h, 512 * h + 512)
                te = tt(dst[:, hs], dst[:, hs], ps[:, cb[h][0], :], ALU.mult, t1, cb[h][1])
                release(cb[h][0], te)
        t_oc = te

        done = all_done()
        for e in (PE, VE, AE, GE):
            e.wait(done)
        hat = [0]

        def hb(n):
            hat[0] += n
            return HT[:, hat[0] - n:hat[0]]
        sets = []
        for i in range(2):
            sets.append([hb(256) for _ in range(3)] + [hb(256) for _ in range(4)] + [hb(512), hb(512)])
        SG = hb(512)
        TS = hb(512)
        GD = sm(876, 32)
        t_sg = memset(VE, SG, 0.0)
        t_og = None
        prev = None
        for t in range(NT):
            Eb, Enb, Er, qi, ki, ks0, ks1, QKT, ST = sets[t % 2]
            la = ZL3[:, t, :]
            b, fr = acquire()
            mm(ps[:, b, 0:256], cst["TRI"], la, True, True, t_la, fr)
            tk = mm(ps[:, b, 256:512], cst["REST"], la, True, True, mark=True)
            fo = [last(PE)]
            t0 = act(Eb, ps[:, b, 0:256], ACT.Exp, tk, last(VE), scale=1.0 / 16)
            t1 = act(Enb, ps[:, b, 0:256], ACT.Exp, scale=-1.0 / 16)
            t2 = act(Er, ps[:, b, 256:512], ACT.Exp, scale=1.0 / 16)
            release(b, t2)
            b, fr = acquire()
            for q in range(2):
                tk = mm(ps[:, b, 2 * q:2 * q + 2], la[:, q * P:(q + 1) * P], cst["col"], True, True, fr, mark=(q == 1))
            gd = GD[:, 4 * t:4 * t + 4]
            t_gd = act(gd, ps[:, b, 0:4], ACT.Exp, tk, scale=1.0 / 16)
            release(b, t_gd)
            qq, kk = QK3[:, t, 0:256], QK3[:, t, 256:512]
            m0 = stt(qi, qq, 0.125, Eb, ALU.mult, ALU.mult, t0, fo)
            m1 = tt(ki, kk, Enb, ALU.mult, t1)
            m2 = stt(ks0, kk, cst["col"][:, 0:1], Er, ALU.mult, ALU.mult, t2)
            m3 = stt(ks1, kk, cst["col"][:, 1:2], Er, ALU.mult, ALU.mult, t2)
            b, fr = acquire()
            for q in range(2):
                tr(ps[:, b, q * P:(q + 1) * P], qi[:, q * P:(q + 1) * P], m0, m1, fr)
            for q in range(2):
                tk = tr(ps[:, b, (2 + q) * P:(3 + q) * P], ki[:, q * P:(q + 1) * P], mark=(q == 1))
            te = cp(AE, QKT, ps[:, b, :], tk)
            release(b, te)
            QT4 = v3(QKT, 4)
            (b0, f0), (b1, f1) = acquire(), acquire()
            for h in range(4):
                lo = 64 * (h % 2)
                b = (b0, b1)[h % 2]
                tk = mm(ps[:, b, (h // 2) * P:(h // 2 + 1) * P], QT4[lo:lo + 64, 2 + h // 2, :],
                        QT4[lo:lo + 64, h // 2, :], True, True, te, f0, f1, mark=(h == 3))
            ST3 = v3(ST, 4)
            for h in range(2):
                t_st = tt(ST3[:, h::2, :], v3(ps[:, (b0, b1)[h], 0:256], 2), bc(cst["TRI"], 2), ALU.mult, tk)
                release((b0, b1)[h], t_st)
            bo, fr = acquire()
            vt = V23[:, t, :]
            for h in range(4):
                mm(ps[:, bo, h * P:(h + 1) * P], ST3[:, h, :], vt[:, h * P:(h + 1) * P], h == 0, False, t_st, fr,
                   lax=True)
            for c in range(2):
                for q in range(2):
                    tk = mm(ps[64 * c:64 * c + 64, bo, q * 256:(q + 1) * 256], QT4[:, q, 64 * c:64 * c + 64],
                            SG[:, q * 256:(q + 1) * 256], False, True, t_sg, lax=True, mark=True)
                bs, fs = acquire()
                ksc = (ks0, ks1)[c]
                for q in range(2):
                    tk2 = mm(ps[:, bs, q * 256:(q + 1) * 256], ksc[:, q * P:(q + 1) * P], vt[:, q * 256:(q + 1) * 256],
                             True, True, m3, fs, mark=(q == 1))
                bd = cst["BD"].rearrange("p (a b) -> p a b", a=2)
                bdv = bd[:, :, 0:1].unsqueeze(1).broadcast_to([P, 2, 2, 128])
                psv = ps[:, bs, :].rearrange("p (q a n) -> p q a n", q=2, a=2)
                tsv = TS.rearrange("p (q a n) -> p q a n", q=2, a=2)
                t1 = None
                for q in range(2):
                    t1 = tt(tsv[:, q], psv[:, q], bl(cst["BD"][:, 0:128:64], 128), ALU.mult, tk2, t_sg)
                release(bs, t1)
                for q in range(2):
                    t_sg = stt(SG[:, q * 256:(q + 1) * 256], SG[:, q * 256:(q + 1) * 256], gd[:, 2 * q + c:2 * q + c + 1],
                               TS[:, q * 256:(q + 1) * 256], ALU.mult, ALU.add, t1, tk, t_gd)
            t_og = cp(AE, OG3[:, t, :], ps[:, bo, :], tk)
            release(bo, t_og)
        RS2 = sm(908, 32)
        done = all_done()
        for e in (PE, VE, AE, GE):
            e.wait(done)
        GN = EX[:, 640:768]
        t_gn = s_g.dma(SP, GN[:, :], a["gla_norm_g_2"].partition_broadcast(P).rearrange("p a n -> p (a n)"))
        SQ2 = AR[:, 0:4096]
        t1 = act(SQ2, OG, ACT.Square)
        t1 = red(RS2, SQ2.rearrange("p (g n) -> p g n", n=128), t1)
        t1 = rstd(RS2, 128, EPS, t1)
        og3 = OG.rearrange("p (g n) -> p g n", n=128)
        t1 = tt(og3, og3, bl(RS2, 128), ALU.mult, t1)
        t1 = tt(og3, og3, bc(GN[:, :], 32), ALU.mult, t1, t_gn)
        t2 = act(SQ2, GP, ACT.Sigmoid, t1)
        t2 = tt(SQ2, SQ2, GP, ALU.mult, t2)
        t2 = tt(OG, OG, SQ2, ALU.mult, t2, t1)
        OGT = AR[:, 4096:8192]
        OGT3 = v3(OGT, 4)
        for t in range(NT):
            b, fr = acquire()
            for p in range(4):
                tk = tr(ps[:, b, p * P:(p + 1) * P], OG3[:, t, p * P:(p + 1) * P], t2, fr, mark=(p == 3))
            te = cp(AE, OGT3[:, :, t * P:(t + 1) * P], v3(ps[:, b, :], 4), tk)
            release(b, te)

        class Two:
            def __getitem__(self, key):
                p, k, n = key
                return OGT3[p, k, n] if k < 4 else OC3[p, k - 4, n]

        def add2(t, nh, b, tk):
            xt = X[:, t * D + nh * 512:t * D + nh * 512 + 512]
            t_x1[t] = tt(xt, xt, b, ALU.add, tk)
            return t_x1[t]
        tokmajor(lambda nh, s: a["w_out"][nh, s], Two(), 8, 2, (te, te), add2)
        room.close()
        ffn(2, pc["g_n2"], a["w_fg2"], a["w_fu2"], a["w_fd2"], False)

        FN = sb("FN", 3072)
        NFB = FN[:, 0:1024]
        s_f = slot()
        t_nf = s_f.dma(SP, NFB, a["norm_f"].partition_broadcast(P).rearrange("p a n -> p (a n)"), all_done())
        s_out = slot()
        for t in range(NT):
            xt = X[:, t * D:(t + 1) * D]
            ss = sm(940 + t, 1)
            tq = act(FN[:, 1024 + 1024 * (t % 2):2048 + 1024 * (t % 2)], xt, ACT.Square, t_x1[t], last(AE), last(PE), accum_out=ss)
            tq = rstd(ss, D, EPS, tq)
            tq = stt(xt, xt, ss, NFB, ALU.mult, ALU.mult, tq, t_nf)
            t_o = s_out.dma(SP, out[t * P:(t + 1) * P, :], xt, tq)
        SP.wait(t_o)
        SP.wait(t_oa)

        block = ctx.enter_context(nc.Block())

        @block.tensor
        def _(e):
            PE.run(e)

        @block.vector
        def _(e):
            VE.run(e)

        @block.scalar
        def _(e):
            AE.run(e)

        @block.gpsimd
        def _(e):
            GE.run(e)

        @block.sync
        def _(e):
            SP.run(e)


def kernel(**inputs):
    import concourse.bacc as _bacc
    from concourse.bass_utils import run_bass_kernel_spmd as _run

    g = {n: np.ascontiguousarray(v) for n, v in inputs.items()}
    asc = np.ascontiguousarray

    def feat(w, n=P):
        return asc(w.reshape(8, P, -1, n).transpose(2, 1, 0, 3).reshape(-1, P, 8 * n))

    def tok(w):
        k, n = w.shape
        return asc(w.reshape(k // 256, 2, P, n // 512, 512).transpose(3, 0, 2, 1, 4).reshape(n // 512, k // 256, P, 1024))

    def cols(v):
        return v.reshape(-1, P).T

    w_in, w2in = g["w_in"][0], g["w_in_2"][0]
    rw = w_in[:, 416:2400]
    zpad = lambda v: np.concatenate([v[..., :1728], v[..., :64], v[..., 1728:]], -1)
    mu = zpad(g["shift_mu"][0])
    order = {
        "g_mix": cols(g["norm_mix_g"][0]), "g_qa": cols(g["q_a_norm_g"][0]), "g_kva": cols(g["kv_a_norm_g"][0]),
        "mup": cols(mu[0]), "mun": cols(mu[1]), "bg": cols(g["b_gate"][0].reshape(-1)),
        "g_ffn": cols(g["norm_ffn_g"][0]), "cw0": cols(g["ffn_conv_w"][0, 0]), "cw1": cols(g["ffn_conv_w"][0, 1]),
        "cw2": cols(g["ffn_conv_w"][0, 2]), "cb": cols(g["ffn_conv_b"][0]), "g_n1": cols(g["norm1_g_2"][0]),
        "g_n2": cols(g["norm2_g_2"][0]), "gw0": cols(g["conv_w_2"][0, 0]), "gw1": cols(g["conv_w_2"][0, 1]),
        "gw2": cols(g["conv_w_2"][0, 2]),
    }
    ins = {
        "x": g["x"][0], "pos": asc(g["positions"].reshape(8, P).T), "cst": const_table(),
        "pcols": asc(np.concatenate([order[n] for n, _ in PCOLS], 1)),
        "w_mla": asc(w_in[:, 0:416].reshape(8, P, 416).transpose(1, 0, 2)),
        "w_rw": feat(zpad(rw)), "w_g": feat(w_in[:, 2400:]), "w_uq": g["w_uq"][0], "w_ukv": g["w_ukv"][0],
        "qn_norm_g": g["qn_norm_g"], "qr_norm_g": g["qr_norm_g"], "kn_norm_g": g["kn_norm_g"],
        "kr_norm_g": g["kr_norm_g"], "k_k": g["k_k"], "k_a": g["k_a"], "r_k": g["r_k"].reshape(1, 512),
        "a0": g["a0"], "w0": g["w0"][0], "a2": g["a2"][0], "w2": g["w2"][0].reshape(128, 512),
        "g2": g["g2"][0].reshape(256, 512), "ln_x_g": g["ln_x_g"], "ln_x_b": g["ln_x_b"],
        "w_o": feat(g["w_o"][0]), "w_merge": tok(g["w_merge"][0]),
        "w_fg": feat(g["w_ffn_gate"][0]), "w_fu": feat(g["w_ffn_up"][0]), "w_fd": tok(g["w_ffn_down"][0]),
        "w_tok2": tok(w2in[:, 0:1536]), "w_a": asc(w2in[:, 1536:1552].reshape(8, P, 16).transpose(1, 0, 2)),
        "w_cv": feat(w2in[:, 1552:]), "w_gate_up": g["w_gate_up_2"][0], "b_gate_2": g["b_gate_2"],
        "gla_norm_g_2": g["gla_norm_g_2"], "w_out": tok(g["w_out_2"][0]),
        "w_fg2": feat(g["w_ffn_gate_2"][0]), "w_fu2": feat(g["w_ffn_up_2"][0]), "w_fd2": tok(g["w_ffn_down_2"][0]),
        "norm_f": g["norm_f_g_2"].reshape(1, 1024),
    }
    nc = _bacc.Bacc("TRN2", target_bir_lowering=False, num_devices=1)
    arrays, a = {}, {}
    for n, v in ins.items():
        v = asc(v)
        arrays[f"in_{n}"] = v
        a[n] = nc.dram_tensor(f"in_{n}", v.shape, mybir.dt.from_np(v.dtype), kind="ExternalInput").ap()
    a["oa_d"] = nc.dram_tensor("oa_d", [512, 1024], F32, kind="Internal").ap()
    a["qk_d"] = nc.dram_tensor("qk_d", [8, 2, 96, 1024], F32, kind="Internal").ap()
    a["v_d"] = nc.dram_tensor("v_d", [8, P, 512], F32, kind="Internal").ap()
    a["g_d"] = nc.dram_tensor("g_d", [16, 2, P, 512], F32, kind="Internal").ap()
    a["rw_d"] = nc.dram_tensor("rw_d", [8, 7, P, 512], F32, kind="Internal").ap()
    a["o_d"] = nc.dram_tensor("o_d", [2, 8, P, 512], F32, kind="Internal").ap()
    out = nc.dram_tensor("out_0", [1024, 1024], F32, kind="ExternalOutput").ap()
    program(nc, a, out)
    r = _run(nc, [arrays], core_ids=[0])
    return r.results[0]["out_0"].reshape(1, 1024, 1024)
```

```python
from contextlib import ExitStack
import math

import numpy as np

import concourse.bass as bass
from concourse import mybir

F32 = mybir.dt.float32
I32 = mybir.dt.int32
ACT = mybir.ActivationFunctionType
ALU = mybir.AluOpType
AX = mybir.AxisListType

P = 128
S = 1024
D = 1024
NT = S // P
FF = 2816
NF = FF // P
EPS = 1e-6
GN_EPS = 64e-5
EH = math.exp(-0.5)
SCALE = 1.0 / math.sqrt(96.0)

CONST = ["ident", "SU", "IU", "SL", "IL", "DU", "DL", "OU", "OL", "BD", "TCF", "TCB", "TRI", "REST"]
COLS = [("col", 2), ("invf", 16)]
PCOLS = [("g_mix", 8), ("g_qa", 2), ("g_kva", 1), ("mup", 16), ("mun", 16), ("bg", 16), ("g_ffn", 8),
         ("cw0", NF), ("cw1", NF), ("cw2", NF), ("cb", NF), ("g_n1", 8), ("g_n2", 8),
         ("gw0", 4), ("gw1", 4), ("gw2", 4)]


def const_table():
    i = np.arange(P)
    p, f = i[:, None], i[None, :]
    blk = (p // 16) == (f // 16)
    half = (p // 64) == (f // 64)
    mid_f = (p <= 63).astype(np.float32)
    mid_b = (p >= 64).astype(np.float32)
    m = {
        "ident": p == f, "SU": p < f, "SL": p > f, "IU": p <= f, "IL": p >= f,
        "DU": (p < f) & blk, "DL": (p > f) & blk, "OU": (p < f) & ~blk, "OL": (p > f) & ~blk,
        "BD": half,
        "TCF": (p <= f).astype(np.float32) - mid_f, "TCB": (p >= f).astype(np.float32) - mid_b,
        "TRI": (p <= f) & half, "REST": (p > f) & half,
    }
    parts = [np.broadcast_to(m[n], (P, P)).astype(np.float32) for n in CONST]
    parts.append(np.stack([(i <= 63), (i > 63)], 1).astype(np.float32))
    inv = 10000.0 ** (-np.arange(0, 32, 2, dtype=np.float64) / 32)
    parts.append(np.broadcast_to(inv.astype(np.float32), (P, 16)))
    return np.ascontiguousarray(np.concatenate(parts, 1))


class Eng:

    def __init__(self, sem):
        self.sem, self.n, self.q, self.seen = sem, 0, [], {}

    def wait(self, *toks):
        for t in toks:
            if t is None:
                continue
            if isinstance(t, list):
                self.wait(*t)
            elif self.seen.get(id(t[0]), 0) < t[1]:
                self.seen[id(t[0])] = t[1]
                self.q.append(lambda e, t=t: e.wait_ge(t[0], t[1]))

    def do(self, fn, *toks):
        self.wait(*toks)
        self.n += 1
        self.q.append(lambda e: fn(e).then_inc(self.sem, 1))
        return (self.sem, self.n)

    def quiet(self, fn, *toks):
        self.wait(*toks)
        self.q.append(lambda e: fn(e))

    def run(self, e):
        for f in self.q:
            f(e)


class Slot:

    def __init__(self, sem, ap=None):
        self.sem, self.n, self.ap, self.free = sem, 0, ap, None

    def dma(self, eng, out, in_, *toks):
        eng.wait(*toks)
        self.n += 16
        eng.q.append(lambda e: e.dma_start(out, in_).then_inc(self.sem, 16))
        return (self.sem, self.n)


def interleave(*gens):
    gens = list(gens)
    while gens:
        for g in list(gens):
            try:
                next(g)
            except StopIteration:
                gens.remove(g)


class K:
    pass


def program(nc, a, out):
    ctx = ExitStack()
    with ctx:
        nsem = [0]

        def sem(name):
            return ctx.enter_context(nc.semaphore(name))

        def sb(name, n):
            return ctx.enter_context(nc.sbuf_tensor(name, [P, n], F32))

        PE, VE, AE, GE, SP = [Eng(sem(f"s_{n}")) for n in ("pe", "ve", "ae", "ge", "sp")]

        def slot(ap=None):
            nsem[0] += 1
            return Slot(sem(f"d{nsem[0]}"), ap)

        X = sb("X", 8192)
        W = sb("W", 4096)
        W1 = sb("W1", 2052)
        NCST = len(CONST) * P + 18
        CS = sb("CS", NCST)
        NPC = sum(n for _, n in PCOLS)
        PC = sb("PC", NPC)
        SM = sb("SM", 1024)
        OTB = sb("OTB", 512)

        def region(st, name, n, dt=F32):
            return st.enter_context(nc.sbuf_tensor(name, [P, n], dt))[:, :]

        FR = mybir.dt.float32r
        room = ExitStack()
        HT, AR, EX = [region(room, n, w) for n, w in (("HT", 8192), ("AR", 22528), ("EX", 4096))]
        ps = ctx.enter_context(nc.psum_tensor("ps", [P, 8, 512], F32))

        cst = {n: CS[:, i * P:(i + 1) * P] for i, n in enumerate(CONST)}
        cst["col"] = CS[:, len(CONST) * P:len(CONST) * P + 2]
        cst["invf"] = CS[:, len(CONST) * P + 2:len(CONST) * P + 18]
        pc = {}
        at = 0
        for n, w in PCOLS:
            pc[n] = PC[:, at:at + w]
            at += w

        def v3(ap, k):
            return ap.rearrange("p (a b) -> p a b", a=k)

        def bc(ap, k):
            return ap.unsqueeze(1).broadcast_to([P, k, ap.shape[1]])

        def bl(ap, k):
            return ap.unsqueeze(2).broadcast_to([P, ap.shape[1], k])

        sc = slot()
        t_cst = sc.dma(SP, CS[:, :], a["cst"])
        t_cst = sc.dma(SP, PC[:, :], a["pcols"])
        ident = cst["ident"]

        bank_free = [None] * 8
        bank_at = [0]
        bank_held = [False] * 8

        def acquire(n=1):
            for _ in range(9):
                if n == 2 and bank_at[0] % 2:
                    bank_at[0] += 1
                b = bank_at[0] % 8
                if not any(bank_held[b:b + n]):
                    break
                bank_at[0] += 1
            else:
                raise RuntimeError("no free bank")
            bank_at[0] += n
            for i in range(n):
                bank_held[b + i] = True
            toks = [bank_free[b + i] for i in range(n)]
            return b, toks

        def release(b, tok, n=1):
            for i in range(n):
                bank_free[b + i] = tok
                bank_held[b + i] = False

        ring = [slot(W[:, i * 1024:(i + 1) * 1024]) for i in range(4)]
        ring_at = [0]

        def load_w(src, n=1024):
            r = ring[ring_at[0] % 4]
            ring_at[0] += 1
            t = r.dma(SP, r.ap[:, 0:n], src, r.free)
            r.free = None
            return r, t

        def mm(o, l, r, start, stop, *toks, mark=False, lax=False):
            f = lambda e: e.matmul(o, l, r, start=start, stop=stop, **({"skip_group_check": True} if lax else {}))
            if mark:
                return PE.do(f, *toks)
            PE.quiet(f, *toks)

        def tr(o, i, *toks, mark=False):
            f = lambda e: e.transpose(o, i, ident)
            if mark:
                return PE.do(f, *toks)
            PE.quiet(f, *toks)

        def act(o, i, f, *toks, **kw):
            return AE.do(lambda e: e.activation(o, i, f, **kw), *toks)

        def tt(o, x, y, op, *toks, eng=None):
            return (eng or VE).do(lambda e: e.tensor_tensor(o, x, y, op), *toks)

        def ts(o, x, s1, s2, o1, o2, *toks, eng=None):
            if s2 is None:
                return (eng or VE).do(lambda e: e.tensor_scalar(o, x, s1, None, o1), *toks)
            return (eng or VE).do(lambda e: e.tensor_scalar(o, x, s1, s2, o1, o2), *toks)

        def stt(o, x, s, y, o1, o2, *toks):
            return VE.do(lambda e: e.scalar_tensor_tensor(out=o, in0=x, scalar=s, in1=y, op0=o1, op1=o2), *toks)

        def red(o, x, *toks, op=ALU.add):
            return VE.do(lambda e: e.tensor_reduce(o, x, AX.X, op), *toks)

        def recip(o, x, *toks):
            return VE.do(lambda e: e.reciprocal(o, x), *toks)

        def cp(eng, o, x, *toks):
            if eng is AE:
                return act(o, x, ACT.Copy, *toks)
            return eng.do(lambda e: e.tensor_copy(o, x), *toks)

        def memset(eng, o, v, *toks):
            return eng.do(lambda e: e.memset(o, v), *toks)

        def last(eng):
            return (eng.sem, eng.n) if eng.n else None

        def all_done():
            return [last(e) for e in (PE, VE, AE, GE)]

        def sm(at, n):
            return SM[:, at:at + n]

        def rstd(o, n, eps, *toks):
            t = ts(o, o, 1.0 / n, eps, ALU.mult, ALU.add, *toks)
            t = act(o, o, ACT.Sqrt, t)
            return recip(o, o, t)

        def transposes(xs, k0, *toks):
            b, fr = acquire()
            for j in range(4):
                tp = tr(ps[:, b, j * P:(j + 1) * P], xs[:, (k0 + j) * P:(k0 + j + 1) * P], fr, *toks, mark=(j == 3))
            return b, tp

        def norm_rows(t, xs, *toks):
            xt = X[:, t * D:(t + 1) * D]
            ss = sm(t, 1)
            tq = act(xs, xt, ACT.Square, *toks, accum_out=ss)
            tq = rstd(ss, D, EPS, tq)
            return ts(xs, xt, ss, None, ALU.mult, None, tq)

        def norm_first(gain, tok_of, tmp, HT):
            fr = [None] * len(tmp)
            half = []
            for t in range(NT):
                s = t % len(tmp)
                tq = norm_rows(t, tmp[s], tok_of[t], fr[s])
                for h in range(2):
                    b, fr[s] = transposes(tmp[s], 4 * h, tq, t_cst)
                    te = tt(v3(HT, 8)[:, 4 * h:4 * h + 4, t * P:(t + 1) * P], v3(ps[:, b, :], 4),
                            bl(gain[:, 4 * h:4 * h + 4], P), ALU.mult, fr[s])
                    release(b, te)
                if t % 4 == 3:
                    half.append(te)
            return half

        bg = [None]

        def bg_step():
            if bg[0] is not None and next(bg[0], "end") == "end":
                bg[0] = None

        def need(tok_h, h):
            while isinstance(tok_h, dict) and h not in tok_h:
                assert bg[0] is not None
                bg_step()
            return tok_h[h]

        def start_norm(gain, free):
            ready, tok_h = {}, {}
            tmp = [W1[:, 0:1024], W1[:, 1024:2048]]
            nt = v3(OTB[:, :], 4)

            def run():
                fr = [free, free]
                nt_free = free
                while 0 not in ready:
                    yield
                cur = norm_rows(0, tmp[0], ready[0], free)
                yield
                for t in range(NT):
                    nxt = None
                    if t + 1 in ready:
                        nxt = norm_rows(t + 1, tmp[(t + 1) % 2], ready[t + 1], fr[(t + 1) % 2])
                    for h in range(2):
                        b, tp = transposes(tmp[t % 2], 4 * h, cur)
                        hi, lo = [v3(q, 8)[:, 4 * h:4 * h + 4, t * P:(t + 1) * P] for q in (HH, HL)]
                        te = tt(nt, v3(ps[:, b, :], 4), bl(gain[:, 4 * h:4 * h + 4], P), ALU.mult, tp, nt_free)
                        release(b, te)
                        th = act(hi, nt, ACT.Copy, te, free)
                        nt_free = tt(lo, nt, hi.bitcast(F32), ALU.subtract, th)
                        if t % 4 == 3 and h == 1:
                            tok_h[t // 4] = nt_free
                        if h == 0:
                            yield
                    fr[t % 2] = tp
                    yield
                    if nxt is None and t < NT - 1:
                        while t + 1 not in ready:
                            yield
                        nxt = norm_rows(t + 1, tmp[(t + 1) % 2], ready[t + 1], fr[(t + 1) % 2])
                        yield
                    cur = nxt

            bg[0] = run()
            return ready, tok_h

        HT3 = v3(HT[:, :], 8)

        def feat(src, ncol, tok_h, HT3):
            r, tw = load_w(src)
            w3 = v3(r.ap, 8)
            res = []
            for h in range(2):
                b, fr = acquire()
                for k in range(8):
                    tk = mm(ps[0:ncol, b, :], w3[:, k, 0:ncol], HT3[:, k, h * 512:(h + 1) * 512],
                            k == 0, k == 7, tw, tok_h[h], fr, mark=(k == 7))
                res.append((b, tk))
            r.free = tk
            return res

        xsl = [slot() for _ in range(NT)]
        t_x = [xsl[t].dma(SP, X[:, t * D:(t + 1) * D], a["x"][t * P:(t + 1) * P, :]) for t in range(NT)]

        A = 0
        MC = AR[:, 0:3328]
        CQT = AR[:, 3328:5376]
        CKT = AR[:, 5376:6400]
        WUQ = AR[:, 6400:7936]
        WUKV = AR[:, 7936:8960]
        Q = AR[:, 8960:15104]
        WM = AR[:, 15104:18432]
        tmpn = [AR[:, 18432:19456], AR[:, 19456:20480]]
        s_m = slot()
        t_wm = s_m.dma(SP, v3(WM, 8), a["w_mla"])
        t_wm = s_m.dma(SP, v3(WUQ, 2), a["w_uq"].rearrange("(k p) n -> p k n", p=P))
        t_wm = s_m.dma(SP, WUKV, a["w_ukv"])
        GB = AR[:, 20480:20480 + 192]
        t_wm = s_m.dma(SP, GB[:, 0:64], a["qn_norm_g"].partition_broadcast(P).rearrange("p a n -> p (a n)"))
        t_wm = s_m.dma(SP, GB[:, 64:96], a["qr_norm_g"].partition_broadcast(P).rearrange("p a n -> p (a n)"))
        t_wm = s_m.dma(SP, GB[:, 96:160], a["kn_norm_g"].partition_broadcast(P).rearrange("p a n -> p (a n)"))
        t_wm = s_m.dma(SP, GB[:, 160:192], a["kr_norm_g"].partition_broadcast(P).rearrange("p a n -> p (a n)"))
        POS = AR[:, 20672:20680].bitcast(I32)
        t_wm = s_m.dma(SP, POS, a["pos"])

        AE.wait(t_cst)
        VE.wait(t_cst)
        t_h = norm_first(pc["g_mix"], t_x, tmpn, HT)

        g_d = a["g_d"]
        gst = [slot(W1[:, 512 * i:512 * i + 512]) for i in range(4)]

        def gates_gen():
            i = 0
            for n in range(16):
                r, tw = load_w(a["w_g"][n])
                w3 = v3(r.ap, 8)
                for h in range(2):
                    b, fr = acquire()
                    for k in range(8):
                        tk = mm(ps[:, b, :], w3[:, k, :], HT3[:, k, h * 512:(h + 1) * 512], k == 0, k == 7, tw, t_h[h],
                                fr, mark=(k == 7))
                    r.free = tk
                    st_ = gst[i % 4]
                    te = act(st_.ap, ps[:, b, :], ACT.Sigmoid, tk, st_.free, bias=pc["bg"][:, n:n + 1])
                    release(b, te)
                    st_.free = st_.dma(GE, g_d[n, h], st_.ap, te, st_.free)
                    i += 1
                    yield

        gates = gates_gen()

        def run_gates(n):
            for _ in range(n):
                next(gates, None)

        MC3 = v3(MC, 8)
        WM3 = v3(WM, 8)
        for t in range(NT):
            b, fr = acquire()
            for k in range(8):
                tk = mm(ps[:, b, 0:416], HT3[:, k, t * P:(t + 1) * P], WM3[:, k, :], k == 0, k == 7, t_h[t // 4], t_wm, fr,
                        mark=(k == 7))
            te = cp(AE, MC3[:, t, :], ps[:, b, 0:416], tk)
            release(b, te)
        t_mc = te
        tk_m = tk
        run_gates(4)
        SQ = WM
        SQ3 = v3(SQ, 8)
        tq = tt(SQ, MC, MC, ALU.mult, t_mc, tk_m)
        ss = v3(sm(16, 24), 3)
        tq1 = red(ss[:, 0, :], SQ3[:, :, 0:256], tq)
        tq2 = red(ss[:, 1, :], SQ3[:, :, 256:384], tq)
        tq3 = red(ss[:, 2, :], SQ3[:, :, 384:416], tq)
        ts(ss[:, 0, :], ss[:, 0, :], 1.0 / 256, EPS, ALU.mult, ALU.add, tq1)
        ts(ss[:, 1, :], ss[:, 1, :], 1.0 / 128, EPS, ALU.mult, ALU.add, tq2)
        tq = ts(ss[:, 2, :], ss[:, 2, :], 1.0 / 32, EPS, ALU.mult, ALU.add, tq3)
        tq = act(sm(16, 24), sm(16, 24), ACT.Sqrt, tq)
        tq = recip(sm(16, 24), sm(16, 24), tq)
        tn = None
        for i, (lo, hi) in enumerate(((0, 256), (256, 384), (384, 416))):
            tn = tt(MC3[:, :, lo:hi], MC3[:, :, lo:hi], bl(ss[:, i, :], hi - lo), ALU.mult, tq)
        CQ3 = v3(CQT, 2)
        for t in range(NT):
            b, fr = acquire()
            for j in range(3):
                tk = tr(ps[:, b, j * P:(j + 1) * P], MC3[:, t, j * P:(j + 1) * P], tn, fr, mark=(j == 2))
            te = tt(CQ3[:, :, t * P:(t + 1) * P], v3(ps[:, b, 0:256], 2), bl(pc["g_qa"], P), ALU.mult, tk)
            te = ts(CKT[:, t * P:(t + 1) * P], ps[:, b, 256:384], pc["g_kva"], None, ALU.mult, None)
            release(b, te)
        t_cT = te

        POSF = sm(40, 8)
        ANG, COS, SIN, TMP = [AR[:, 20700 + 128 * i:20828 + 128 * i] for i in range(4)]
        tr0 = cp(VE, POSF, POS, t_wm)
        tr0 = tt(v3(ANG, 8), bl(POSF, 16), bc(cst["invf"], 8), ALU.mult, tr0)
        MAGIC = 12582912.0
        tr0 = ts(TMP, ANG, 1.0 / (2 * math.pi), MAGIC, ALU.mult, ALU.add, tr0)
        tr0 = ts(TMP, TMP, -MAGIC, None, ALU.add, None, tr0)
        C1 = 6.28125
        C2 = float(np.float32(int((2 * math.pi - C1) * 2 ** 20) / 2 ** 20))
        C3 = 2 * math.pi - C1 - C2
        for c in (C1, C2, C3):
            tr0 = stt(ANG, TMP, -c, ANG, ALU.mult, ALU.add, tr0)
        LIM = 3.1415925
        tr0 = ts(ANG, ANG, LIM, -LIM, ALU.min, ALU.max, tr0)
        tr1 = stt(TMP, ANG, -1.0, ANG, ALU.mult, ALU.max, tr0)
        tr1 = ts(TMP, TMP, -1.0, math.pi / 2, ALU.mult, ALU.add, tr1)
        act(SIN, ANG, ACT.Sin, tr0)
        t_rope = act(COS, TMP, ACT.Sin, tr1)

        Q4 = Q.rearrange("p (t h d) -> p t h d", t=8, h=8)
        Q3 = v3(Q, 8)
        KV3 = v3(X[:, :], 8)
        KV4 = X[:, :].rearrange("p (t h d) -> p t h d", t=8, h=8)
        WUQ3 = v3(WUQ, 2)
        for t in range(NT):
            for hh in range(2):
                b, fr = acquire()
                for k in range(2):
                    tk = mm(ps[:, b, 0:384], CQ3[:, k, t * P:(t + 1) * P], WUQ3[:, k, hh * 384:(hh + 1) * 384],
                            k == 0, k == 1, t_cT, fr, mark=(k == 1))
                te = cp(AE, Q3[:, t, hh * 384:(hh + 1) * 384], ps[:, b, 0:384], tk)
                release(b, te)
                b, fr = acquire()
                tk = mm(ps[:, b, :], CKT[:, t * P:(t + 1) * P], WUKV[:, hh * 512:(hh + 1) * 512], True, True, fr,
                        t_cT, mark=True)
                tv = cp(VE, KV3[:, t, hh * 512:(hh + 1) * 512], ps[:, b, :], tk, last(GE))
                release(b, tv)
        t_q, t_kv = te, tv
        s_v = slot()
        for h in range(8):
            t_vd = s_v.dma(GE, a["v_d"][h].rearrange("p (t n) -> p t n", t=8), KV4[:, :, h, 64:128], t_kv)
        run_gates(5)
        SQ = AR[:, 0:4096]
        SQn = SQ.rearrange("p (t h d) -> p t h d", t=8, h=8)
        ssq = [v3(sm(64 + 64 * i, 64), 8) for i in range(3)]
        KR = AR[:, 21300:21556]
        KR3 = v3(KR, 8)
        tkr = tt(KR3, MC3[:, :, 384:416], bc(GB[:, 160:192], 8), ALU.mult, tn, t_wm)
        PE_t = last(PE)
        g3 = lambda ap, o: ap.rearrange("p t h d -> p (t h) d")
        SQk = AR[:, 15104:19200].rearrange("p (g d) -> p g d", d=64)
        SQr = EX[:, 0:2048].rearrange("p (g d) -> p g d", d=32)
        t1 = act(g3(SQn, 0), g3(Q4[:, :, :, 0:64], 0), ACT.Square, t_q, t_kv, tkr, PE_t)
        t2 = act(SQr, g3(Q4[:, :, :, 64:96], 0), ACT.Square)
        t3 = act(SQk, g3(KV4[:, :, :, 0:64], 0), ACT.Square)
        red(sm(64, 64), g3(SQn, 0), t1)
        red(sm(128, 64), SQr, t2)
        tq = red(sm(192, 64), SQk, t3)
        ts(sm(64, 64), sm(64, 64), 1.0 / 64, EPS, ALU.mult, ALU.add, tq)
        ts(sm(128, 64), sm(128, 64), 1.0 / 32, EPS, ALU.mult, ALU.add, tq)
        tq = ts(sm(192, 64), sm(192, 64), 1.0 / 64, EPS, ALU.mult, ALU.add, tq)
        tq = act(sm(64, 192), sm(64, 192), ACT.Sqrt, tq)
        run_gates(5)
        tq = recip(sm(64, 192), sm(64, 192), tq)
        qn, qr, kn = g3(Q4[:, :, :, 0:64], 0), g3(Q4[:, :, :, 64:96], 0), g3(KV4[:, :, :, 0:64], 0)
        t1 = tt(qn, qn, bl(sm(64, 64), 64), ALU.mult, tq)
        t2 = tt(qr, qr, bl(sm(128, 64), 32), ALU.mult, tq)
        t3 = tt(kn, kn, bl(sm(192, 64), 64), ALU.mult, tq)
        t1 = tt(qn, qn, bc(GB[:, 0:64], 64), ALU.mult, t1)
        t2 = tt(qr, qr, bc(GB[:, 64:96], 64), ALU.mult, t2)
        RA, RB, RC, RD = [AR[:, 1024 * i:1024 * (i + 1)] for i in range(4)]

        def rotate(a4, b4, shp, tok):
            c4, s4 = COS, SIN
            if shp == "q":
                c4 = v3(COS, 8).unsqueeze(2).broadcast_to([P, 8, 8, 16])
                s4 = v3(SIN, 8).unsqueeze(2).broadcast_to([P, 8, 8, 16])
                w = [r.rearrange("p (t h d) -> p t h d", t=8, h=8) for r in (RA, RB, RC, RD)]
            else:
                c4, s4 = v3(COS, 8), v3(SIN, 8)
                w = [v3(r[:, 0:128], 8) for r in (RA, RB, RC, RD)]
            m0 = tt(w[0], a4, c4, ALU.mult, tok, t_rope)
            m1 = tt(w[1], b4, s4, ALU.mult, tok)
            m2 = tt(w[2], b4, c4, ALU.mult, tok)
            m3 = tt(w[3], a4, s4, ALU.mult, tok)
            tt(a4, w[0], w[1], ALU.subtract, m3)
            return tt(b4, w[2], w[3], ALU.add, m3)

        tkr = rotate(KR3[:, :, 0:16], KR3[:, :, 16:32], "k", t3)
        t_qf = rotate(Q4[:, :, :, 64:80], Q4[:, :, :, 80:96], "q", tkr)

        QT = [AR[0:96, 15104 + 1024 * i:16128 + 1024 * i] for i in range(2)]
        KT = [AR[0:96, 17152 + 1024 * i:18176 + 1024 * i] for i in range(2)]
        K96 = [v3(EX[:, 2048 + 768 * i:2816 + 768 * i], 8) for i in range(2)]
        oa_d = a["oa_d"]
        start_att = [t_qf, last(PE)]
        k_free = [None, None]
        t_kr = [cp(VE, K96[i][:, :, 64:96], KR3, start_att) for i in range(2)]
        s_qt = [slot(), slot()]
        q_out = [None, None]
        for h in range(8):
            s_ = h % 2
            K3 = K96[s_]
            tc = [tt(K3[:, :, 0:64], KV4[:, :, h, 0:64], bc(GB[:, 96:160], 8), ALU.mult, start_att, k_free[s_], eng=GE),
                  t_kr[s_]]
            toks = []
            for (dst, src) in ((QT[s_], lambda t: Q4[:, t, h, :]), (KT[s_], lambda t: K3[:, t, :])):
                for g in range(2):
                    b, fr = acquire()
                    for j in range(4):
                        tk = tr(ps[0:96, b, j * P:(j + 1) * P], src(4 * g + j), tc, start_att, fr, mark=(j == 3))
                    te = cp(AE if g else VE, dst[:, g * 512:(g + 1) * 512], ps[0:96, b, :], tk, q_out[s_])
                    release(b, te)
                    toks.append(te)
            k_free[s_] = tk
            s_qt[s_].dma(SP, a["qk_d"][h, 0], QT[s_], toks)
            q_out[s_] = s_qt[s_].dma(SP, a["qk_d"][h, 1], KT[s_])
        t_mla = [t_vd] + q_out


        def attention(start):
            QT = [HT[0:96, 2048 * i:2048 * i + 1024] for i in range(2)]
            KT = [HT[0:96, 2048 * i + 1024:2048 * i + 2048] for i in range(2)]
            VH = [v3(HT[:, 4096 + 512 * i:4608 + 512 * i], 8) for i in range(2)]
            PB = [HT[:, 5120 + 1024 * i:6144 + 1024 * i] for i in range(2)]
            OP = HT[:, 7168:8192]
            PT = [W1[:, 1024 * i:1024 * (i + 1)] for i in range(2)]
            s_h = [slot(), slot()]
            h_tok, h_free = {}, [None, None]
            s_oa = slot()
            att = {}
            pb_free, pt_free = [None, None], [None, None]
            fr_o = {"op": None, "ot": None}

            def load(h):
                x = h % 2
                s_h[x].dma(SP, QT[x], a["qk_d"][h, 0], start, h_free[x])
                s_h[x].dma(SP, KT[x], a["qk_d"][h, 1])
                h_tok[h] = s_h[x].dma(SP, VH[x], a["v_d"][h].rearrange("p (t n) -> p t n", t=8))

            def a_scores(i):
                h, q = divmod(i, 8)
                b, fr = acquire(2)
                for j in range(2):
                    tk = mm(ps[:, b + j, :], QT[h % 2][:, q * P:(q + 1) * P], KT[h % 2][:, j * 512:(j + 1) * 512],
                            True, True, h_tok[h], fr, mark=(j == 1))
                m, nb, rs = sm(256 + i % 4, 1), sm(264 + i % 4, 1), sm(272 + i % 4, 1)
                src = ps[:, b:b + 2, :].rearrange("p a b -> p (a b)")
                tm = red(m, src, tk, op=ALU.max)
                tm = ts(nb, m, -SCALE, None, ALU.mult, None, tm)
                te = act(PB[i % 2], src, ACT.Exp, tm, pb_free[i % 2], bias=nb, scale=SCALE, accum_out=rs)
                release(b, te, 2)
                att[i] = te

            def a_transp(i):
                b, fr = acquire(2)
                for j in range(8):
                    tk = tr(ps[:, b + j // 4, (j % 4) * P:(j % 4 + 1) * P], PB[i % 2][:, j * P:(j + 1) * P],
                            att[i], fr, mark=(j in (3, 7)))
                    if j == 3:
                        tk0 = tk
                pb_free[i % 2] = tk
                t0 = cp(AE, PT[i % 2][:, 0:512], ps[:, b, :], tk0, pt_free[i % 2])
                t1 = cp(AE, PT[i % 2][:, 512:1024], ps[:, b + 1, :], tk, pt_free[i % 2])
                release(b, t0)
                release(b + 1, t1)
                att[i] = [att[i], t0, t1]

            def a_pv(i):
                h, q = divmod(i, 8)
                b, fr = acquire()
                for j in range(8):
                    tk = mm(ps[:, b, 0:64], PT[i % 2][:, j * P:(j + 1) * P], VH[h % 2][:, j, :], j == 0, j == 7,
                            att[i], fr, mark=(j == 7))
                pt_free[i % 2] = tk
                if q == 7:
                    h_free[h % 2] = tk
                rs = sm(272 + i % 4, 1)
                tq = recip(rs, rs, att[i])
                dst = v3(OP, 8)[:, q, (h % 2) * 64:(h % 2) * 64 + 64]
                te = ts(dst, ps[:, b, 0:64], rs, None, ALU.mult, None, tq, tk, fr_o["op"])
                release(b, te)
                if i % 16 == 15:
                    pr = h // 2
                    for g in range(2):
                        b, fr = acquire()
                        for j in range(4):
                            tk = tr(ps[:, b, j * P:(j + 1) * P], OP[:, (4 * g + j) * P:(4 * g + j + 1) * P], te, fr,
                                    mark=(j == 3))
                        tw = cp(VE, OTB[:, :], ps[:, b, :], tk, fr_o["ot"])
                        release(b, tw)
                        fr_o["ot"] = s_oa.dma(GE, oa_d[pr * P:(pr + 1) * P, 512 * g:512 * g + 512], OTB[:, :], tw)
                    fr_o["op"] = tk

            load(0)
            yield
            for i in range(64 + 2):
                if i % 8 == 2 and i // 8 + 1 < 8:
                    load(i // 8 + 1)
                if i < 64:
                    a_scores(i)
                    yield
                if 1 <= i <= 64:
                    a_transp(i - 1)
                    yield
                if i >= 2:
                    a_pv(i - 2)
                    yield
            t_att.append(fr_o["ot"])

        t_att = []

        done = all_done() + t_mla
        for e in (PE, VE, AE, GE):
            e.wait(done)
        U = AR[:, 0:12288]
        U3 = v3(U, 8)
        UL = [AR[:, 12288 + 1024 * i:13312 + 1024 * i] for i in range(4)]
        BCT = AR[:, 16384:19456]
        KKB, KAB, RKB, A0B, W0F, W0B = [BCT[:, 512 * i:512 * (i + 1)] for i in range(6)]
        LW = AR[:, 19456:20480]
        A2W, W2B = LW[:, 0:512], LW[:, 512:1024]
        s_b = slot()
        rows = [(KKB, a["k_k"][0:1, :]), (KAB, a["k_a"][0:1, :]), (RKB, a["r_k"][0:1, :]), (A0B, a["a0"][0:1, :]),
                (W0F, a["w0"][0:1, :]), (W0B, a["w0"][1:2, :])]
        for dst, src in rows:
            t_b = s_b.dma(SP, dst, src.partition_broadcast(P).rearrange("p a n -> p (a n)"), done)
        t_b = s_b.dma(SP, A2W[0:64, :], a["a2"])
        t_b = s_b.dma(SP, A2W[64:128, :], a["w2"][0:64, :])
        t_b = s_b.dma(SP, W2B[0:64, :], a["w2"][64:128, :])
        RAW = [X[:, 1100 * i:1100 * i + 1026] for i in range(2)]
        U1 = [X[:, 2200 + 1024 * i:3224 + 1024 * i] for i in range(2)]
        U2 = [X[:, 4300 + 1024 * i:5324 + 1024 * i] for i in range(2)]
        C0 = sm(280, 16)
        tc0 = tt(C0, pc["mup"], pc["mun"], ALU.add)
        tc0 = ts(C0, C0, -1.0, 1.0, ALU.mult, ALU.add, tc0)
        for i in range(2):
            memset(VE, RAW[i][:, 0:1], 0.0)
            tz = memset(VE, RAW[i][:, 1025:1026], 0.0)
        raw_free, u2_free = [None, None], [None, None]
        pend = []

        def fin_shift(ft, n, dst, tok):
            s = ft % 2
            for g in range(2):
                b, fr = acquire()
                for j in range(4):
                    tk = tr(ps[:, b, j * P:(j + 1) * P], U2[s][:, (4 * g + j) * P:(4 * g + j + 1) * P], tok, fr,
                            mark=(j == 3))
                te = cp(AE, U3[:, 4 * g:4 * g + 4, ft * P:(ft + 1) * P], v3(ps[:, b, :], 4), tk)
                release(b, te)
            u2_free[s] = tk

        for ft in range(16):
            n = 64 if ft == 13 else 128
            s = ft % 2
            res = feat(a["w_rw"][ft], n, t_h, HT3)
            for h, (b, tk) in enumerate(res):
                te = cp(AE, RAW[s][0:n, 1 + 512 * h:513 + 512 * h], ps[0:n, b, :], tk, raw_free[s])
                release(b, te)
            t1 = act(U1[s][0:n, :], RAW[s][0:n, 1:1025], ACT.Copy, te, tc0, raw_free[s], scale=C0[0:n, ft:ft + 1])
            t2 = stt(U1[s][0:n, :], RAW[s][0:n, 0:1024], pc["mup"][0:n, ft:ft + 1], U1[s][0:n, :], ALU.mult, ALU.add,
                     t1, tz)
            dst = U2[s] if ft < 12 else UL[ft - 12]
            t3 = stt(dst[0:n, :], RAW[s][0:n, 2:1026], pc["mun"][0:n, ft:ft + 1], U1[s][0:n, :], ALU.mult, ALU.add,
                     t2, u2_free[s] if ft < 12 else None)
            raw_free[s] = t3
            if pend:
                fin_shift(*pend.pop())
            if ft < 12:
                pend.append((ft, n, dst, t3))
            elif ft == 12:
                tl = act(dst[64:128, :], dst[64:128, :], ACT.Tanh, t3)
            elif ft == 13:
                tl = act(dst[0:64, :], dst[0:64, :], ACT.Tanh, t3)
            else:
                tl = act(dst, dst, ACT.Sigmoid, t3)
        t_ul = [tl, t3]
        t_u = te
        t_u = last(AE)

        names = ["r", "k2", "v", "kkn", "b", "sgf", "sgb"]
        rw_d = a["rw_d"]
        RN = sm(300, 64)
        RN3 = v3(RN, 8)
        BS = sm(364, 64)
        BS3 = v3(BS, 8)
        CT = sm(428, 128)
        CT3 = v3(CT, 8)
        KT0, KT1 = X[:, 0:512], X[:, 512:1024]
        VE.wait(t_u, t3, last(PE))
        VE.wait(t_b)
        for t in range(NT):
            tq = tt(KT0, U3[:, t, 512:1024], KKB, ALU.mult, last(VE))
            tq = tt(KT0, KT0, KT0, ALU.mult, tq)
            tq = red(RN3[:, t, :], v3(KT0, 8), tq)
        tq = act(RN, RN, ACT.Sqrt, tq)
        tq = ts(RN, RN, 1e-12, None, ALU.max, None, tq)
        tq = recip(RN, RN, tq)
        t_rn = ts(RN, RN, -1.0, None, ALU.mult, None, tq)
        run_gates(2)
        wb = [[X[:, 1024 + 3584 * i + 512 * j:1536 + 3584 * i + 512 * j] for j in range(7)] for i in range(2)]
        s_st = [slot(), slot()]
        st_free = [None, None]
        st_all = {}
        for t in range(NT):
            s = t % 2
            aa, k2, kkn, bb, sgf, sgb, tm = wb[s]
            sl = slice(t * P, (t + 1) * P)
            fre = st_free[s]
            sig = []
            for (row, lh, wt, bias, dst) in ((0, UL[0][0:64, sl], A2W[0:64, :], A0B, aa),
                                             (64, UL[0][64:128, sl], A2W[64:128, :], W0F, sgf),
                                             (0, UL[1][0:64, sl], W2B[0:64, :], W0B, sgb)):
                b, fr = acquire()
                tk = mm(ps[:, b, :], lh, wt, True, True, t_ul, t_b, fr, mark=True)
                te = tt(dst, ps[:, b, :], bias, ALU.add, tk, fre)
                release(b, te)
                sig.append(act(dst, dst, ACT.Sigmoid, te))
            t_a, t_f, t_g = sig
            r_, k_, v_ = U3[:, t, 0:512], U3[:, t, 512:1024], U3[:, t, 1024:1536]
            t1 = tt(kkn, k_, KKB, ALU.mult, fre)
            t1 = tt(v3(kkn, 8), v3(kkn, 8), bl(RN3[:, t, :], 64), ALU.mult, t1, t_rn)
            t1 = stt(bb, kkn, -1.0, aa, ALU.mult, ALU.mult, t1, t_a)
            t2 = stt(tm, aa, -1.0, KAB, ALU.add, ALU.mult, t_a)
            t2 = stt(k2, tm, 1.0, k_, ALU.add, ALU.mult, t2)
            t3 = tt(tm, r_, RKB, ALU.mult, t2)
            t3 = tt(tm, tm, k2, ALU.mult, t3)
            t3 = red(BS3[:, t, :], v3(tm, 8), t3)
            b, fr = acquire()
            for d, (sg, tsg) in enumerate(((sgf, t_f), (sgb, t_g))):
                for p in range(4):
                    tk = mm(ps[:, b, d * 8 + 2 * p:d * 8 + 2 * p + 2], sg[:, p * P:(p + 1) * P], cst["col"], True, True,
                            tsg, fr, mark=(d == 1 and p == 3))
            te = cp(VE, CT3[:, t, :], ps[:, b, 0:16], tk)
            release(b, te)
            ss_ = s_st[s]
            for j, (src, tok) in enumerate(((r_, t_u), (k2, t2), (v_, t_u), (kkn, t1), (bb, t1), (sgf, t_f), (sgb, t_g))):
                tw = ss_.dma(GE, rw_d[t, j], src, tok, fre)
            st_free[s] = [tw, t3, tk]
            st_all[t] = tw
            run_gates(2)
        GG = sm(556, 64)
        G4 = GG.rearrange("p (d i q) -> p d i q", d=2, i=8)
        for d in range(2):
            for i in range(8):
                t = i if d == 0 else 7 - i
                o, r1 = G4[:, d, i, :], CT3[:, t, d * 8:d * 8 + 8].rearrange("p (q c) -> p q c", c=2)
                rest = r1[:, :, 1 - d]
                if i < 7:
                    nx = CT3[:, t + 1 - 2 * d, d * 8:d * 8 + 8].rearrange("p (q c) -> p q c", c=2)[:, :, d]
                    tg = tt(o, rest, nx, ALU.add, te)
                else:
                    tg = cp(VE, o, rest, te)
        t_g = act(GG, GG, ACT.Exp, tg, scale=-EH)

        run_gates(99)
        done = all_done() + list(st_all.values()) + [g.free for g in gst]
        for e in (PE, VE, AE, GE):
            e.wait(done)
        GS = [UL[2], UL[3]]
        spaces = [[AR[:, 0:14336], EX[:, 0:4096]], [X[:, 0:8192], AR[:, 16384:22528], W[:, 0:4096]]]

        def allocator(regions):
            left = [[r, 0] for r in regions]

            def take(n):
                for x in left:
                    if x[0].shape[1] - x[1] >= n:
                        o = x[0][:, x[1]:x[1] + n]
                        x[1] += n
                        return o
                raise RuntimeError("no room")
            return take

        o_d = a["o_d"]
        o_marks = [{}, {}]
        MU, VR = sm(620, 128), sm(748, 128)
        t_vr = {}

        def stream(d):
            take = allocator(spaces[d])
            M4 = take(2048).rearrange("p (h c n) -> p h c n", h=4, c=4)
            ART = take(1024).rearrange("p (q c n) -> p q c n", q=4, c=2)
            BT, KT = v3(take(1024), 8), v3(take(1024), 8)
            E = [take(512) for _ in range(3)]
            Rt, Kt, Bt = E[0], E[1], take(512)
            r_, k2, kkn, bb, sg = [take(512) for _ in range(5)]
            vb = [take(512) for _ in range(2)]
            Z0 = [take(512).rearrange("p (c h n) -> p c h n", c=2, h=4) for _ in range(2)]
            An, Dn, DT = [v3(take(512), 4) for _ in range(3)]
            D2, D2T, D4, D4T, D8 = [v3(take(512), 4) for _ in range(5)]
            Fn, FT, F2, F2T, F4T = D2, D2T, D4, D4T, D8
            XA, XB = [v3(take(512), 4) for _ in range(2)]
            zv = lambda z: z.rearrange("p h n -> p (h n)").rearrange("p (c h n) -> p c h n", c=2, h=4)
            ZA, ZB = zv(Dn), zv(DT)
            QT_, PT_ = v3(take(256), 2), v3(take(256), 2)
            SS = v3(take(512), 4)
            OB = take(512)
            s_ld, s_o = slot(), slot()
            s_v = [slot(), slot()]
            v_free = [None, None]
            TC = cst["TCF"] if d == 0 else cst["TCB"]
            sT, iT, sN = ("SU", "IU", "SL") if d == 0 else ("SL", "IL", "SU")
            at2 = CONST.index(sT) * P
            mask2 = CS[:, at2:at2 + 256]
            dN, dT, oN, oT = ("DL", "DU", "OL", "OU") if d == 0 else ("DU", "DL", "OU", "OL")
            t_s = [memset(GE, SS, 0.0)] * 4
            o_free = e2_free = None
            b4 = lambda n: bc(cst[n], 4)
            for z in (BT, KT):
                memset(GE, z, 0.0)
            t_zero = last(GE)

            def batch(lhs, rhs, *toks):
                b, fr = acquire()
                for h in range(4):
                    tk = mm(ps[:, b, h * P:(h + 1) * P], lhs[:, h, :], rhs[:, h, :], True, True, fr, *toks,
                            mark=(h == 3))
                return b, v3(ps[:, b, :], 4), tk

            def apply(lhs, z, *toks):
                b, fr = acquire()
                pv = ps[:, b, :].rearrange("p (c h n) -> p c h n", c=2, h=4)
                for h in range(4):
                    tk = mm(pv[:, :, h, :], lhs[:, h, :], z[:, :, h, :], True, True, fr, *toks, mark=(h == 3))
                return b, pv, tk

            def load(i, free):
                t = i if d == 0 else 7 - i
                for dst, jj in ((sg, 5 + d), (r_, 0), (k2, 1), (kkn, 3), (bb, 4)):
                    t1 = s_ld.dma(SP, dst, rw_d[t, jj], free)
                return t1, s_v[i % 2].dma(SP, vb[i % 2], rw_d[t, 2], v_free[i % 2])

            for i in range(8):
                t = i if d == 0 else 7 - i
                v_ = vb[i % 2]
                if i == 0:
                    t_ld, t_v = load(0, done)
                b, fr = acquire()
                tk = mm(ps[:, b, :], TC, sg, True, True, t_ld, fr, mark=True)
                te = tt(E[2], ps[:, b, :], sg, ALU.subtract, tk, e2_free)
                t0 = act(E[0], ps[:, b, :], ACT.Exp, te, scale=-EH)
                t1 = act(E[1], ps[:, b, :], ACT.Exp, te, scale=EH)
                t2 = act(E[2], E[2], ACT.Exp, te, scale=-EH)
                release(b, t1)
                yield
                for u in range(2):
                    c = slice(256 * u, 256 * u + 256)
                    t_A = tt(Z0[u][:, 0, :, :], v3(kkn[:, c], 4), v3(E[2][:, c], 4), ALU.mult, t2, t_ld)
                t_B = tt(Bt, bb, E[1], ALU.mult, t1, t_ld, eng=GE)
                pt = [t_A, tt(Rt, r_, E[0], ALU.mult, t0, t_ld), t_B,
                      tt(Kt, k2, E[1], ALU.mult, t_B, eng=GE)]
                tT = []
                az = lambda p: Z0[p // 2][:, 0, 2 * (p % 2):2 * (p % 2) + 2, :].rearrange("p h n -> p (h n)")
                for n, (src, dst) in enumerate(((None, ART[:, :, 0, :]), (Rt, ART[:, :, 1, :]), (Bt, BT), (Kt, KT))):
                    b, fr = acquire()
                    for p in range(4):
                        tk = tr(ps[:, b, p * P:(p + 1) * P], src[:, p * P:(p + 1) * P] if n else az(p), pt[n], fr,
                                mark=(p == 3))
                    if n < 2:
                        te = cp(AE if n else VE, dst, v3(ps[:, b, :], 4), tk)
                    else:
                        eng = AE if n == 3 else VE
                        cp(eng, dst[0:64, 0::2, :], v3(ps[0:64, b, :], 4), tk, t_zero)
                        te = cp(eng, dst[64:128, 1::2, :], v3(ps[64:128, b, :], 4))
                    release(b, te)
                    tT.append(te)
                t_vi = t_v
                if i < 7:
                    t_ld, t_v = load(i + 1, tT + pt)
                yield
                for u in range(2):
                    tM = []
                    for h in range(4):
                        p = 2 * u + h // 2
                        b, fr = acquire()
                        rr = ART[:, p, :, :].rearrange("k c n -> k (c n)")
                        mm(ps[:, b, 0:256], BT[:, 4 * u + h, :], rr, True, True, tT, fr)
                        tk = mm(ps[:, b, 256:512], KT[:, 4 * u + h, :], rr, True, True, mark=True)
                        ta = tt(M4[:, h, :, :].rearrange("p (a c) n -> p a (c n)", a=2), v3(ps[:, b, :], 2),
                                bc(mask2, 2), ALU.mult, tk)
                        release(b, ta)
                        tM.append(ta)
                    b, fr = acquire()
                    for q in range(2):
                        h = 4 * u + 2 * q
                        tk = mm(ps[:, b, 256 * q:256 * q + 256], ART[:, 2 * u + q, 0, :],
                                BT[:, h:h + 2, :].rearrange("p h n -> p (h n)"), True, True, fr, mark=(q == 1))
                    tA = tt(An, v3(ps[:, b, :], 4), b4(sN), ALU.mult, tk)
                    release(b, tA)
                    yield
                    b, fr = acquire()
                    for h in range(4):
                        c = (4 * u + h) * 64
                        tk = mm(ps[:, b, h * 64:(h + 1) * 64], M4[:, h, 2, :], v_[:, c:c + 64], True, True, tM, fr,
                                t_vi, mark=(h == 3))
                    tAV = cp(AE, Z0[u][:, 1, :, :], v3(ps[:, b, 0:256], 4), tk)
                    release(b, tAV)
                    tDT = tt(DT, M4[:, :, 0, :], b4(dT), ALU.mult, tM)
                    tDn = tt(Dn, An, b4(dN), ALU.mult, tA)
                    tX = tt(XA, DT, b4("ident"), ALU.add, tDT, tA, eng=GE)
                    b, pv, tk = batch(DT, Dn, tDT, tDn)
                    t2 = cp(AE, D2, pv, tk)
                    release(b, t2)
                    b, pv, tk = batch(Dn, DT, tDT, tDn)
                    t2T = cp(VE, D2T, pv, tk)
                    release(b, t2T)
                    yield
                    b, pv, tk = batch(D2T, D2, t2, t2T)
                    t4 = cp(AE, D4, pv, tk)
                    release(b, t4)
                    b, pv, tk = batch(D2, D2T, t2, t2T)
                    t4T = cp(AE, D4T, pv, tk)
                    release(b, t4T)
                    b, pv, tk = batch(D2, XA, tX)
                    tX2 = tt(XB, pv, XA, ALU.add, tk)
                    release(b, tX2)
                    yield
                    b, pv, tk = batch(D4T, D4, t4, t4T)
                    t8 = cp(AE, D8, pv, tk)
                    release(b, t8)
                    b, pv, tk = batch(D4, XB, t4, tX2)
                    tX3 = tt(XA, pv, XB, ALU.add, tk)
                    release(b, tX3)
                    yield
                    b, pv, tk = batch(D8, XA, t8, tX3)
                    tX4 = tt(XB, pv, XA, ALU.add, tk)
                    release(b, tX4)
                    yield
                    b, pv, tk = batch(XB, An, tX4, tA)
                    tF = tt(Fn, pv, b4(oN), ALU.mult, tk)
                    release(b, tF)
                    b, pv, tk = batch(An, XB, tX4, tA)
                    tFT = tt(FT, pv, b4(oT), ALU.mult, tk)
                    release(b, tFT)
                    b, pv, tk = apply(XB, Z0[u], tX4, tAV, t_A)
                    tZ = cp(AE, ZA, pv, tk)
                    release(b, tZ)
                    yield
                    b, pv, tk = batch(FT, Fn, tF, tFT)
                    tF2 = cp(AE, F2, pv, tk)
                    release(b, tF2)
                    b, pv, tk = batch(Fn, FT, tF, tFT)
                    tF2T = cp(VE, F2T, pv, tk)
                    release(b, tF2T)
                    b, pv, tk = apply(FT, ZA, tZ)
                    tZ2 = tt(ZB, pv, ZA, ALU.add, tk)
                    release(b, tZ2)
                    yield
                    b, pv, tk = batch(F2, F2T, tF2, tF2T)
                    tF4T = cp(AE, F4T, pv, tk)
                    release(b, tF4T)
                    b, pv, tk = apply(F2T, ZB, tZ2)
                    tZ3 = tt(ZA, pv, ZB, ALU.add, tk)
                    release(b, tZ3)
                    yield
                    b, pv, tk = apply(F4T, ZA, tF4T, tZ3)
                    tZ4 = tt(ZB, pv, ZA, ALU.add, tk)
                    release(b, tZ4)
                    yield
                    b, fr = acquire()
                    for h in range(4):
                        lo = 64 * (h % 2)
                        tk = mm(ps[lo:lo + 64, b, (h // 2) * P:(h // 2 + 1) * P], ZB[:, 0, h, :], M4[:, h, 1, :],
                                True, True, tZ4, fr, mark=(h == 3))
                    tQ = tt(QT_, v3(ps[:, b, 0:256], 2), ART[:, 2 * u:2 * u + 2, 1, :], ALU.add, tk)
                    release(b, tQ)
                    b, fr = acquire()
                    for q in range(2):
                        p = 2 * u + q
                        tk = mm(ps[:, b, q * P:(q + 1) * P], ZB[:, 0, 2 * q:2 * q + 2, :].rearrange("p h n -> p (h n)"), Bt[:, p * P:(p + 1) * P],
                                True, True, fr, mark=(q == 1))
                    tP = tt(PT_, v3(ps[:, b, 0:256], 2), bc(cst["BD"], 2), ALU.mult, tk)
                    release(b, tP)
                    tP = tt(PT_, PT_, bc(ident, 2), ALU.add, tP, eng=GE)
                    yield
                    b, fr = acquire()
                    for q in range(2):
                        p = 2 * u + q
                        mm(ps[:, b, q * P:(q + 1) * P], QT_[:, q, :], SS[:, p, :], True, False, tQ, t_s[p], fr, lax=True)
                        for hh in range(2):
                            h = 2 * q + hh
                            c = (4 * u + h) * 64
                            o = ps[:, b, h * 64:(h + 1) * 64]
                            mm(o, M4[:, h, 1, :], ZB[:, 1, h, :], False, False, lax=True)
                            tk = mm(o, M4[:, h, 3, :], v_[:, c:c + 64], False, hh == 1, lax=True, mark=(h == 3))
                    tO = cp(AE, OB[:, u * 256:(u + 1) * 256], ps[:, b, 0:256], tk, o_free)
                    release(b, tO)
                    b, fr = acquire()
                    for q in range(2):
                        p = 2 * u + q
                        o = ps[:, b, q * P:(q + 1) * P]
                        mm(o, PT_[:, q, :], SS[:, p, :], True, False, tP, fr)
                        mm(o, Bt[:, p * P:(p + 1) * P], ZB[:, 1, 2 * q:2 * q + 2, :], False, False)
                        tk = mm(o, Kt[:, p * P:(p + 1) * P], v_[:, p * P:(p + 1) * P], False, True, mark=(q == 1))
                    for q in range(2):
                        p = 2 * u + q
                        t_s[p] = stt(SS[:, p, :], ps[:, b, q * P:(q + 1) * P], G4[:, d, i, p:p + 1], cst["BD"],
                                     ALU.mult, ALU.mult, tk)
                    release(b, t_s[p])
                    yield
                v_free[i % 2] = last(PE)
                mu, vr = [q[:, d * 64 + t * 8:d * 64 + t * 8 + 8] for q in (MU, VR)]
                o3, e3 = v3(OB, 8), v3(E[2], 8)
                t1 = red(mu, o3, tO)
                t1 = ts(mu, mu, 1.0 / 64, None, ALU.mult, None, t1)
                tO = tt(o3, o3, bl(mu, 64), ALU.subtract, t1)
                t1 = tt(e3, o3, o3, ALU.mult, tO, eng=GE)
                e2_free = t_vr[d, t] = red(vr, e3, t1)
                o_marks[d][t] = s_o.dma(GE, o_d[d, t], OB, tO)
                o_free = [o_marks[d][t], t1]

        LG, LB_ = W1[:, 0:512], W1[:, 512:1024]
        G2 = [W1[:, 1024:1536], W1[:, 1536:2048]]
        GT = [slot(HT[:, 4096 + 512 * i:4608 + 512 * i]) for i in range(4)]
        WO = [slot(HT[:, 6144 + 512 * i:6656 + 512 * i]) for i in range(4)]
        s_of, s_oat = slot(), slot()
        t_ln = []

        def out_a():
            free = [last(PE), last(VE), last(AE)] + t_att
            OAT3 = v3(HT[:, 0:4096], 4)
            t_oat = s_oat.dma(SP, OAT3, oa_d.rearrange("(k p) n -> p k n", p=P), free)
            s_of.dma(SP, LG, a["ln_x_g"].partition_broadcast(P).rearrange("p a n -> p (a n)"))
            s_of.dma(SP, LB_, a["ln_x_b"].partition_broadcast(P).rearrange("p a n -> p (a n)"))
            s_of.dma(SP, G2[0], a["g2"][0:128, :])
            t_ln.append(s_of.dma(SP, G2[1], a["g2"][128:256, :]))
            for x in WO + GT:
                x.free = free

            def load(n):
                r = WO[n % 4]
                return r, r.dma(SP, r.ap, a["w_o"][n][:, 0:512], r.free)

            def gate(i):
                g = GT[i % 4]
                return g, g.dma(SP, g.ap, g_d[i // 2, i % 2], g.free)
            lds, gts = [load(n) for n in range(3)], [gate(i) for i in range(3)]
            yield
            for n in range(8):
                r, tw = lds[n]
                if n + 3 < 8:
                    lds.append(load(n + 3))
                w3 = v3(r.ap, 4)
                for h in range(2):
                    hs = slice(512 * h, 512 * h + 512)
                    g, tg = gts[2 * n + h]
                    if 2 * n + h + 3 < 16:
                        gts.append(gate(2 * n + h + 3))
                    b, fr = acquire()
                    for k in range(4):
                        tk = mm(ps[:, b, :], w3[:, k, :], OAT3[:, k, hs], k == 0, k == 3, tw, t_oat, fr, mark=(k == 3))
                    r.free = tk
                    g.free = te = tt(MIX3[:, n, hs], g.ap, ps[:, b, :], ALU.mult, tk, tg)
                    release(b, te)
                    yield

        oa_pass = out_a()

        def attention_and_loads():
            yield from attention(done)
            next(oa_pass)

        s0, s1, at_ = stream(0), stream(1), attention_and_loads()
        for _ in range(7):
            next(s0)
            next(at_)
        interleave(s0, s1, at_)
        t_oa = t_att

        done = all_done() + [o_marks[0][7], o_marks[1][0]]
        for e in (PE, VE, AE, GE):
            e.wait(done)
        OF = [X[:, 0:4096], X[:, 4096:8192]]
        VV = AR[:, 0:4096]
        t_of = []
        for t in range(NT):
            s_t = slot()
            for d in range(2):
                s_t.dma(SP, OF[d][:, t * 512:(t + 1) * 512], o_d[d, t], done)
            t_of.append([s_t.dma(SP, VV[:, t * 512:(t + 1) * 512], rw_d[t, 2])] + t_ln)
            if t == 3:
                s_w = slot()
                for n in range(8):
                    t_wo = s_w.dma(SP, W[:, 512 * n:512 * n + 512], a["w_o"][n][:, 512:1024])
        SQT = AR[:, 6144:10240]
        tv = ts(VR, VR, 1.0 / 64, GN_EPS, ALU.mult, ALU.add, list(t_vr.values()))
        tv = act(VR, VR, ACT.Sqrt, tv)
        tv = recip(VR, VR, tv)
        OBT = AR[:, 10240:14336]
        OBT3 = v3(OBT, 4)

        class Mix:

            def __getitem__(self, key):
                p, k, n = key
                o = (AR[:, 16384 + 1024 * k:17408 + 1024 * k] if k < 6 else EX[:, 1024 * (k - 6):1024 * (k - 5)])
                return o[p, n]

        MIX3 = Mix()

        def group_norm():
            tb_free = [None, None]
            for t in range(NT):
                bon = SQT[:, 0:512]
                acc = SQT[:, 512 + 512 * (t % 2):1024 + 512 * (t % 2)]
                tb = tt(v3(bon, 8), v3(VV[:, t * 512:(t + 1) * 512], 8), bl(BS3[:, t, :], 64), ALU.mult, last(VE), t_of[t],
                        eng=GE)
                tb = tt(bon, bon, LB_, ALU.add, tb, eng=GE)
                for d in range(2):
                    b, fr = acquire()
                    tk = mm(ps[:, b, :], GS[d][:, t * P:(t + 1) * P], G2[d], True, True, t_of[t], fr, mark=True)
                    ot = OF[d][:, t * 512:(t + 1) * 512]
                    v = VR[:, d * 64 + t * 8:d * 64 + t * 8 + 8]
                    t1 = tt(v3(ot, 8), v3(ot, 8), bl(v, 64), ALU.mult, tv, t_of[t])
                    t1 = tt(ot, ot, LG, ALU.mult, t1)
                    t1 = tt(ot, ot, bon, ALU.add, t1, tb)
                    t1 = tt(acc if d == 0 else ot, ot, ps[:, b, :], ALU.mult, tk, t1, tb_free[t % 2])
                    release(b, t1)
                t1 = tt(acc, acc, OF[1][:, t * 512:(t + 1) * 512], ALU.add, t1)
                yield
                b, fr = acquire()
                for p in range(4):
                    tk = tr(ps[:, b, p * P:(p + 1) * P], acc[:, p * P:(p + 1) * P], t1, fr, mark=(p == 3))
                tb_free[t % 2] = tk
                te = cp(AE, OBT3[:, :, t * P:(t + 1) * P], v3(ps[:, b, :], 4), tk)
                release(b, te)
                if t % 4 == 3:
                    t_ob.append(te)
                yield

        t_ob = []
        TY = [W1[:, 512 * i:512 * i + 512] for i in range(4)]
        room.close()
        HH, HL, WS = [region(ctx, n, w, FR) for n, w in (("HH", 8192), ("HL", 8192), ("WS", 4096))]
        HH3, HL3 = v3(HH, 8), v3(HL, 8)
        room = ExitStack()
        region(room, "pad", 4096)
        ML3 = v3(region(room, "ML", 8192, FR), 8)

        def out_b(h):
            hs = slice(512 * h, 512 * h + 512)

            def load(n):
                g = GT[n % 4]
                return g, g.dma(SP, g.ap, g_d[8 + n, h], g.free)
            lds = [load(n) for n in range(4)]
            for n in range(8):
                g, tg = lds[n]
                b, fr = acquire()
                w3 = v3(W[:, 512 * n:512 * n + 512], 4)
                for k in range(4):
                    tk = mm(ps[:, b, :], w3[:, k, :], OBT3[:, k, hs], k == 0, k == 3, t_wo, t_ob[h], fr, mark=(k == 3))
                ty = TY[n % 4]
                te = tt(ty, g.ap, ps[:, b, :], ALU.mult, tk, tg, mix_tok.get(n - 4))
                release(b, te)
                g.free = te
                te = tt(MIX3[:, n, hs], MIX3[:, n, hs], ty, ALU.add, te)
                t1 = act(HL3[:, n, hs], MIX3[:, n, hs], ACT.Copy, te)
                mix_tok[n] = tt(ML3[:, n, hs], MIX3[:, n, hs], HL3[:, n, hs].bitcast(F32), ALU.subtract, t1)
                if n + 4 < 8:
                    lds.append(load(n + 4))
                yield

        mix_tok, t_mix = {}, []
        for _ in range(2):
            next(oa_pass)
        interleave(oa_pass, group_norm())
        VE.wait(last(VE), last(GE))
        t_xr = [xsl[t].dma(SP, X[:, t * D:(t + 1) * D], a["x"][t * P:(t + 1) * P, :], last(VE), last(AE)) for t in range(NT)]
        for _ in out_b(0):
            pass
        t_mix.append(mix_tok[7])
        for _ in out_b(1):
            pass
        t_mix.append(mix_tok[7])
        for i in range(4):
            ring[i].free = last(PE)
        free = [last(PE), last(VE), last(AE), last(GE), t_oa]
        ready, t_h = start_norm(pc["g_ffn"], free)

        def add_x(t, nh, b, tk):
            xt = X[:, t * D + nh * 512:t * D + nh * 512 + 512]
            te = tt(xt, xt, b, ALU.add, tk, t_xr[t])
            if nh == 1:
                ready[t] = te
            return te


        class Split:

            def __init__(self, WS, free):
                self.WS, self.at, self.free = WS, 0, [free, free]
                self.ahead, self.todo = [], []

            def one(self):
                if not self.todo:
                    return
                src, n = self.todo.pop(0)
                r, tw = load_w(src, n)
                s = self.at % 2
                self.at += 1
                hi, lo = self.WS[:, s * 2048:s * 2048 + n], self.WS[:, s * 2048 + 1024:s * 2048 + 1024 + n]
                t1 = act(hi, r.ap[:, 0:n], ACT.Copy, tw, self.free[s])
                t2 = tt(lo, r.ap[:, 0:n], hi.bitcast(F32), ALU.subtract, t1)
                r.free = t2
                self.ahead.append((s, hi, lo, t2))

            def take(self):
                if not self.ahead:
                    self.one()
                return self.ahead.pop(0)

            def next(self):
                x = self.take()
                self.one()
                return x

        def featr_steps(sp, HH3, HL3, tok_h, res, ncol=P, step=8):
            s, wh, wl, tw = sp.next()
            wh, wl = v3(wh, 8), v3(wl, 8)
            for h in range(2):
                hs = slice(h * 512, h * 512 + 512)
                need(tok_h, h)
                b, fr = acquire()
                o = ps[0:ncol, b, :]
                for k in range(8):
                    mm(o, wh[:, k, :], HL3[:, k, hs], k == 0, False, tw, tok_h[h], fr)
                    mm(o, wl[:, k, :], HH3[:, k, hs], False, False)
                    tk = mm(o, wh[:, k, :], HH3[:, k, hs], False, k == 7, mark=(k == 7))
                    if k == 7:
                        res.append((b, tk))
                    if k % step == step - 1:
                        yield
            sp.free[s] = tk

        def tokmajor3(sp, nk, ncols, AH3, AL3, tok_a, evac):
            for tg in range(2):
                need(tok_a, tg)
                for nh in range(ncols):
                    banks = [acquire() for _ in range(4)]
                    marks = [None] * 4
                    for q in range(nk // 2):
                        s, wh, wl, tw = sp.next()
                        wh, wl = v3(wh, 2), v3(wl, 2)
                        for kk in range(2):
                            k = 2 * q + kk
                            for j in range(4):
                                b, fr = banks[j]
                                o = ps[:, b, :]
                                js = slice((4 * tg + j) * P, (4 * tg + j + 1) * P)
                                lk = k == nk - 1
                                mm(o, AH3[:, k, js], wl[:, kk, :], k == 0, False, tw, tok_a[tg], fr)
                                mm(o, AL3[:, k, js], wh[:, kk, :], False, False)
                                m = mm(o, AH3[:, k, js], wh[:, kk, :], False, lk, mark=(lk or (kk == 1 and j == 3)))
                                if lk:
                                    marks[j] = m
                            bg_step()
                        sp.free[s] = m
                    for j in range(4):
                        release(banks[j][0], evac(tg * 4 + j, nh, ps[:, banks[j][0], :], marks[j]))

        sp = Split(WS, free)
        sp.todo += [(a["w_merge"][nh, q], 1024) for tg in range(2) for nh in range(2) for q in range(4)]

        def ffn_weights(wg, wu, wd):
            for f0, nf in ((0, 12), (12, 10)):
                for f in range(f0, f0 + nf):
                    sp.todo += [(wg[f], 1024), (wu[f], 1024)]
                sp.todo += [(wd[nh, f0 // 2 + q], 1024) for tg in range(2) for nh in range(2) for q in range(nf // 2)]

        ffn_weights(a["w_fg"], a["w_fu"], a["w_fd"])
        sp.todo += [(a["w_tok2"][nh, q], 1024) for tg in range(2) for nh in range(3) for q in range(4)]
        sp.todo.append((a["w_a"].rearrange("p k n -> p (k n)"), 128))
        for j in range(4):
            sp.todo += [(a["w_cv"][x + j], 1024) for x in (4, 8, 0)]
        sp.todo += [(a["w_out"][nh, q], 1024) for tg in range(2) for nh in range(2) for q in range(4)]
        ffn_weights(a["w_fg2"], a["w_fu2"], a["w_fd2"])
        tokmajor3(sp, 8, 2, HL3, ML3, t_mix, add_x)
        room.close()

        def ffn(conv, t_h, then):
            start = [last(PE), last(VE), last(AE), last(GE)]
            room = ExitStack()
            HA = v3(region(room, f"HA{int(conv)}", 12288), 12)
            SA = region(room, f"SA{int(conv)}", 2048, FR)

            def first_pair():
                ws = [sp.take(), sp.take()]
                res = [[], []]
                for h in range(2):
                    need(t_h, h)
                    hs = slice(h * 512, h * 512 + 512)
                    for (s, wh, wl, tw), rs in zip(ws, res):
                        wh, wl = v3(wh, 8), v3(wl, 8)
                        b, fr = acquire()
                        o = ps[:, b, :]
                        for k in range(8):
                            mm(o, wh[:, k, :], HL3[:, k, hs], k == 0, False, tw, t_h[h], fr)
                            mm(o, wl[:, k, :], HH3[:, k, hs], False, False)
                            tk = mm(o, wh[:, k, :], HH3[:, k, hs], False, k == 7, mark=(k == 7))
                            if k % 2:
                                bg_step()
                        rs.append((b, tk))
                        sp.free[s] = tk
                sp.one()
                return res

            def featr():
                res = []
                for _ in featr_steps(sp, HH3, HL3, t_h, res):
                    pass
                return res

            def down(f0, nf, tok_a, ready):
                sa_free = [None, None]
                for tg in range(2):
                    for nh in range(2):
                        banks = [acquire() for _ in range(4)]
                        marks = [None] * 4
                        for q in range(nf // 2):
                            s, wh, wl, tw = sp.take()
                            wh, wl = v3(wh, 2), v3(wl, 2)
                            parts = []
                            for x in range(2):
                                src = HA[:, 2 * q + x, tg * 512:tg * 512 + 512]
                                ah, al = SA[:, x * 1024:x * 1024 + 512], SA[:, x * 1024 + 512:x * 1024 + 1024]
                                t1 = act(ah, src, ACT.Copy, tok_a, sa_free[x])
                                t1 = tt(al, src, ah.bitcast(F32), ALU.subtract, t1)
                                parts.append((ah, al, t1))
                            sp.one()
                            for kk in range(2):
                                k = 2 * q + kk
                                ah, al, t1 = parts[kk]
                                for j in range(4):
                                    b, fr = banks[j]
                                    lk = k == nf - 1
                                    o = ps[:, b, :]
                                    js = slice(j * P, (j + 1) * P)
                                    mm(o, ah[:, js], wl[:, kk, :], k == 0, False, t1, tw, fr)
                                    mm(o, al[:, js], wh[:, kk, :], False, False)
                                    m = mm(o, ah[:, js], wh[:, kk, :], False, lk, mark=(lk or j == 3))
                                    if lk:
                                        marks[j] = m
                                sa_free[kk] = m
                                bg_step()
                            sp.free[s] = m
                        for j in range(4):
                            t = tg * 4 + j
                            xt = X[:, t * D + nh * 512:t * D + nh * 512 + 512]
                            te = tt(xt, xt, ps[:, banks[j][0], :], ALU.add, marks[j])
                            release(banks[j][0], te)
                            if nh == 1 and ready is not None:
                                ready[t] = te

            rawf = [W1[:, 0:1026], W1[:, 1026:2052]]
            fr_raw = [None, None]
            ha_free = None
            for f in range(NF):
                s = f % 2
                gb, ub = (featr(), featr()) if f else first_pair()
                if f == 0:
                    for e in (AE, VE):
                        e.wait(start, last(VE), last(AE), t_h[1])
                    if conv:
                        for x in rawf:
                            memset(VE, x[:, 0:1], 0.0)
                            tz = memset(VE, x[:, 1025:1026], 0.0)
                dst = HA[:, f % 12, :]
                if f == 12:
                    VE.wait(ha_free)
                if conv:
                    for h, (b, tk) in enumerate(gb):
                        te = cp(AE, rawf[s][:, 1 + 512 * h:513 + 512 * h], ps[:, b, :], tk, fr_raw[s])
                        release(b, te)
                    t1 = ts(dst, rawf[s][:, 1:1025], pc["cw1"][:, f:f + 1], pc["cb"][:, f:f + 1], ALU.mult, ALU.add, te)
                    t1 = stt(dst, rawf[s][:, 0:1024], pc["cw0"][:, f:f + 1], dst, ALU.mult, ALU.add, t1)
                    t1 = stt(dst, rawf[s][:, 2:1026], pc["cw2"][:, f:f + 1], dst, ALU.mult, ALU.add, t1)
                    fr_raw[s] = t1
                    sg = act(rawf[s][:, 1:1025], dst, ACT.Sigmoid, t1)
                    t1 = tt(dst, dst, rawf[s][:, 1:1025], ALU.mult, sg)
                    fr_raw[s] = t1
                    for h, (b, tk) in enumerate(ub):
                        te = tt(dst[:, 512 * h:512 * h + 512], dst[:, 512 * h:512 * h + 512], ps[:, b, :], ALU.mult, tk, t1)
                        release(b, te)
                else:
                    for h, (b, tk) in enumerate(gb):
                        hs = slice(512 * h, 512 * h + 512)
                        sg = act(rawf[s][:, hs], ps[:, b, :], ACT.Sigmoid, tk, fr_raw[s])
                        t1 = tt(dst[:, hs], rawf[s][:, hs], ps[:, b, :], ALU.mult, sg)
                        release(b, t1)
                        b2, tk2 = ub[h]
                        te = tt(dst[:, hs], dst[:, hs], ps[:, b2, :], ALU.mult, tk2, t1)
                        release(b2, te)
                    fr_raw[s] = te
                if f == 11:
                    down(0, 12, te, None)
                    ha_free = [last(PE), last(VE), last(AE)]
            down(12, 10, te, then([last(PE), last(VE), last(AE), last(GE)]))
            room.close()

        t_x1 = {}

        def then_norm(free):
            ready, tok = start_norm(pc["g_n1"], free)
            t_x1.update(h=tok, ready=ready)
            return ready

        ffn(True, t_h, then_norm)
        t_h, t_x1 = t_x1["h"], t_x1["ready"]

        room = ExitStack()
        AR = region(room, "AR_b", 14336)
        start = [last(PE), last(VE), last(AE), last(GE)]
        QK, V2, OC, ZL = AR[:, 0:4096], AR[:, 4096:8192], AR[:, 8192:12288], AR[:, 12288:14336]
        QK3, V23, OC3, ZL3 = v3(QK, 8), v3(V2, 8), v3(OC, 4), v3(ZL, 8)
        WAG = OC[:, 0:512]
        PA = OC[:, 512:1536]
        ZT = OC[:, 1536:3584]
        s_g, s_gn = slot(), slot()
        t_wg = s_g.dma(SP, WAG[0:16, 0:256], a["w_gate_up"], start)
        t_wg = s_g.dma(SP, WAG[:, 256:512], a["b_gate_2"].partition_broadcast(P).rearrange("p a n -> p (a n)"))
        s_xd = slot()
        for t in range(NT):
            t_xd = s_xd.dma(GE, a["x_d"][t], X[:, t * D:(t + 1) * D], t_x1[t])
        GP = X[:, 0:4096]
        GP3 = v3(GP, 8)
        xat = [4096]

        def xb(n):
            xat[0] += n
            return X[:, xat[0] - n:xat[0]]
        GN = xb(128)
        x_free, t_gn = [], []
        t_gp = {}

        def ev2(t, nh, b, tk):
            if nh < 2:
                t_gp[t, nh] = cp(AE, (QK3, V23)[nh][:, t, :], b, tk, start)
                return t_gp[t, nh]
            if not x_free:
                need(t_h, 1)
                x_free.extend([t_xd, last(VE), last(AE)])
                t_gn.append(s_gn.dma(SP, GN, a["gla_norm_g_2"].partition_broadcast(P).rearrange("p a n -> p (a n)"),
                                     x_free))
            dst = GP3[:, t, :]
            te = act(dst, b, ACT.Sigmoid, tk, x_free)
            te = tt(dst, dst, b, ALU.mult, te)
            t_gp[t, 2] = tt(v3(dst, 4), v3(dst, 4), bc(GN, 4), ALU.mult, te, t_gn, eng=GE)
            return te
        tokmajor3(sp, 8, 3, HH3, HL3, t_h, ev2)
        res = []
        s, wh, wl, tw = sp.next()
        wh, wl = v3(wh, 8), v3(wl, 8)
        for h in range(2):
            b, fr = acquire()
            hs = slice(512 * h, 512 * h + 512)
            o = ps[0:16, b, :]
            for k in range(8):
                mm(o, wh[:, k, :], HL3[:, k, hs], k == 0, False, tw, t_h[h], fr)
                mm(o, wl[:, k, :], HH3[:, k, hs], False, False)
                tk = mm(o, wh[:, k, :], HH3[:, k, hs], False, k == 7, mark=(k == 7))
            te = cp(VE, PA[0:16, hs], o, tk, start)
            release(b, te)
        sp.free[s] = tk
        t_pa = te
        for t in range(NT):
            b, fr = acquire()
            tk_pa = mm(ps[:, b, 0:256], PA[0:16, t * P:(t + 1) * P], WAG[0:16, 0:256], True, True, t_pa, t_wg, fr,
                       mark=True)
            te = tt(ZL3[:, t, :], ps[:, b, 0:256], WAG[:, 256:512], ALU.add, tk_pa, t_wg)
            release(b, te)
        t1 = stt(ZT, ZL, -1.0, ZL, ALU.mult, ALU.max, te)
        t1 = act(ZT, ZT, ACT.Exp, t1, scale=-1.0)
        t1 = act(ZT, ZT, ACT.Ln, t1, bias=1.0)
        t_la = stt(ZL, ZL, 0.0, ZT, ALU.min, ALU.subtract, t1)

        UC, CC = W1[:, 0:1026], W1[:, 1026:2050]

        def conv_branch():
            uc_free = memset(VE, UC[:, 0:2], 0.0, last(PE), last(AE), last(VE))
            for j in range(4):
                cc, ch, cb = [], [], []
                yield from featr_steps(sp, HH3, HL3, t_h, cc, step=2)
                for h in range(2):
                    te = cp(AE, CC[:, 512 * h:512 * h + 512], ps[:, cc[h][0], :], cc[h][1], uc_free)
                    release(cc[h][0], te)
                yield from featr_steps(sp, HH3, HL3, t_h, ch, step=2)
                for h in range(2):
                    te = tt(UC[:, 2 + 512 * h:514 + 512 * h], CC[:, 512 * h:512 * h + 512], ps[:, ch[h][0], :], ALU.mult,
                            te, ch[h][1], uc_free)
                    release(ch[h][0], te)
                dst = OC3[:, j, :]
                t1 = ts(dst, UC[:, 2:1026], pc["gw2"][:, j:j + 1], None, ALU.mult, None, te, t_la, tk_pa)
                t1 = stt(dst, UC[:, 1:1025], pc["gw1"][:, j:j + 1], dst, ALU.mult, ALU.add, t1)
                t1 = stt(dst, UC[:, 0:1024], pc["gw0"][:, j:j + 1], dst, ALU.mult, ALU.add, t1)
                uc_free = t1
                yield from featr_steps(sp, HH3, HL3, t_h, cb, step=2)
                for h in range(2):
                    hs = slice(512 * h, 512 * h + 512)
                    te = tt(dst[:, hs], dst[:, hs], ps[:, cb[h][0], :], ALU.mult, t1, cb[h][1])
                    release(cb[h][0], te)
            t_br["oc"] = te

        t_br = {}
        Eb, Enb, Er, qi, ki, ks0, ks1 = [xb(256) for _ in range(7)]
        QKT, ST, SG, TS = [xb(512) for _ in range(4)]
        GD = sm(876, 32)
        RS2 = sm(908, 32)

        def gla():
            t_sg = memset(VE, SG, 0.0, x_free)
            AE.wait(x_free)
            QT4, ST3 = v3(QKT, 4), v3(ST, 4)
            e_free = tp_free = s_free = st_free = None
            for t in range(NT):
                la = ZL3[:, t, :]
                b, fr = acquire()
                mm(ps[:, b, 0:256], cst["TRI"], la, True, True, t_la, fr)
                tk = mm(ps[:, b, 256:512], cst["REST"], la, True, True, mark=True)
                t0 = act(Eb, ps[:, b, 0:256], ACT.Exp, tk, e_free, scale=1.0 / 16)
                t1 = act(Enb, ps[:, b, 0:256], ACT.Exp, scale=-1.0 / 16)
                t2 = act(Er, ps[:, b, 256:512], ACT.Exp, scale=1.0 / 16)
                release(b, t2)
                b, fr = acquire()
                for q in range(2):
                    tk = mm(ps[:, b, 2 * q:2 * q + 2], la[:, q * P:(q + 1) * P], cst["col"], True, True, fr,
                            mark=(q == 1))
                gd = GD[:, 4 * t:4 * t + 4]
                t_gd = act(gd, ps[:, b, 0:4], ACT.Exp, tk, scale=1.0 / 16)
                release(b, t_gd)
                qq, kk = QK3[:, t, 0:256], QK3[:, t, 256:512]
                m0 = stt(qi, qq, 0.125, Eb, ALU.mult, ALU.mult, t0, tp_free, t_gp[t, 0])
                m1 = tt(ki, kk, Enb, ALU.mult, t1)
                m2 = stt(ks0, kk, cst["col"][:, 0:1], Er, ALU.mult, ALU.mult, t2, s_free)
                m3 = stt(ks1, kk, cst["col"][:, 1:2], Er, ALU.mult, ALU.mult, t2)
                e_free = m3
                yield
                yield
                b, fr = acquire()
                for q in range(2):
                    tr(ps[:, b, q * P:(q + 1) * P], qi[:, q * P:(q + 1) * P], m0, m1, fr)
                for q in range(2):
                    tk = tr(ps[:, b, (2 + q) * P:(3 + q) * P], ki[:, q * P:(q + 1) * P], mark=(q == 1))
                tp_free = tk
                te = cp(AE, QKT, ps[:, b, :], tk, s_free)
                release(b, te)
                yield
                (b0, f0), (b1, f1) = acquire(), acquire()
                for h in range(4):
                    lo = 64 * (h % 2)
                    b = (b0, b1)[h % 2]
                    tk = mm(ps[:, b, (h // 2) * P:(h // 2 + 1) * P], QT4[lo:lo + 64, 2 + h // 2, :],
                            QT4[lo:lo + 64, h // 2, :], True, True, te, f0, f1, mark=(h == 3))
                for h in range(2):
                    t_st = tt(ST3[:, h::2, :], v3(ps[:, (b0, b1)[h], 0:256], 2), bc(cst["TRI"], 2), ALU.mult, tk,
                              st_free)
                    release((b0, b1)[h], t_st)
                yield
                bo, fr = acquire()
                vt = V23[:, t, :]
                for h in range(4):
                    t_mst = mm(ps[:, bo, h * P:(h + 1) * P], ST3[:, h, :], vt[:, h * P:(h + 1) * P], h == 0, False,
                               t_st, t_gp[t, 1], fr, lax=True, mark=(h == 3))
                for c in range(2):
                    for q in range(2):
                        tk = mm(ps[64 * c:64 * c + 64, bo, q * 256:(q + 1) * 256], QT4[:, q, 64 * c:64 * c + 64],
                                SG[:, q * 256:(q + 1) * 256], False, True, t_sg, lax=True, mark=True)
                    bs, fs = acquire()
                    ksc = (ks0, ks1)[c]
                    for q in range(2):
                        tk2 = mm(ps[:, bs, q * 256:(q + 1) * 256], ksc[:, q * P:(q + 1) * P],
                                 vt[:, q * 256:(q + 1) * 256], True, True, m3, fs, mark=(q == 1))
                    psv = ps[:, bs, :].rearrange("p (q a n) -> p q a n", q=2, a=2)
                    tsv = TS.rearrange("p (q a n) -> p q a n", q=2, a=2)
                    for q in range(2):
                        t1 = tt(tsv[:, q], psv[:, q], bl(cst["BD"][:, 0:128:64], 128), ALU.mult, tk2, t_sg)
                    release(bs, t1)
                    for q in range(2):
                        t_sg = stt(SG[:, q * 256:(q + 1) * 256], SG[:, q * 256:(q + 1) * 256],
                                   gd[:, 2 * q + c:2 * q + c + 1], TS[:, q * 256:(q + 1) * 256], ALU.mult, ALU.add, t1,
                                   tk, t_gd)
                    yield
                    yield
                s_free = [tk, tk2]
                og = QK3[:, t, :]
                te = cp(AE, og, ps[:, bo, :], tk, m3)
                release(bo, te)
                t1 = act(ST, og, ACT.Square, te, t_mst)
                rs = RS2[:, 4 * t:4 * t + 4]
                t1 = red(rs, ST3, t1)
                st_free = t1
                t1 = rstd(rs, 128, EPS, t1)
                t1 = tt(v3(og, 4), v3(og, 4), bl(rs, 128), ALU.mult, t1)
                t_br["og", t] = tt(og, og, GP3[:, t, :], ALU.mult, t1, t_gp[t, 2])
                yield

        interleave(gla(), conv_branch())

        done = [last(PE), last(VE), last(AE), last(GE)]
        x2sl = [slot() for _ in range(NT)]
        t_xr = [x2sl[t].dma(GE, X[:, t * D:(t + 1) * D], a["x_d"][t], done, t_xd) for t in range(NT)]
        t_ab = []
        for h in range(2):
            for t in range(4 * h, 4 * h + 4):
                b, fr = acquire()
                for p in range(4):
                    tk = tr(ps[:, b, p * P:(p + 1) * P], QK3[:, t, p * P:(p + 1) * P], t_br["og", t], fr, mark=(p == 3))
                hi, lo = HH3[:, 0:4, t * P:(t + 1) * P], HL3[:, 0:4, t * P:(t + 1) * P]
                te = act(hi, v3(ps[:, b, :], 4), ACT.Copy, tk, done)
                te = tt(lo, v3(ps[:, b, :], 4), hi.bitcast(F32), ALU.subtract, te, done)
                release(b, te)
            hs = slice(512 * h, 512 * h + 512)
            te = act(HH3[:, 4:8, hs], OC3[:, :, hs], ACT.Copy, t_br["oc"])
            te = tt(HL3[:, 4:8, hs], OC3[:, :, hs], HH3[:, 4:8, hs].bitcast(F32), ALU.subtract, te)
            t_ab.append(te)

        ready, t_h = start_norm(pc["g_n2"], done)

        def add2(t, nh, b, tk):
            xt = X[:, t * D + nh * 512:t * D + nh * 512 + 512]
            te = tt(xt, xt, b, ALU.add, tk, t_xr[t])
            if nh == 1:
                ready[t] = te
            return te
        tokmajor3(sp, 8, 2, HH3, HL3, t_ab, add2)
        room.close()

        t_end = []

        def then_out(free):
            NFB = W1[:, 1024:2048]
            s_f, s_out = slot(), slot()
            t_nf = s_f.dma(SP, NFB, a["norm_f"].partition_broadcast(P).rearrange("p a n -> p (a n)"), free)
            ready = {}

            def run():
                for t in range(NT):
                    while t not in ready:
                        yield
                    xt = X[:, t * D:(t + 1) * D]
                    ss = sm(940 + t, 1)
                    tq = act(W1[:, 0:1024], xt, ACT.Square, ready[t], free,
                             last(AE), accum_out=ss)
                    tq = rstd(ss, D, EPS, tq)
                    yield
                    tq = stt(xt, xt, ss, NFB, ALU.mult, ALU.mult, tq, t_nf)
                    t_end.append(s_out.dma(SP, out[t * P:(t + 1) * P, :], xt, tq))
                    yield

            bg[0] = run()
            return ready

        ffn(False, t_h, then_out)
        while bg[0] is not None:
            bg_step()
        t_o = t_end[-1]
        SP.wait(t_o)
        SP.wait(t_oa)

        block = ctx.enter_context(nc.Block())

        @block.tensor
        def _(e):
            PE.run(e)

        @block.vector
        def _(e):
            VE.run(e)

        @block.scalar
        def _(e):
            AE.run(e)

        @block.gpsimd
        def _(e):
            GE.run(e)

        @block.sync
        def _(e):
            SP.run(e)


def kernel(**inputs):
    import concourse.bacc as _bacc
    from concourse.bass_utils import run_bass_kernel_spmd as _run

    g = {n: np.ascontiguousarray(v) for n, v in inputs.items()}
    asc = np.ascontiguousarray

    def feat(w, n=P):
        return asc(w.reshape(8, P, -1, n).transpose(2, 1, 0, 3).reshape(-1, P, 8 * n))

    def tok(w):
        k, n = w.shape
        return asc(w.reshape(k // 256, 2, P, n // 512, 512).transpose(3, 0, 2, 1, 4).reshape(n // 512, k // 256, P, 1024))

    def cols(v):
        return v.reshape(-1, P).T

    w_in, w2in = g["w_in"][0], g["w_in_2"][0]
    rw = w_in[:, 416:2400]
    zpad = lambda v: np.concatenate([v[..., :1728], v[..., :64], v[..., 1728:]], -1)
    mu = zpad(g["shift_mu"][0])
    order = {
        "g_mix": cols(g["norm_mix_g"][0]), "g_qa": cols(g["q_a_norm_g"][0]), "g_kva": cols(g["kv_a_norm_g"][0]),
        "mup": cols(mu[0]), "mun": cols(mu[1]), "bg": cols(g["b_gate"][0].reshape(-1)),
        "g_ffn": cols(g["norm_ffn_g"][0]), "cw0": cols(g["ffn_conv_w"][0, 0]), "cw1": cols(g["ffn_conv_w"][0, 1]),
        "cw2": cols(g["ffn_conv_w"][0, 2]), "cb": cols(g["ffn_conv_b"][0]), "g_n1": cols(g["norm1_g_2"][0]),
        "g_n2": cols(g["norm2_g_2"][0]), "gw0": cols(g["conv_w_2"][0, 0]), "gw1": cols(g["conv_w_2"][0, 1]),
        "gw2": cols(g["conv_w_2"][0, 2]),
    }
    ins = {
        "x": g["x"][0], "pos": asc(g["positions"].reshape(8, P).T), "cst": const_table(),
        "pcols": asc(np.concatenate([order[n] for n, _ in PCOLS], 1)),
        "w_mla": asc(w_in[:, 0:416].reshape(8, P, 416).transpose(1, 0, 2)),
        "w_rw": feat(zpad(rw)), "w_g": feat(w_in[:, 2400:]), "w_uq": g["w_uq"][0], "w_ukv": g["w_ukv"][0],
        "qn_norm_g": g["qn_norm_g"], "qr_norm_g": g["qr_norm_g"], "kn_norm_g": g["kn_norm_g"],
        "kr_norm_g": g["kr_norm_g"], "k_k": g["k_k"], "k_a": g["k_a"], "r_k": g["r_k"].reshape(1, 512),
        "a0": g["a0"], "w0": g["w0"][0], "a2": g["a2"][0], "w2": g["w2"][0].reshape(128, 512),
        "g2": g["g2"][0].reshape(256, 512), "ln_x_g": g["ln_x_g"], "ln_x_b": g["ln_x_b"],
        "w_o": feat(g["w_o"][0]), "w_merge": tok(g["w_merge"][0]),
        "w_fg": feat(g["w_ffn_gate"][0]), "w_fu": feat(g["w_ffn_up"][0]), "w_fd": tok(g["w_ffn_down"][0]),
        "w_tok2": tok(w2in[:, 0:1536]), "w_a": asc(w2in[:, 1536:1552].reshape(8, P, 16).transpose(1, 0, 2)),
        "w_cv": feat(w2in[:, 1552:]), "w_gate_up": g["w_gate_up_2"][0], "b_gate_2": g["b_gate_2"],
        "gla_norm_g_2": g["gla_norm_g_2"], "w_out": tok(g["w_out_2"][0]),
        "w_fg2": feat(g["w_ffn_gate_2"][0]), "w_fu2": feat(g["w_ffn_up_2"][0]), "w_fd2": tok(g["w_ffn_down_2"][0]),
        "norm_f": g["norm_f_g_2"].reshape(1, 1024),
    }
    nc = _bacc.Bacc("TRN2", target_bir_lowering=False, num_devices=1)
    arrays, a = {}, {}
    for n, v in ins.items():
        v = asc(v)
        arrays[f"in_{n}"] = v
        a[n] = nc.dram_tensor(f"in_{n}", v.shape, mybir.dt.from_np(v.dtype), kind="ExternalInput").ap()
    a["oa_d"] = nc.dram_tensor("oa_d", [512, 1024], F32, kind="Internal").ap()
    a["qk_d"] = nc.dram_tensor("qk_d", [8, 2, 96, 1024], F32, kind="Internal").ap()
    a["v_d"] = nc.dram_tensor("v_d", [8, P, 512], F32, kind="Internal").ap()
    a["x_d"] = nc.dram_tensor("x_d", [8, P, 1024], F32, kind="Internal").ap()
    a["g_d"] = nc.dram_tensor("g_d", [16, 2, P, 512], F32, kind="Internal").ap()
    a["rw_d"] = nc.dram_tensor("rw_d", [8, 7, P, 512], F32, kind="Internal").ap()
    a["o_d"] = nc.dram_tensor("o_d", [2, 8, P, 512], F32, kind="Internal").ap()
    out = nc.dram_tensor("out_0", [1024, 1024], F32, kind="ExternalOutput").ap()
    program(nc, a, out)
    r = _run(nc, [arrays], core_ids=[0])
    return r.results[0]["out_0"].reshape(1, 1024, 1024)
```
